# Optimizing a Trainium2 kernel written in Bass

```python
import math
import jax, jax.numpy as jnp
from jax import lax
import numpy as np
import jax
import jax.numpy as jnp

D_MODEL = 1024
BATCH = 1
SEQ = 256
DEPTH = 2

HEAD_DIM = 64
N_HEADS_SB = 8
N_HEADS_FOX = 8
W_SB = N_HEADS_SB * HEAD_DIM
W_FOX = N_HEADS_FOX * HEAD_DIM
Q_BLOCK = 128
D_FF = 2816
N_EXPERTS = 8
TOP_K = 2
D_FF_EXPERT = 1408
N_DENSE = (DEPTH + 1) // 2
N_MOE = DEPTH // 2
RMS_EPS = 1e-6
PROJ_IN = 3 * W_SB + 3 * W_FOX + N_HEADS_FOX + 2 * D_MODEL


def rmsnorm(x, g):
    x32 = x.astype(jnp.float32)
    y = x32 * lax.rsqrt(jnp.mean(x32 * x32, axis=-1, keepdims=True) + RMS_EPS)
    return (y * g.astype(jnp.float32)).astype(x.dtype)

def split_heads(t, n_heads):
    b, s, _ = t.shape
    return t.reshape(b, s, n_heads, HEAD_DIM).transpose(0, 2, 1, 3)

def merge_heads(t):
    b, h, s, d = t.shape
    return t.transpose(0, 2, 1, 3).reshape(b, s, h * d)

def stick_breaking_attention(q, k, v):
    seq = q.shape[2]
    scale = 1.0 / math.sqrt(HEAD_DIM)
    outs = []
    for i in range(seq // Q_BLOCK):
        t0 = i * Q_BLOCK
        kv_len = t0 + Q_BLOCK
        qb = q[:, :, t0:kv_len]
        kb = k[:, :, :kv_len]
        vb = v[:, :, :kv_len]
        z = jnp.einsum('bhqd,bhkd->bhqk', qb, kb).astype(jnp.float32) * scale
        q_pos = t0 + jnp.arange(Q_BLOCK)[:, None]
        k_pos = jnp.arange(kv_len)[None, :]
        mask = k_pos < q_pos
        log_beta = jax.nn.log_sigmoid(z)
        log_keep = jnp.where(mask, jax.nn.log_sigmoid(-z), 0.0)
        tail = lax.cumsum(log_keep, axis=log_keep.ndim - 1, reverse=True) - log_keep
        w = jnp.where(mask, jnp.exp(log_beta + tail), 0.0)
        outs.append(jnp.einsum('bhqk,bhkd->bhqd', w.astype(vb.dtype), vb))
    return jnp.concatenate(outs, axis=2)

def forgetting_attention(q, k, v, log_f):
    seq = q.shape[2]
    scale = 1.0 / math.sqrt(HEAD_DIM)
    cum_f = lax.cumsum(log_f, axis=log_f.ndim - 1)
    outs = []
    for i in range(seq // Q_BLOCK):
        t0 = i * Q_BLOCK
        kv_len = t0 + Q_BLOCK
        qb = q[:, :, t0:kv_len]
        kb = k[:, :, :kv_len]
        vb = v[:, :, :kv_len]
        z = jnp.einsum('bhqd,bhkd->bhqk', qb, kb).astype(jnp.float32) * scale
        decay = cum_f[:, :, t0:kv_len, None] - cum_f[:, :, None, :kv_len]
        q_pos = t0 + jnp.arange(Q_BLOCK)[:, None]
        k_pos = jnp.arange(kv_len)[None, :]
        logits = jnp.where(k_pos <= q_pos, z + decay, -jnp.inf)
        p = jax.nn.softmax(logits, axis=-1)
        outs.append(jnp.einsum('bhqk,bhkd->bhqd', p.astype(vb.dtype), vb))
    return jnp.concatenate(outs, axis=2)

def swiglu(h, w_gu, w_dn):
    gu = h @ w_gu
    g, u = jnp.split(gu, 2, axis=-1)
    return (jax.nn.silu(g) * u) @ w_dn

def moe_swiglu(h, w_router, w_gu_e, w_dn_e):
    logits = (h @ w_router).astype(jnp.float32)
    top_val, top_idx = lax.top_k(logits, TOP_K)
    top_w = jax.nn.softmax(top_val, axis=-1)
    combine = jnp.sum(jax.nn.one_hot(top_idx, N_EXPERTS, dtype=jnp.float32) * top_w[..., None], axis=-2)
    combine = combine.astype(h.dtype)
    out = jnp.zeros_like(h)
    for e in range(N_EXPERTS):
        out = out + combine[..., e:e + 1] * swiglu(h, w_gu_e[e], w_dn_e[e])
    return out

def first_inputs(seed: int = 0) -> dict:
    key = jax.random.key(seed)
    ks = jax.random.split(key, 16)
    nrm = lambda k, shape, fan_in: jax.random.normal(k, shape, jnp.float32) * fan_in ** -0.5
    return {
        "x": jax.random.normal(ks[0], (BATCH, SEQ, D_MODEL), jnp.float32),
        "g_mix": 1.0 + 0.02 * jax.random.normal(ks[1], (DEPTH, D_MODEL), jnp.float32),
        "w_in": nrm(ks[2], (DEPTH, D_MODEL, PROJ_IN), D_MODEL),
        "b_f": 2.0 + 0.1 * jax.random.normal(ks[3], (DEPTH, N_HEADS_FOX), jnp.float32),
        "b_gate": 0.02 * jax.random.normal(ks[4], (DEPTH, 2 * D_MODEL), jnp.float32),
        "g_q": 1.0 + 0.02 * jax.random.normal(ks[5], (DEPTH, HEAD_DIM), jnp.float32),
        "g_k": 1.0 + 0.02 * jax.random.normal(ks[6], (DEPTH, HEAD_DIM), jnp.float32),
        "w_o_sb": nrm(ks[7], (DEPTH, W_SB, D_MODEL), W_SB),
        "w_o_fox": nrm(ks[8], (DEPTH, W_FOX, D_MODEL), W_FOX),
        "w_out": nrm(ks[9], (DEPTH, D_MODEL, D_MODEL), D_MODEL),
        "g_ffn": 1.0 + 0.02 * jax.random.normal(ks[10], (DEPTH, D_MODEL), jnp.float32),
        "w_gu_dense": nrm(ks[11], (N_DENSE, D_MODEL, 2 * D_FF), D_MODEL),
        "w_dn_dense": nrm(ks[12], (N_DENSE, D_FF, D_MODEL), D_FF),
        "w_router": nrm(ks[13], (N_MOE, D_MODEL, N_EXPERTS), D_MODEL),
        "w_gu_exp": nrm(ks[14], (N_MOE, N_EXPERTS, D_MODEL, 2 * D_FF_EXPERT), D_MODEL),
        "w_dn_exp": nrm(ks[15], (N_MOE, N_EXPERTS, D_FF_EXPERT, D_MODEL), D_FF_EXPERT),
    }

def first_block(x, g_mix, w_in, b_f, b_gate, g_q, g_k, w_o_sb, w_o_fox, w_out,
              g_ffn, w_gu_dense, w_dn_dense, w_router, w_gu_exp, w_dn_exp):
    splits = [int(c) for c in np.cumsum([W_SB, W_SB, W_SB, W_FOX, W_FOX, W_FOX, N_HEADS_FOX])]
    for l in range(DEPTH):
        h = rmsnorm(x, g_mix[l])
        p = h @ w_in[l]
        q_sb, k_sb, v_sb, q_fx, k_fx, v_fx, f_pre, gate_pre = jnp.split(p, splits, axis=-1)

        y_sb = stick_breaking_attention(split_heads(q_sb, N_HEADS_SB),
                                        split_heads(k_sb, N_HEADS_SB),
                                        split_heads(v_sb, N_HEADS_SB))
        y_sb = merge_heads(y_sb) @ w_o_sb[l]

        qf = rmsnorm(split_heads(q_fx, N_HEADS_FOX), g_q[l])
        kf = rmsnorm(split_heads(k_fx, N_HEADS_FOX), g_k[l])
        log_f = jax.nn.log_sigmoid(f_pre.astype(jnp.float32) + b_f[l].astype(jnp.float32))
        y_fx = forgetting_attention(qf, kf, split_heads(v_fx, N_HEADS_FOX), log_f.transpose(0, 2, 1))
        y_fx = merge_heads(y_fx) @ w_o_fox[l]

        g_sb, g_fx = jnp.split(jax.nn.sigmoid(gate_pre + b_gate[l]), 2, axis=-1)
        x = x + (g_sb * y_sb + g_fx * y_fx) @ w_out[l]

        h = rmsnorm(x, g_ffn[l])
        if l % 2 == 0:
            x = x + swiglu(h, w_gu_dense[l // 2], w_dn_dense[l // 2])
        else:
            x = x + moe_swiglu(h, w_router[l // 2], w_gu_exp[l // 2], w_dn_exp[l // 2])
    return x


CTX_LEN = 256
GRID_W = 64
N_BRANCH = 3
BRANCH_W = D_MODEL // 2
ML_HEADS = 4
ML_HEAD_DIM = BRANCH_W // ML_HEADS
ML_CHUNK = 64
GQA_HEADS = BRANCH_W // HEAD_DIM
GQA_KV_HEADS = 2
GQA_GROUP = GQA_HEADS // GQA_KV_HEADS
NA_HEADS = BRANCH_W // HEAD_DIM
NA_WIN_R = 8
NA_WIN_C = 16
ROPE_THETA = 10000.0
FFN_DIM = ((8 * D_MODEL // 3 + 127) // 128) * 128
CONV_K = 3
EPS = 1e-6
IN_SIZES = (BRANCH_W, BRANCH_W, BRANCH_W, BRANCH_W, 4 * ML_HEADS,
            GQA_HEADS * HEAD_DIM, GQA_KV_HEADS * HEAD_DIM, GQA_KV_HEADS * HEAD_DIM,
            NA_HEADS * HEAD_DIM, NA_HEADS * HEAD_DIM, NA_HEADS * HEAD_DIM,
            N_BRANCH * D_MODEL)
IN_SPLITS = tuple(sum(IN_SIZES[:i + 1]) for i in range(len(IN_SIZES) - 1))
D_IN = sum(IN_SIZES)


def rms_norm(x, g):
    xf = x.astype(jnp.float32)
    y = xf * lax.rsqrt(jnp.mean(xf * xf, axis=-1, keepdims=True) + EPS)
    return (y * g.astype(jnp.float32)).astype(x.dtype)

def modulate(h, shift, scale):
    return h * (1 + scale) + shift

def rope_tables(n_tok, dtype):
    half = HEAD_DIM // 2
    t = jnp.arange(n_tok)
    inv = ROPE_THETA ** (-jnp.arange(0, half, 2, dtype=jnp.float32) / half)
    ang_r = (t // GRID_W).astype(jnp.float32)[:, None] * inv
    ang_c = (t % GRID_W).astype(jnp.float32)[:, None] * inv
    ang = jnp.concatenate([ang_r, ang_r, ang_c, ang_c], axis=-1)
    return jnp.cos(ang).astype(dtype), jnp.sin(ang).astype(dtype)

def apply_rope(x, cos, sin):
    x1, x2, x3, x4 = jnp.split(x, 4, axis=-1)
    rot = jnp.concatenate([-x2, x1, -x4, x3], axis=-1)
    return x * cos[:, None, :] + rot * sin[:, None, :]

def split_heads_2(z, n_heads):
    B, T, _ = z.shape
    return z.reshape(B, T, n_heads, HEAD_DIM)

def attend(q, k, v):
    s = jnp.einsum('bqkgd,bskd->bkgqs', q, k).astype(jnp.float32) * (HEAD_DIM ** -0.5)
    p = jax.nn.softmax(s, axis=-1).astype(v.dtype)
    return jnp.einsum('bkgqs,bskd->bqkgd', p, v)

def zero_state(B):
    return (jnp.zeros((B, ML_HEADS, ML_HEAD_DIM, ML_HEAD_DIM), jnp.float32),
            jnp.zeros((B, ML_HEADS, ML_HEAD_DIM), jnp.float32),
            jnp.zeros((B, ML_HEADS), jnp.float32))

def mlstm_scan(q, k, v, ig, lf, state):
    B, H, T, d = q.shape
    nc = T // ML_CHUNK

    def to_chunks(a):
        return jnp.moveaxis(a.reshape((B, H, nc, ML_CHUNK) + a.shape[3:]), 2, 0)

    tril = jnp.tril(jnp.ones((ML_CHUNK, ML_CHUNK), dtype=bool))

    def body(carry, xs):
        C, n, m = carry
        qc, kc, vc, igc, lfc = xs
        b = jnp.cumsum(lfc, axis=-1)
        logd = jnp.where(tril, b[..., :, None] - b[..., None, :] + igc[..., None, :], -jnp.inf)
        m_t = jnp.maximum(b + m[..., None], jnp.max(logd, axis=-1))
        dw = jnp.exp(logd - m_t[..., None])
        inter = jnp.exp(b + m[..., None] - m_t)
        s = jnp.einsum('bhtd,bhsd->bhts', qc, kc) * dw
        num = jnp.einsum('bhts,bhse->bhte', s, vc) + inter[..., None] * jnp.einsum('bhtd,bhde->bhte', qc, C)
        den = jnp.sum(s, axis=-1) + inter * jnp.einsum('bhtd,bhd->bht', qc, n)
        h = num / jnp.maximum(jnp.abs(den), jnp.exp(-m_t))[..., None]
        b_last = b[..., -1]
        log_w = b_last[..., None] - b + igc
        m_new = jnp.maximum(b_last + m, jnp.max(log_w, axis=-1))
        w = jnp.exp(log_w - m_new[..., None])
        decay = jnp.exp(b_last + m - m_new)
        C_new = decay[..., None, None] * C + jnp.einsum('bhs,bhsd,bhse->bhde', w, kc, vc)
        n_new = decay[..., None] * n + jnp.einsum('bhs,bhsd->bhd', w, kc)
        return (C_new, n_new, m_new), h

    final, h = lax.scan(body, state, (to_chunks(q), to_chunks(k), to_chunks(v), to_chunks(ig), to_chunks(lf)))
    h = jnp.moveaxis(h, 0, 2).reshape(B, H, T, d)
    return h, final

def mlstm_branch(zq, zk, zv, zo, zgate, gate_bias, g_out, state_f, state_b):
    B, T, _ = zq.shape

    def heads(z):
        return z.reshape(B, T, ML_HEADS, ML_HEAD_DIM).transpose(0, 2, 1, 3)

    q, k, v = heads(zq), heads(zk) * (ML_HEAD_DIM ** -0.5), heads(zv)
    g = (zgate.astype(jnp.float32) + gate_bias.astype(jnp.float32)).reshape(B, T, 4, ML_HEADS).transpose(2, 0, 3, 1)
    i_f, f_f, i_b, f_b = g[0], g[1], g[2], g[3]
    h_f, st_f = mlstm_scan(q, k, v, i_f, jax.nn.log_sigmoid(f_f), state_f)
    rev = lambda a: jnp.flip(a, axis=2)
    h_b, st_b = mlstm_scan(rev(q), rev(k), rev(v), rev(i_b), jax.nn.log_sigmoid(rev(f_b)), state_b)
    h = (h_f + rev(h_b)).transpose(0, 2, 1, 3)
    h = rms_norm(h, g_out.reshape(ML_HEADS, ML_HEAD_DIM)).reshape(B, T, BRANCH_W)
    y = h * jax.nn.sigmoid(zo.astype(jnp.float32))
    return y.astype(zq.dtype), st_f, st_b

def gqa_qkv(zq, zk, zv, g_q, g_k):
    B, T, _ = zq.shape
    q = rms_norm(zq.reshape(B, T, GQA_HEADS, HEAD_DIM), g_q)
    k = rms_norm(zk.reshape(B, T, GQA_KV_HEADS, HEAD_DIM), g_k)
    v = zv.reshape(B, T, GQA_KV_HEADS, HEAD_DIM)
    return q, k, v

def gqa_latent(q, k, v, kc, vc):
    B, T = q.shape[:2]
    k_all = jnp.concatenate([kc, k], axis=1)
    v_all = jnp.concatenate([vc, v], axis=1)
    qb = q.reshape(B, T // Q_BLOCK, Q_BLOCK, GQA_KV_HEADS, GQA_GROUP, HEAD_DIM)
    out = lax.map(lambda qi: attend(qi, k_all, v_all), jnp.moveaxis(qb, 1, 0))
    return jnp.moveaxis(out, 0, 1).reshape(B, T, BRANCH_W)

def na_latent(q, k, v, kc, vc, rpb):
    B, T, H, d = q.shape
    rows = T // GRID_W
    wr = min(NA_WIN_R, rows)
    wc = NA_WIN_C
    qg = q.reshape(B, rows, GRID_W, H, d)
    kg = k.reshape(B, rows, GRID_W, H, d)
    vg = v.reshape(B, rows, GRID_W, H, d)
    cols = jnp.arange(GRID_W)
    c0 = jnp.clip(cols - wc // 2, 0, GRID_W - wc)
    col_idx = c0[:, None] + jnp.arange(wc)[None, :]
    dc = col_idx - cols[:, None] + (NA_WIN_C - 1)
    scale = d ** -0.5

    def row_block(r):
        r0 = jnp.clip(r - wr // 2, 0, rows - wr)
        k_win = lax.dynamic_slice_in_dim(kg, r0, wr, axis=1)[:, :, col_idx]
        v_win = lax.dynamic_slice_in_dim(vg, r0, wr, axis=1)[:, :, col_idx]
        q_row = lax.dynamic_index_in_dim(qg, r, axis=1, keepdims=False)
        dr = r0 + jnp.arange(wr) - r + (NA_WIN_R - 1)
        bias = rpb[:, dr[None, :, None], dc[:, None, :]]
        s_win = jnp.einsum('bqhd,brqjhd->bhqrj', q_row, k_win).astype(jnp.float32) * scale + bias.astype(jnp.float32)
        s_ctx = jnp.einsum('bqhd,bshd->bhqs', q_row, kc).astype(jnp.float32) * scale
        s = jnp.concatenate([s_win.reshape(B, H, GRID_W, wr * wc), s_ctx], axis=-1)
        p = jax.nn.softmax(s, axis=-1).astype(v.dtype)
        p_win = p[..., :wr * wc].reshape(B, H, GRID_W, wr, wc)
        p_ctx = p[..., wr * wc:]
        o = jnp.einsum('bhqrj,brqjhd->bqhd', p_win, v_win) + jnp.einsum('bhqs,bshd->bqhd', p_ctx, vc)
        return o.reshape(B, GRID_W, H * d)

    out = lax.map(row_block, jnp.arange(rows))
    return jnp.moveaxis(out, 0, 1).reshape(B, T, H * d)

def merge_branches(y_ml, y_ga, y_na, zg, w_branch, w_out):
    B, T, _ = zg.shape
    gates = jax.nn.sigmoid(zg.astype(jnp.float32)).astype(zg.dtype).reshape(B, T, N_BRANCH, D_MODEL)
    ys = jnp.stack([y_ml, y_ga, y_na], axis=2)
    proj = jnp.einsum('btnc,ncd->btnd', ys, w_branch)
    return jnp.sum(gates * proj, axis=2) @ w_out

def conv_ffn(h, w_up, conv_w, conv_b, w_down):
    u = h @ w_up
    up = jnp.pad(u, ((0, 0), (1, 1), (0, 0)))
    u = up[:, :-2] * conv_w[0] + up[:, 1:-1] * conv_w[1] + up[:, 2:] * conv_w[2] + conv_b
    a, g = jnp.split(u, 2, axis=-1)
    return (a * jax.nn.silu(g)) @ w_down

def second_inputs(seed: int = 0) -> dict:
    key = jax.random.key(seed)
    ks = jax.random.split(key, 24)
    f32 = jnp.float32

    def nrm(k, shape, s):
        return jax.random.normal(k, shape, f32) * s

    x = nrm(ks[0], (BATCH, SEQ, D_MODEL), 1.0)
    c = nrm(ks[1], (BATCH, D_MODEL), 1.0)
    ctx = nrm(ks[2], (BATCH, CTX_LEN, D_MODEL), 1.0)
    c_ctx = nrm(ks[3], (D_MODEL,), 1.0)
    w_mod = nrm(ks[4], (DEPTH, D_MODEL, 6 * D_MODEL), 0.5 * D_MODEL ** -0.5)
    b_mod = nrm(ks[5], (DEPTH, 6 * D_MODEL), 0.02)
    g_pre_mix = 1.0 + nrm(ks[6], (DEPTH, D_MODEL), 0.05)
    g_post_mix = 1.0 + nrm(ks[7], (DEPTH, D_MODEL), 0.05)
    g_pre_ffn = 1.0 + nrm(ks[8], (DEPTH, D_MODEL), 0.05)
    g_post_ffn = 1.0 + nrm(ks[9], (DEPTH, D_MODEL), 0.05)
    w_in = nrm(ks[10], (DEPTH, D_MODEL, D_IN), D_MODEL ** -0.5)
    i_bias = nrm(ks[11], (DEPTH, 2, ML_HEADS), 0.1)
    f_bias = jnp.linspace(3.0, 6.0, ML_HEADS, dtype=f32) + nrm(ks[12], (DEPTH, 2, ML_HEADS), 0.1)
    b_ml_gates = jnp.stack([i_bias[:, 0], f_bias[:, 0], i_bias[:, 1], f_bias[:, 1]], axis=1).reshape(DEPTH, 4 * ML_HEADS)
    g_ml_out = 1.0 + nrm(ks[13], (DEPTH, BRANCH_W), 0.05)
    g_q = 1.0 + nrm(ks[14], (DEPTH, HEAD_DIM), 0.05)
    g_k = 1.0 + nrm(ks[15], (DEPTH, HEAD_DIM), 0.05)
    na_rpb = nrm(ks[16], (DEPTH, NA_HEADS, 2 * NA_WIN_R - 1, 2 * NA_WIN_C - 1), 0.1)
    w_branch = nrm(ks[17], (DEPTH, N_BRANCH, BRANCH_W, D_MODEL), BRANCH_W ** -0.5)
    w_out = nrm(ks[18], (DEPTH, D_MODEL, D_MODEL), D_MODEL ** -0.5)
    w_up = nrm(ks[19], (DEPTH, D_MODEL, 2 * FFN_DIM), D_MODEL ** -0.5)
    conv_w = nrm(ks[20], (DEPTH, CONV_K, 2 * FFN_DIM), 0.3) + jnp.array([0.0, 1.0, 0.0], f32)[None, :, None]
    conv_b = nrm(ks[21], (DEPTH, 2 * FFN_DIM), 0.02)
    w_down = nrm(ks[22], (DEPTH, FFN_DIM, D_MODEL), FFN_DIM ** -0.5)
    return {'x': x, 'c': c, 'ctx': ctx, 'c_ctx': c_ctx, 'w_mod': w_mod, 'b_mod': b_mod,
            'g_pre_mix': g_pre_mix, 'g_post_mix': g_post_mix, 'g_pre_ffn': g_pre_ffn, 'g_post_ffn': g_post_ffn,
            'w_in': w_in, 'b_ml_gates': b_ml_gates, 'g_ml_out': g_ml_out, 'g_q': g_q, 'g_k': g_k,
            'na_rpb': na_rpb, 'w_branch': w_branch, 'w_out': w_out, 'w_up': w_up, 'conv_w': conv_w,
            'conv_b': conv_b, 'w_down': w_down}

def second_block(x, c, ctx, c_ctx, w_mod, b_mod, g_pre_mix, g_post_mix, g_pre_ffn, g_post_ffn, w_in, b_ml_gates,
              g_ml_out, g_q, g_k, na_rpb, w_branch, w_out, w_up, conv_w, conv_b, w_down):
    B, T, _ = x.shape
    cos, sin = rope_tables(T, x.dtype)
    xc = ctx
    for l in range(DEPTH):
        last = l == DEPTH - 1
        mod = (jax.nn.silu(c) @ w_mod[l] + b_mod[l])[:, None, :]
        mod_c = jax.nn.silu(c_ctx) @ w_mod[l] + b_mod[l]
        sh1, sc1, ga1, sh2, sc2, ga2 = jnp.split(mod, 6, axis=-1)
        csh1, csc1, cga1, csh2, csc2, cga2 = jnp.split(mod_c, 6, axis=-1)

        h = modulate(rms_norm(x, g_pre_mix[l]), sh1, sc1)
        hc = modulate(rms_norm(xc, g_pre_mix[l]), csh1, csc1)
        (mq, mk, mv, mo, mg, aq, ak, av, nq, nk, nv, zg) = jnp.split(h @ w_in[l], IN_SPLITS, axis=-1)
        (cmq, cmk, cmv, cmo, cmg, caq, cak, cav, cnq, cnk, cnv, czg) = jnp.split(hc @ w_in[l], IN_SPLITS, axis=-1)

        yc_ml, st_f, st_b = mlstm_branch(cmq, cmk, cmv, cmo, cmg, b_ml_gates[l], g_ml_out[l], zero_state(B), zero_state(B))
        y_ml, _, _ = mlstm_branch(mq, mk, mv, mo, mg, b_ml_gates[l], g_ml_out[l], st_f, st_b)

        qc_a, kc_a, vc_a = gqa_qkv(caq, cak, cav, g_q[l], g_k[l])
        q_a, k_a, v_a = gqa_qkv(aq, ak, av, g_q[l], g_k[l])
        y_ga = gqa_latent(apply_rope(q_a, cos, sin), apply_rope(k_a, cos, sin), v_a, kc_a, vc_a)

        kc_n = split_heads_2(cnk, NA_HEADS)
        vc_n = split_heads_2(cnv, NA_HEADS)
        y_na = na_latent(split_heads_2(nq, NA_HEADS), split_heads_2(nk, NA_HEADS), split_heads_2(nv, NA_HEADS), kc_n, vc_n, na_rpb[l])

        o = merge_branches(y_ml, y_ga, y_na, zg, w_branch[l], w_out[l])
        x = x + ga1 * rms_norm(o, g_post_mix[l])
        f = conv_ffn(modulate(rms_norm(x, g_pre_ffn[l]), sh2, sc2), w_up[l], conv_w[l], conv_b[l], w_down[l])
        x = x + ga2 * rms_norm(f, g_post_ffn[l])

        if not last:
            Tc = xc.shape[1]
            yc_ga = attend(qc_a.reshape(B, Tc, GQA_KV_HEADS, GQA_GROUP, HEAD_DIM), kc_a, vc_a).reshape(B, Tc, BRANCH_W)
            yc_na = attend(split_heads_2(cnq, NA_HEADS)[:, :, :, None, :], kc_n, vc_n).reshape(B, Tc, BRANCH_W)
            oc = merge_branches(yc_ml, yc_ga, yc_na, czg, w_branch[l], w_out[l])
            xc = xc + cga1 * rms_norm(oc, g_post_mix[l])
            fc = conv_ffn(modulate(rms_norm(xc, g_pre_ffn[l]), csh2, csc2), w_up[l], conv_w[l], conv_b[l], w_down[l])
            xc = xc + cga2 * rms_norm(fc, g_post_ffn[l])
    return x


def setup_inputs(seed=0):
    out = dict(first_inputs(seed))
    for name, value in second_inputs(seed + 1).items():
        if name != "x":
            out[name + "_2"] = value
    return out


def reference(
    x, g_mix, w_in, b_f, b_gate, g_q, g_k, w_o_sb, w_o_fox, w_out, g_ffn, w_gu_dense,
    w_dn_dense, w_router, w_gu_exp, w_dn_exp, c_2, ctx_2, c_ctx_2, w_mod_2, b_mod_2,
    g_pre_mix_2, g_post_mix_2, g_pre_ffn_2, g_post_ffn_2, w_in_2, b_ml_gates_2, g_ml_out_2,
    g_q_2, g_k_2, na_rpb_2, w_branch_2, w_out_2, w_up_2, conv_w_2, conv_b_2, w_down_2,
):
    x = first_block(
        x, g_mix, w_in, b_f, b_gate, g_q, g_k, w_o_sb, w_o_fox, w_out, g_ffn, w_gu_dense,
        w_dn_dense, w_router, w_gu_exp, w_dn_exp,
    )
    return second_block(
        x, c_2, ctx_2, c_ctx_2, w_mod_2, b_mod_2, g_pre_mix_2, g_post_mix_2, g_pre_ffn_2,
        g_post_ffn_2, w_in_2, b_ml_gates_2, g_ml_out_2, g_q_2, g_k_2, na_rpb_2, w_branch_2,
        w_out_2, w_up_2, conv_w_2, conv_b_2, w_down_2,
    )


_drawn_inputs = setup_inputs


def setup_inputs(seed=0):
    import zlib

    import numpy as np

    out = dict(_drawn_inputs(seed))
    spreads = {}
    factors = {'b_gate': 8.0,
     'g_k': 3.082,
     'g_post_mix_2': 3.444,
     'g_post_ffn_2': 3.688,
     'g_ml_out_2': 4.248,
     'g_q_2': 8.0,
     'g_k_2': 8.0,
     'na_rpb_2': 8.0,
     'conv_b_2': 7.64}
    for name, (base, spread) in spreads.items():
        noise = np.random.default_rng([zlib.crc32(name.encode()), seed]).standard_normal(out[name].shape)
        drawn = base * np.exp(spread * noise) if base else spread * noise
        out[name] = jnp.asarray(drawn.astype(out[name].dtype))
    for name, factor in factors.items():
        out[name] = (out[name] * factor).astype(out[name].dtype)
    return out
```

```python
import concourse.bass as bass
from concourse import mybir
from contextlib import ExitStack
import numpy as np

F32 = mybir.dt.float32
F32R = mybir.dt.float32r
U32 = mybir.dt.uint32
ALU = mybir.AluOpType
ACT = mybir.ActivationFunctionType
AX = mybir.AxisListType

P = 128
D = 1024
T = 256
TT = T // P
DC = D // P
DEPTH = 2
HD = 64
NH = 8
W_HEADS = NH * HD
BC = W_HEADS // P
KV = 2
ML_H, ML_D = 4, 128
D_FF = 2816
FE = 1408
FB = FE // P
N_EXP = 8
NB2 = 3
GRID_W, NA_R, NA_C = 64, 8, 16
ROWS = T // GRID_W
EPS = 1e-6
NEG = -1e30
ROPE_THETA = 10000.0
BOUND = 85.0
NT = 512
UNIT = 1024
RAW, HL = 4, 2
QK_SB, V_SB, QK_FX, V_FX, F_FX, G_1 = 0, 1024, 1536, 2560, 3072, 3080
MQ, MK, MV, MO, MG, AQ, NQ, NK, NV, G_2 = 0, 512, 1024, 1536, 2048, 2064, 2832, 3344, 3856, 4368
MOD_W = 6 * D
BANKS = 8

COL_FIRST = 2 * DC
COL_CONV = 2 * D_FF // P
COL_SECOND = 4 * DC + BC + MOD_W // P + 4 * COL_CONV
COL_C = DEPTH * (COL_FIRST + COL_SECOND)
COLS = COL_C + 2 * DC


def col_first(layer, name):
    return layer * COL_FIRST + {"g_mix": 0, "g_ffn": DC}[name]


def col_second(layer, name):
    at = 0
    for known, n in (("g_pre_mix", DC), ("g_pre_ffn", DC), ("g_post_mix", DC), ("g_post_ffn", DC), ("g_ml_out", BC),
                     ("b_mod", MOD_W // P), ("conv_b", COL_CONV), ("conv_w", 3 * COL_CONV)):
        if known == name:
            return DEPTH * COL_FIRST + layer * COL_SECOND + at
        at += n
    raise KeyError(name)


class Segment:

    def __init__(self, units, iters, mode, at, evac, A=None, B=None, N=None, tiles=None, dst=None, scale=None, bias=None,
                 M=None, tmp=None, route=None, n_branch=None, gates=None, bias_layer=None, vp=None, o=None, cw=None, cb=None):
        self.units, self.iters, self.n = units, iters, len(units)
        assert self.n % HL == 0
        self.results = max(u[0] for u in units) + 1
        self.uses = [len(range(s, self.n, RAW)) for s in range(RAW)]
        self.next = None
        self.mode, self.at, self.evac = mode, at, evac
        self.A, self.B, self.N, self.tiles = A, B, N, tiles
        self.dst, self.scale, self.bias, self.M = dst, scale, bias, M
        self.tmp, self.route, self.o, self.cw, self.cb = tmp, route, o, cw, cb
        self.n_branch, self.gates, self.bias_layer, self.vp = n_branch, gates, bias_layer, vp

    def unit(self, it, j):
        return it * self.n + (self.unit0 + j)

    def result(self, it, q):
        return it * self.results + (self.result0 + q)

    def loaded(self, it, j):
        s = j % RAW
        return it * (16 * self.uses[s]) + 16 * (self.slot0[s] + j // RAW + 1)


class Step:

    def __init__(self, kind, at=None, seg=None, tiles=None, items=None, mode=None, bias=None, tmp=None, arows=None, mcols=None,
                 decay=None, src=None, sq=None, n=None, parts=None, rope=None, kd=None, jobs=None, dst=None, rows=None,
                 logits=None, route=None, l=None, d=None, mh=None, nq=None, o=None, which=None, diag=None):
        self.kind, self.at, self.seg = kind, at, seg
        self.tiles, self.items, self.mode, self.jobs, self.dst = tiles, items, mode, jobs, dst
        self.bias, self.tmp, self.decay, self.arows, self.mcols = bias, tmp, decay, arows, mcols
        self.src, self.sq, self.n, self.parts, self.rope, self.kd = src, sq, n, parts, rope, kd
        self.rows, self.logits, self.route, self.l, self.d = rows, logits, route, l, d
        self.mh, self.nq, self.o, self.which, self.diag = mh, nq, o, which, diag


def build(nc, a, out):
    ctx = ExitStack()
    with ctx:
        def sb(name, shape, dt=F32):
            return ctx.enter_context(nc.sbuf_tensor(name, shape, dt))

        def sem(name):
            return ctx.enter_context(nc.semaphore(name))

        raw = sb("raw", [P, RAW, UNIT])
        w_hi = sb("w_hi", [P, HL, UNIT], F32R)
        w_lo = sb("w_lo", [P, HL, UNIT], F32R)
        x_tm = sb("x_tm", [P, 2 * TT, D])
        h_hi = sb("h_hi", [P, DC, 2 * T], F32R)
        h_lo = sb("h_lo", [P, DC, 2 * T], F32R)
        act_hi = sb("act_hi", [P, FB * 2 * T], F32R)
        act_lo = sb("act_lo", [P, FB * 2 * T], F32R)
        y_hi = act_hi[:, 0:BC * 2 * T].rearrange("p (c t) -> p c t", c=BC)
        y_lo = act_lo[:, 0:BC * 2 * T].rearrange("p (c t) -> p c t", c=BC)
        c_split = sb("c_split", [P, DC, 4], F32R)
        ident = sb("ident", [P, P])
        ones = sb("ones", [P, P])
        row_of = sb("row_of", [NH, NH, P])
        causal = sb("causal", [P, TT, T])
        anti = sb("anti", [P, TT, T])
        strict = sb("strict", [P, TT, T]) 
        window = sb("window", [P, TT, T])
        rope_cos = sb("rope_cos", [P, TT, HD])
        rope_sin = sb("rope_sin", [P, TT, HD])
        pair_sum = sb("pair_sum", [4, 2])
        expert_no = sb("expert_no", [P, N_EXP])
        cols = sb("cols", [P, COLS])
        mod = sb("mod", [P, MOD_W // P, 2])
        mod_gain = sb("mod_gain", [P, 2, DC, 2])
        mod_post = sb("mod_post", [P, 2, DC, 2])
        g_rows = sb("g_rows", [P, 4 * DEPTH, HD])
        gate_bias = sb("gate_bias", [4 * ML_H, 2 * DEPTH])
        bias_rows = sb("bias_rows", [4, DEPTH, NT])
        small = sb("small", [P, 192])
        eps = sb("eps", [P, 1])
        AR = 15360
        arena = sb("arena", [P, AR])
        ps = ctx.enter_context(nc.psum_tensor("ps", [P, BANKS, 512], F32))

        def view(at, *shape):
            n = int(np.prod(shape))
            assert at + n <= AR, (at, n, AR)
            names = "abcd"[:len(shape)]
            if len(shape) == 1:
                return arena[:, at:at + n]
            return arena[:, at:at + n].rearrange(f"p ({' '.join(names)}) -> p {' '.join(names)}",
                                                 **dict(zip(names, shape)))

        merged = view(0, 2 * TT, D)
        FREE = 2 * TT * D
        XN = view(FREE, 2 * TT, D)
        prob = view(FREE, 2, 512)
        prob_t = view(FREE + 1024, 2, 512)
        WORK = FREE + 2048
        turn_value = view(AR - 1024, 2, 512)

        raw_loaded = [sem(f"raw_loaded_{i}") for i in range(RAW)]
        hi_ready = sem("hi_ready")
        lo_ready = sem("lo_ready")
        hi_used = sem("hi_used")
        units_used = sem("units_used")
        results_saved = sem("results_saved")
        params_loaded = sem("params_loaded")
        at_barrier = sem("at_barrier")
        sums_done = sem("sums_done")
        root_done = sem("root_done")
        turned = sem("turned")
        value_ready = sem("value_ready")
        split_hi_done = sem("split_hi_done")
        split_done = sem("split_done")
        scores_done = sem("scores_done")
        max_done = sem("max_done")
        bounded = sem("bounded")
        exp_done = sem("exp_done")
        probs_done = sem("probs_done")
        pt_done = sem("pt_done")
        pt_saved = sem("pt_saved")
        pv_done = sem("pv_done")
        ml_saved = sem("ml_saved")
        y_hi_done = sem("y_hi_done")
        y_saved = sem("y_saved")
        taps_ready = sem("taps_ready")
        gate_ready = sem("gate_ready")
        act_value = sem("act_value")
        act_hi_done = sem("act_hi_done")
        act_done = sem("act_done")
        stage_pe = sem("stage_pe")
        stage_act = sem("stage_act")
        stage_dve = sem("stage_dve")
        bias_loaded = sem("bias_loaded")
        bias_ready = sem("bias_ready")
        constants_set = sem("constants_set")
        act_step = sem("act_step")
        dve_step = sem("dve_step")
        stored = sem("stored")

        START = {"unit": RAW, "result": 2, "turn": 4, "item": 2, "pair": 2, "ml": 2}
        STARTS = [(hi_ready, RAW), (lo_ready, RAW), (hi_used, RAW), (units_used, RAW), (results_saved, 2), (turned, 4), (value_ready, 4),
                  (split_hi_done, 4), (split_done, 4), (scores_done, 2), (exp_done, 2), (probs_done, 2), (pt_done, 2),
                  (pt_saved, 2), (pv_done, 2), (y_hi_done, 2), (y_saved, 2), (ml_saved, 2)]

        plan, segments = [], []
        count = {"barrier": 0, "sum": 0, "root": 0, "gate": 0, "tap": 0, "act": 0, "value": 0,
                 "pe": 0, "a": 0, "d": 0, "max": 0, "bounded": 0, "bias": 0, **START}
        slot_count = [0] * RAW

        def add(kind, **kw):
            plan.append(Step(kind, dict(count), **kw))

        def took(**kw):
            for name, n in kw.items():
                count[name] += n

        def add_segment(mode, units, iters=1, **kw):
            s = Segment(units, iters, mode=mode, at=dict(count), **kw)
            s.unit0, s.result0, s.slot0 = count["unit"], count["result"], list(slot_count)
            took(unit=s.n * iters, result=s.results * iters)
            for i in range(RAW):
                slot_count[i] += s.uses[i] * iters
            if segments:
                segments[-1].next = s
            segments.append(s)
            plan.append(Step("segment", seg=s))

        def meet():
            add("barrier")
            took(barrier=1)

        def tm_units(w, c0, q=0, chunks=DC, width=NT):
            n = UNIT // width
            return [(q, k, min(n, chunks - k), k == 0, k + n >= chunks, width,
                     lambda it, k=k: w[k * P:min(k + n, chunks) * P, c0:c0 + width].rearrange("(c p) n -> p c n", p=P))
                    for k in range(0, chunks, n)]

        def fm_units(w, c0, q=0, width=2 * P):
            n = UNIT // (2 * P)
            return [(q, k, n, k == 0, k + n == DC, width,
                     lambda it, k=k: w[k * P:(k + n) * P, c0:c0 + width].rearrange("(c p) n -> p c n", p=P))
                    for k in range(0, DC, n)]

        def ffn_units(w_up, w_down, dense):
            def up(it, half, b):
                if dense:
                    f0 = half * D_FF + it * FE + b * P
                    return w_up[:, f0:f0 + P].rearrange("(c p) n -> p c n", p=P)
                f0 = half * FE + b * P
                return w_up[bass.ds(it, 1), :, f0:f0 + P].rearrange("e (c p) n -> p (e c) n", p=P)

            def down(it, k, m, half):
                if dense:
                    return w_down[it * FE + k * P:it * FE + (k + m) * P, half * NT:(half + 1) * NT]\
                        .rearrange("(c p) n -> p c n", p=P)
                return w_down[bass.ds(it, 1), k * P:(k + m) * P, half * NT:(half + 1) * NT]\
                    .rearrange("e (c p) n -> p (e c) n", p=P)

            units = [(b, 0, DC, half == 0, half == 1, P, lambda it, half=half, b=b: up(it, half, b))
                     for b in range(FB) for half in range(2)]
            for half in range(2):
                for k in range(0, FB, 2):
                    m = min(2, FB - k)
                    units.append((FB + half, k, m, k == 0, k + m == FB, NT,
                                  lambda it, k=k, m=m, half=half: down(it, k, m, half)))
            return units

        def norm(tiles):
            add("norm", tiles=tiles)
            took(root=1)
            meet()

        def turn(items):
            add("turn", items=items)
            took(turn=len(items))
            meet()

        def turn_tokens(src, tiles, gain, shift):
            turn([([src[:, t, (4 * h + c) * P:(4 * h + c + 1) * P] for c in range(4)],
                   gain(t)[:, 4 * h:4 * h + 4] if gain else None, shift(t)[:, 4 * h:4 * h + 4] if shift else None,
                   h_hi[:, 4 * h:4 * h + 4, t * P:(t + 1) * P], h_lo[:, 4 * h:4 * h + 4, t * P:(t + 1) * P])
                  for t in range(tiles) for h in range(2)])

        def attend(kind, items, bias=None, tmp=None, arows=None, mcols=None, decay=None):
            add("attend", mode=kind, items=items, bias=bias, tmp=tmp, arows=arows, mcols=mcols, decay=decay)
            took(item=len(items))
            if kind == "mlstm":
                took(ml=len(items))
            else:
                took(pair=len(items) // 2, max=len(items) if kind == "soft" else 0, bounded=len(items) if kind == "stick" else 0)
            meet()

        def head_norm(**kw):
            add("head_norm", **kw)
            took(sum=1, root=1)
            meet()

        def turn_heads(jobs):
            add("turn_heads", jobs=jobs)
            took(pe=len(jobs), a=len(jobs))
            meet()

        def zero_v(dst):
            add("zero_v", dst=dst)
            meet()

        def merge(n, w, g0, w_b, tiles, bias_layer):
            units = []
            for dt in range(2):
                units += tm_units(w, g0 + dt * NT, 2 * dt)
                units += tm_units(w_b, dt * NT, 2 * dt + 1, BC)
            add_segment("tm", units, A=(h_hi, h_lo), B=(y_hi, y_lo), tiles=tiles, evac="merge", n_branch=n,
                        gates=view(WORK, 2 * TT, NT), bias_layer=bias_layer)
            meet()

        def mixed_out(w, tiles, **kw):
            turn_tokens(merged, tiles, None, None)
            add_segment("tm", tm_units(w, 0, 0) + tm_units(w, NT, 1), A=(h_hi, h_lo), tiles=tiles, **kw)
            meet()

        def first_layer(l):
            w = a["w_in"][l]
            qk = view(WORK, 2 * BC, T)
            vp = view(WORK + 2048, TT, NH, P)
            tmp = view(WORK + 4096, 8, T)
            pre = view(WORK + 4096, TT, 2 * W_HEADS)
            sq = view(WORK + 6144, TT, 2 * W_HEADS)
            rows = view(TT * D, 4, 2 * T)
            H = (h_hi, h_lo)
            norm(TT)
            add("zero_v", dst=vp)
            turn_tokens(XN, TT, lambda t: cols[:, col_first(l, "g_mix"):][:, 0:DC], None)
            add_segment("fm", sum((fm_units(w, QK_SB + q * 2 * P, q) for q in range(4)), []), A=H, N=T, evac="fm", dst=qk,
                        scale=[HD ** -0.5] * 2 + [1.0] * 2)
            add_segment("tm", tm_units(w, V_SB), A=H, tiles=TT, evac="v_heads", dst=vp)
            meet()

            def heads(hh, pr, t):
                return dict(q=qk[hh * HD:(hh + 1) * HD, pr, t * P:(t + 1) * P],
                            k=qk[hh * HD:(hh + 1) * HD, BC + pr, 0:(t + 1) * P], nk=(t + 1) * P, add=[],
                            v=[vp[:, s, 2 * pr + hh, :] for s in range(t + 1)], hh=hh, y=(pr, t))

            order = [(hh, pr, t) for pr in range(BC) for t in range(TT) for hh in range(2)]
            attend("stick", [dict(heads(*o), cap=strict[:, o[2], 0:(o[2] + 1) * P]) for o in order], tmp=tmp)
            merge(0, w, G_1, a["w_o_sb"][l], TT, l)
            zero_v(vp)
            add_segment("tm", tm_units(w, QK_FX, 0) + tm_units(w, QK_FX + NT, 1), A=H, tiles=TT, evac="tm", dst=pre)
            add_segment("tm", tm_units(w, V_FX), A=H, tiles=TT, evac="v_heads", dst=vp)
            add_segment("fm", fm_units(w, F_FX, 0, NH), A=H, N=T, evac="rows", dst=rows[0:NH, 0, 0:T],
                        bias=gate_bias[0:NH, l:l + 1], M=NH)
            meet()
            add("fox_rows", rows=rows)
            took(a=1)
            head_norm(src=pre, sq=sq, tiles=TT, n=2 * NH, parts=[(0, NH, 2 * l, HD ** -0.5), (NH, 2 * NH, 2 * l + 1, 1.0)],
                      rope=False)
            turn_heads([([pre[:, t, (part * BC + c) * P:(part * BC + c + 1) * P] for c in range(BC)],
                         qk[:, part * BC:(part + 1) * BC, t * P:(t + 1) * P]) for t in range(TT) for part in range(2)])
            attend("soft", [dict(heads(hh, pr, t),
                                 add=[(row_of[:, 2 * pr + hh, :], rows[0:NH, 3, 0:(t + 1) * P], None),
                                      (ident[:, :], causal[:, t, 0:(t + 1) * P], None)]) for hh, pr, t in order])
            merge(1, w, G_1 + D, a["w_o_fox"][l], TT, l)
            mixed_out(a["w_out"][l], TT, evac="residual")
            norm(TT)
            turn_tokens(XN, TT, lambda t: cols[:, col_first(l, "g_ffn"):][:, 0:DC], None)
            gu = view(0, 4, 2 * T)
            route = None
            if l % 2:
                logits = view(2048, 2, 512)[0:N_EXP, 0, 0:T]
                route = view(3072, TT, 64)
                add_segment("fm", fm_units(a["w_router"][l // 2], 0, 0, N_EXP), A=H, N=T, evac="rows", dst=logits, bias=None,
                            M=N_EXP)
                meet()
                add("route", logits=logits, route=route)
                took(pe=1, d=1, a=1)
                meet()
            n = N_EXP if l % 2 else D_FF // FE
            w_up, w_down = (a["w_gu_exp"], a["w_dn_exp"]) if l % 2 else (a["w_gu_dense"], a["w_dn_dense"])
            add_segment("ffn", ffn_units(w_up[l // 2], w_down[l // 2], l % 2 == 0), n, A=H, N=T, tiles=TT, evac="swiglu",
                        tmp=gu, route=route)
            took(act=FB * n, tap=FB * n)
            meet()

        def second_layer(l):
            w = a["w_in_2"][l]
            nq = TT if l == DEPTH - 1 else 2 * TT
            nn = 2 * TT
            H = (h_hi, h_lo)
            rows4 = view(0, MOD_W)
            units = []
            for q in range(2):
                for k in range(0, DC, 2):
                    units.append((q, k, 2, k == 0, k + 2 == DC, NT, lambda it, q=q, k=k:
                                  a["w_mod_2"][l][k * P:(k + 2) * P, bass.ds(it * (2 * NT) + q * NT, NT)]
                                  .rearrange("(c p) n -> p c n", p=P)))
            add_segment("mod", units, MOD_W // (2 * NT), evac="mod", dst=rows4)
            meet()
            add("mod_cols", rows=rows4, l=l)
            took(pe=1)
            meet()
            norm(nn)
            turn_tokens(XN, nn, lambda t: mod_gain[:, 0, :, t // TT], lambda t: mod[:, 0:DC, t // TT])

            def span(t):
                return 0 if t < TT else T

            mqk = view(WORK, 2 * ML_H, 2 * T)
            mv = view(WORK + 4096, nn, W_HEADS)
            arows = view(WORK + 6144, 2, 2 * T)
            rows = view(WORK + 7168, 2, 2 * T)
            drows = view(FREE, 4, 2 * T)
            mcols = small[:, 128:192].rearrange("p (t k h) -> p t k h", t=nn, k=4)
            add_segment("fm", sum((fm_units(w, MQ + q * 2 * P, q) for q in range(4)), []), A=H, N=2 * T, evac="fm", dst=mqk,
                        scale=[1.0] * 2 + [ML_D ** -0.5] * 2)
            add_segment("tm", tm_units(w, MV), A=H, tiles=nn, evac="tm", dst=mv)
            add_segment("fm", fm_units(w, MG, 0, 4 * ML_H), A=H, N=2 * T, evac="rows", dst=rows[0:4 * ML_H, 0, :],
                        bias=gate_bias[0:4 * ML_H, DEPTH + l:DEPTH + l + 1], M=4 * ML_H)
            meet()
            add("ml_rows", rows=rows, d=drows, arows=arows, mcols=mcols)
            took(a=2, d=2, pe=2)
            meet()
            attend("mlstm", [dict(q=mqk[:, h, t * P:(t + 1) * P], k=mqk[:, ML_H + h, span(t):2 * T], nk=2 * T - span(t),
                                  k0=span(t), t=t, h=h, masks=(causal[:, t % TT, :], anti[:, t % TT, :]),
                                  v=[mv[:, s, h * ML_D:(h + 1) * ML_D] for s in range(span(t) // P, nn)],
                                  dst=mqk[:, h, t * P:(t + 1) * P])
                             for t in range(nq) for h in range(ML_H)], arows=arows, mcols=mcols,
                   decay=view(WORK + 7168, 2, 512))
            mh = mqk[:, 0:ML_H, 0:nq * P].rearrange("p h (t e) -> p h t e", e=P)
            add("ml_norm", mh=mh, sq=view(WORK + 4096, ML_H, nq, P), nq=nq)
            took(sum=1, root=1)
            meet()
            add_segment("tm", tm_units(w, MO), A=H, tiles=nq, evac="ml_gate", gates=view(WORK + 4096, 2 * TT, NT),
                        dst=mqk[:, 0:ML_H, 0:nq * P].rearrange("p h (t e) -> p t h e", e=P))
            took(gate=1)
            meet()
            g = cols[:, col_second(l, "g_ml_out"):][:, 0:BC]
            turn([([mqk[:, c, t * P:(t + 1) * P] for c in range(BC)], g, None, y_hi[:, :, t * P:(t + 1) * P],
                   y_lo[:, :, t * P:(t + 1) * P]) for t in range(nq)])
            merge(0, w, G_2, a["w_branch_2"][l, 0], nq, None)
            QKW = (NH + KV) * HD
            pre = view(WORK, nn, QKW)
            sq = view(WORK + nn * QKW, nn, QKW)
            kd = view(WORK + nn * QKW, nn, KV, 2, HD)
            qT = view(WORK + nn * QKW + 1024, BC, 2 * T)
            kT = view(WORK + nn * QKW + 3072, KV, 2 * T)
            vp = view(WORK + nn * QKW + 4096, nn, 2, KV, P)
            zero_v(vp.rearrange("p a b c d -> p (a b c d)"))
            add_segment("tm", tm_units(w, AQ), A=H, tiles=nn, evac="tm", dst=pre)
            add_segment("tm", tm_units(w, AQ + W_HEADS, 0, DC, 2 * KV * HD), A=H, tiles=nn, evac="gqa_kv", dst=pre, vp=vp)
            meet()
            head_norm(src=pre, sq=sq, tiles=nn, n=NH + KV, rope=True, kd=kd,
                      parts=[(0, NH, 2 * DEPTH + 2 * l, HD ** -0.5), (NH, NH + KV, 2 * DEPTH + 2 * l + 1, 1.0)])
            turn_heads([j for t in range(nn) for j in
                        (([pre[:, t, c * P:(c + 1) * P] for c in range(BC)], qT[:, :, t * P:(t + 1) * P]),
                         ([kd[:, t, g, :, :].rearrange("p a d -> p (a d)") for g in range(KV)], kT[:, :, t * P:(t + 1) * P]))])

            def gqa(hh, pr, t):
                g = 2 * pr // (NH // KV)
                return dict(q=qT[hh * HD:(hh + 1) * HD, pr, t * P:(t + 1) * P], k=kT[hh * HD:(hh + 1) * HD, g, span(t):2 * T],
                            nk=2 * T - span(t), add=[], v=[vp[:, s, hh, g, :] for s in range(span(t) // P, nn)], hh=hh, y=(pr, t))

            order = [(hh, pr, t) for pr in range(BC) for t in range(nq) for hh in range(2)]
            attend("soft", [gqa(*o) for o in order])
            merge(1, w, G_2 + D, a["w_branch_2"][l, 1], nq, None)
            nqk = view(WORK, 2 * BC, 2 * T)
            nvp = view(WORK + 4096, nn, NH, P)
            nbias = view(WORK + 8192, 2, TT, T)
            zero_v(nvp.rearrange("p a b c -> p (a b c)"))
            add_segment("fm", sum((fm_units(w, NQ + q * 2 * P, q) for q in range(4)), []), A=H, N=2 * T, evac="fm", dst=nqk,
                        scale=[HD ** -0.5] * 2 + [1.0] * 2)
            add_segment("tm", tm_units(w, NV), A=H, tiles=nn, evac="v_heads", dst=nvp)
            meet()

            def na(hh, pr, t):
                h = 2 * pr + hh
                return dict(q=nqk[hh * HD:(hh + 1) * HD, pr, t * P:(t + 1) * P],
                            k=nqk[hh * HD:(hh + 1) * HD, BC + pr, span(t):2 * T], nk=2 * T - span(t),
                            add=[(ident[:, :], nbias[:, hh, t, :], count["bias"] + h + 1)] if t < TT else [],
                            v=[nvp[:, s, h, :] for s in range(span(t) // P, nn)], hh=hh, y=(pr, t))

            attend("soft", [na(*o) for o in order], bias=(nbias, l, 2 * nq))
            took(bias=NH)
            merge(2, w, G_2 + 2 * D, a["w_branch_2"][l, 2], nq, None)
            o = view(FREE, 2 * TT, D)
            diag = view(FREE + 4096, 2, DC, P)
            mixed_out(a["w_out_2"][l], nq, evac="tm", dst=o)

            def post(which):
                add("post", o=o, nq=nq, which=which, diag=diag)
                took(root=1, d=1, pe=1)
                meet()

            post(0)
            norm(nq)
            turn_tokens(XN, nq, lambda t: mod_gain[:, 1, :, t // TT], lambda t: mod[:, 3 * DC:4 * DC, t // TT])
            add_segment("ffn", ffn_units(a["w_up_2"][l], a["w_down_2"][l], True), D_FF // FE, A=H, N=nq * P, tiles=nq,
                        evac="conv", tmp=view(FREE + 4096, 4, 2 * T), o=o, cw=col_second(l, "conv_w"),
                        cb=col_second(l, "conv_b"), route=None)
            n = FB * (D_FF // FE)
            took(act=n, tap=2 * n, gate=n, value=n)
            meet()
            post(1)

        for l in range(DEPTH):
            first_layer(l)
        for l in range(DEPTH):
            second_layer(l)

        params = [(x_tm[:, 0:TT, :], a["x"][0].rearrange("(t p) d -> p t d", p=P)),
                  (x_tm[:, TT:2 * TT, :], a["ctx_2"][0].rearrange("(t p) d -> p t d", p=P)),
                  (cols[:, :], a["cols"]), (ident[:, :], a["ident"]), (row_of[:, :, :], a["row_of"]),
                  (causal[:, :, :], a["causal"]), (anti[:, :, :], a["anti"]), (strict[:, :, :], a["strict"]),
                  (window[:, :, :], a["window"]), (rope_cos[:, :, :], a["rope_cos"]), (rope_sin[:, :, :], a["rope_sin"]),
                  (pair_sum[:, :], a["pair_sum"]), (gate_bias[:, :], a["gate_bias"]), (bias_rows[:, :, :], a["bias_rows"]),
                  (expert_no[:, :], a["expert_no"].partition_broadcast(P)), (g_rows[:, :, :], a["g_rows"].partition_broadcast(P))]
        PARAMS = 16 * len(params)

        block = ctx.enter_context(nc.Block())

        @block.sync
        def _(sp):
            def load(seg, it, j):
                q, k, m, opens, closes, width, source = seg.units[j]
                sp.wait_ge(lo_ready, seg.unit(it, j) - (2 if j < 2 else RAW) + 1)
                dst = raw[:, j % RAW, 0:m * width].rearrange("p (c n) -> p c n", c=m)
                sp.dma_start(dst, source(it)).then_inc(raw_loaded[j % RAW], 16)

            for seg in segments:
                if seg.iters > 2:
                    with sp.Fori(0, seg.iters) as it:
                        for j in range(seg.n):
                            load(seg, it, j)
                else:
                    for it in range(seg.iters):
                        for j in range(seg.n):
                            load(seg, it, j)
            sp.wait_ge(at_barrier, 4 * count["barrier"])
            sp.dma_start(out[0].rearrange("(t p) d -> p t d", p=P), x_tm[:, 0:TT, :]).then_inc(stored, 16)
            sp.wait_ge(stored, 16)

        @block.gpsimd
        def _(pool):
            for s, n in STARTS:
                pool.sem_inc(s, n)
            nc.gpsimd.memset(ones[:, :], 1.0)
            nc.gpsimd.memset(eps[:, :], EPS).then_inc(constants_set, 1)
            pool.wait_ge(params_loaded, PARAMS)

            for st in plan:
                if st.kind == "barrier":
                    pool.drain().then_inc(at_barrier, 1)
                    pool.wait_ge(at_barrier, 4 * (st.at["barrier"] + 1))
                elif st.kind == "zero_v":
                    nc.gpsimd.memset(st.dst, 0.0)
                elif st.kind == "attend" and st.bias is not None:
                    nbias, l, per_pair = st.bias
                    for pr in range(BC):
                        if pr:
                            pool.wait_ge(scores_done, st.at["item"] + pr * per_pair)
                        pool.dma_start(nbias.rearrange("p h t k -> p (h t) k"),
                                       a["position_bias"][l, 2 * pr:2 * pr + 2].rearrange("h (t p) k -> p (h t) k", p=P))\
                            .then_inc(bias_loaded, 16)
                        pool.wait_ge(bias_loaded, 16 * (st.at["bias"] // 2 + pr + 1))
                        for hh in range(2):
                            nc.gpsimd.tensor_tensor(nbias[:, hh, :, :], nbias[:, hh, :, :], window[:, :, :], ALU.add)\
                                .then_inc(bias_ready, 1)

        @block.scalar
        def _(act):
            steps = [0]

            def settled(ins):
                steps[0] += 1
                ins.then_inc(act_step, 1)
                act.wait_ge(act_step, steps[0])

            for dst, src in params:
                act.dma_start(dst, src).then_inc(params_loaded, 16)
            act.wait_ge(params_loaded, PARAMS)
            act.wait_ge(constants_set, 1)
            silu_c = small[:, 104:104 + 2 * DC].rearrange("p (c s) -> p c s", s=2)
            settled(nc.scalar.activation(silu_c, cols[:, COL_C:COL_C + 2 * DC].rearrange("p (c s) -> p c s", s=2), ACT.Silu))
            nc.scalar.activation(c_split[:, :, 0:2], silu_c, ACT.Copy).then_inc(split_hi_done, 1)

            def split(seg, it, j):
                q, k, m, opens, closes, width, source = seg.units[j]
                n = m * width
                act.wait_ge(raw_loaded[j % RAW], seg.loaded(it, j))
                act.wait_ge(hi_used, seg.unit(it, j) - HL + 1)
                act.wait_ge(lo_ready, seg.unit(it, j) - HL + 1)
                nc.scalar.activation(w_hi[:, j % HL, 0:n], raw[:, j % RAW, 0:n], ACT.Copy).then_inc(hi_ready, 1)

            def save(seg, it, j):
                q, k, m, opens, closes, width, source = seg.units[j]
                if not closes or seg.evac == "residual":
                    return
                r = seg.result(it, q)
                b = 4 * (q % 2)
                if seg.mode == "ffn" and q >= FB:
                    return
                if seg.evac == "merge" and q % 2:
                    return
                act.wait_ge(units_used, seg.unit(it, j) + 1)
                if seg.evac == "fm":
                    nc.scalar.activation(seg.dst[:, 2 * q:2 * q + 2, 0:seg.N], ps[:, b:b + 2, 0:seg.N], ACT.Copy,
                                         scale=seg.scale[q]).then_inc(results_saved, 1)
                elif seg.evac == "tm":
                    nc.scalar.activation(seg.dst[:, 0:seg.tiles, q * NT:(q + 1) * NT], ps[:, b:b + seg.tiles, :], ACT.Copy)\
                        .then_inc(results_saved, 1)
                elif seg.evac == "v_heads":
                    for hh in range(2):
                        dst = seg.dst[:, 0:seg.tiles, :, :].rearrange("p t (c g) e -> p t c (g e)", g=2)
                        src = ps[:, b:b + seg.tiles, :].rearrange("p t (c g e) -> p t c (g e)", g=2, e=HD)
                        ins = nc.scalar.activation(dst[:, :, :, hh * (P + HD):hh * (P + HD) + HD],
                                                   src[:, :, :, hh * HD:(hh + 1) * HD], ACT.Copy)
                    ins.then_inc(results_saved, 1)
                elif seg.evac == "gqa_kv":
                    n = KV * HD
                    nc.scalar.activation(seg.dst[:, :, W_HEADS:W_HEADS + n], ps[:, b:b + seg.tiles, 0:n], ACT.Copy)
                    for side in range(2):
                        ins = nc.scalar.activation(seg.vp[:, :, side, :, side * HD:(side + 1) * HD],
                                                   ps[:, b:b + seg.tiles, n:2 * n].rearrange("p t (g e) -> p t g e", e=HD),
                                                   ACT.Copy)
                    ins.then_inc(results_saved, 1)
                elif seg.evac == "rows":
                    if seg.bias is None:
                        ins = nc.scalar.activation(seg.dst, ps[0:seg.M, b, 0:seg.N], ACT.Copy)
                    else:
                        ins = nc.scalar.activation(seg.dst, ps[0:seg.M, b, 0:seg.N], ACT.Identity, bias=seg.bias)
                    ins.then_inc(results_saved, 1)
                elif seg.evac == "mod":
                    nc.scalar.activation(seg.dst[0:4, bass.ds(it * (2 * NT) + q * NT, NT)], ps[0:4, b, :], ACT.Copy)\
                        .then_inc(results_saved, 1)
                elif seg.evac == "merge":
                    act.wait_ge(results_saved, r)
                    nc.scalar.activation(seg.gates[:, 0:seg.tiles, :], ps[:, b:b + seg.tiles, :], ACT.Sigmoid)\
                        .then_inc(results_saved, 1)
                elif seg.evac == "ml_gate":
                    nc.scalar.activation(seg.gates[:, 0:seg.tiles, :], ps[:, b:b + seg.tiles, :], ACT.Sigmoid)\
                        .then_inc(gate_ready, 1)
                elif seg.evac == "swiglu":
                    done = it * FB + (seg.at["act"] + q)
                    nc.scalar.activation(seg.tmp[:, q % 2, 0:seg.N], ps[:, b, 0:seg.N], ACT.Silu).then_inc(taps_ready, 1)
                elif seg.evac == "conv":
                    for part in range(2):
                        c = it * FB + q + part * (COL_CONV // 2)
                        nc.scalar.activation(seg.tmp[:, 2 * (q % 2) + part, 0:seg.N], ps[:, b + part, 0:seg.N], ACT.Identity,
                                             scale=cols[:, seg.cw + COL_CONV + c:seg.cw + COL_CONV + c + 1],
                                             bias=cols[:, seg.cb + c:seg.cb + c + 1]).then_inc(taps_ready, 1)

            def save_late(seg, it, j):
                q, k, m, opens, closes, width, source = seg.units[j]
                if not closes or seg.mode != "ffn" or q >= FB:
                    return
                r = seg.result(it, q)
                if seg.evac == "swiglu":
                    act.wait_ge(results_saved, r + 1)
                    nc.scalar.activation(act_hi[:, q * seg.N:(q + 1) * seg.N], seg.tmp[:, 2 + q % 2, 0:seg.N], ACT.Copy)\
                        .then_inc(act_hi_done, 1)
                elif seg.evac == "conv":
                    act.wait_ge(results_saved, r + 1)
                    g = seg.tmp[:, 2 * (q % 2) + 1, 0:seg.N]
                    nc.scalar.activation(g, g, ACT.Silu).then_inc(gate_ready, 1)
                    act.wait_ge(act_value, it * FB + q + seg.at["value"] + 1)
                    nc.scalar.activation(act_hi[:, q * seg.N:(q + 1) * seg.N], seg.tmp[:, 2 * (q % 2), 0:seg.N], ACT.Copy)\
                        .then_inc(act_hi_done, 1)

            def stream(seg):
                def body(it, before, first):
                    for j in range(seg.n):
                        if not (first and j == 0):
                            split(seg, it, j)
                        if j:
                            save(seg, it, j - 1)
                        elif not first:
                            save(seg, before, seg.n - 1)
                        if j > 1:
                            save_late(seg, it, j - 2)

                body(0, None, True)
                if seg.iters > 2:
                    with act.Fori(1, seg.iters) as it:
                        body(it, it - 1, False)
                elif seg.iters == 2:
                    body(1, 0, False)
                if seg.next:
                    split(seg.next, 0, 0)
                save(seg, seg.iters - 1, seg.n - 1)

            def root(n, width):
                nc.scalar.activation(small[:, 64:64 + n], small[:, 0:n], ACT.Sqrt, scale=1.0 / width, bias=eps[:, :])\
                    .then_inc(root_done, 1)

            def attend(st):
                k0 = st.at["item"]
                n = len(st.items)

                def weights(i):
                    e, i0 = st.items[i], k0 + i
                    nk = e["nk"]
                    z = ps[:, i0 % 2, 0:nk]
                    if st.mode == "soft":
                        act.wait_ge(max_done, st.at["max"] + i + 1)
                        act.wait_ge(pt_done, i0 - 1)
                        nc.scalar.activation(prob[:, i0 % 2, 0:nk], z, ACT.Exp, bias=small[:, i0 % 2:i0 % 2 + 1],
                                             accum_out=small[:, 2 + i0 % 2:3 + i0 % 2]).then_inc(exp_done, 1)
                    elif st.mode == "stick":
                        e_, e1 = st.tmp[:, 2 + i0 % 2, 0:nk], st.tmp[:, 4 + i0 % 2, 0:nk]
                        act.wait_ge(bounded, st.at["bounded"] + i + 1)
                        act.wait_ge(probs_done, i0 - 1)
                        settled(nc.scalar.activation(e_, st.tmp[:, i0 % 2, 0:nk], ACT.Exp, scale=-1.0))
                        nc.scalar.activation(e1, e_, ACT.Identity, bias=ones[:, 0:1]).then_inc(exp_done, 1)
                    else:
                        act.wait_ge(scores_done, i0 + 1)
                        act.wait_ge(probs_done, i0)
                        for d in range(2):
                            ins = nc.scalar.activation(st.decay[:, d, 0:nk], ps[:, 4 + 2 * (i0 % 2) + d, 0:nk], ACT.Exp,
                                                       bias=st.mcols[:, e["t"], 2 + d, e["h"]:e["h"] + 1])
                        ins.then_inc(exp_done, 1)

                def turned_weights(i):
                    e, i0 = st.items[i], k0 + i
                    act.wait_ge(pt_done, i0 + 1)
                    act.wait_ge(pv_done, i0 - 1)
                    nc.scalar.activation(prob_t[:, i0 % 2, 0:e["nk"]], ps[:, 2 + i0 % 2, 0:e["nk"]], ACT.Copy)\
                        .then_inc(pt_saved, 1)

                def output(i):
                    e, i0 = st.items[i], k0 + i
                    if st.mode == "mlstm":
                        act.wait_ge(pv_done, i0 + 1)
                        nc.scalar.activation(e["dst"], ps[:, 4 + 2 * (i0 % 2), 0:P], ACT.Copy).then_inc(ml_saved, 1)
                    elif e["hh"]:
                        pr, t = e["y"]
                        act.wait_ge(pv_done, i0 + 1)
                        nc.scalar.activation(y_hi[:, pr, t * P:(t + 1) * P], ps[:, 4 + (st.at["pair"] + i // 2) % 2, 0:P],
                                             ACT.Copy).then_inc(y_hi_done, 1)

                if st.mode == "mlstm":
                    for i in range(n + 2):
                        if i >= 2:
                            output(i - 2)
                        if i < n:
                            weights(i)
                        if 1 <= i <= n:
                            turned_weights(i - 1)
                else:
                    for i in range(n + 3):
                        if i < n:
                            weights(i)
                        if 2 <= i <= n + 1:
                            turned_weights(i - 2)
                        if i >= 3:
                            output(i - 3)

            first = True
            for st in plan:
                if st.kind == "segment":
                    if first:
                        split(st.seg, 0, 0)
                        first = False
                    stream(st.seg)
                elif st.kind == "barrier":
                    act.drain().then_inc(at_barrier, 1)
                    act.wait_ge(at_barrier, 4 * (st.at["barrier"] + 1))
                elif st.kind == "norm":
                    for t in range(st.tiles):
                        ins = nc.scalar.activation(XN[:, t, :], x_tm[:, t, :], ACT.Square, accum_out=small[:, t:t + 1])
                    settled(ins)
                    root(st.tiles, D)
                elif st.kind == "post":
                    for t in range(st.nq):
                        ins = nc.scalar.activation(merged[:, t, :], st.o[:, t, :], ACT.Square, accum_out=small[:, t:t + 1])
                    settled(ins)
                    root(st.nq, D)
                elif st.kind == "head_norm":
                    act.wait_ge(sums_done, st.at["sum"] + 1)
                    root(st.tiles * st.n, HD)
                elif st.kind == "ml_norm":
                    act.wait_ge(sums_done, st.at["sum"] + 1)
                    root(st.nq * ML_H, ML_D)
                elif st.kind == "turn":
                    for i, (src, gain, shift, hi, lo) in enumerate(st.items):
                        i0 = st.at["turn"] + i
                        act.wait_ge(value_ready, i0 + 1)
                        nc.scalar.activation(hi, turn_value[:, i0 % 2, :].rearrange("p (c t) -> p c t", t=P), ACT.Copy)\
                            .then_inc(split_hi_done, 1)
                elif st.kind == "turn_heads":
                    for i, (src, dst) in enumerate(st.jobs):
                        act.wait_ge(stage_pe, st.at["pe"] + i + 1)
                        nc.scalar.activation(dst, ps[:, i % 4, 0:len(src) * P].rearrange("p (c t) -> p c t", t=P), ACT.Copy)\
                            .then_inc(stage_act, 1)
                elif st.kind == "attend":
                    attend(st)
                elif st.kind == "fox_rows":
                    u, e, sp_ = (st.rows[0:NH, i, 0:T] for i in range(3))
                    settled(nc.scalar.activation(e, u, ACT.Abs))
                    settled(nc.scalar.activation(e, e, ACT.Exp, scale=-1.0))
                    nc.scalar.activation(sp_, e, ACT.Ln, bias=1.0).then_inc(stage_act, 1)
                elif st.kind == "ml_rows":
                    n = 4 * ML_H
                    u, e = st.rows[0:n, 0, :], st.arows[0:n, 0, :]
                    settled(nc.scalar.activation(e, u, ACT.Abs))
                    settled(nc.scalar.activation(e, e, ACT.Exp, scale=-1.0))
                    nc.scalar.activation(e, e, ACT.Ln, bias=1.0).then_inc(stage_act, 1)
                    act.wait_ge(stage_pe, st.at["pe"] + 2)
                    m = ps[:, 4, 0:64].rearrange("p (t k h) -> p t k h", t=2 * TT, k=4)
                    nc.scalar.activation(st.mcols[:, :, 0:2, :], m[:, :, 0:2, :], ACT.Exp, scale=-1.0)
                    nc.scalar.activation(st.mcols[:, :, 2:4, :], m[:, :, 2:4, :], ACT.Copy, scale=-1.0).then_inc(stage_act, 1)
                elif st.kind == "route":
                    act.wait_ge(stage_dve, st.at["d"] + 1)
                    nc.scalar.activation(st.route[:, :, 49:50], st.route[:, :, 48:49], ACT.Exp).then_inc(stage_act, 1)

        @block.vector
        def _(dve):
            steps = [0]

            def settled(ins):
                steps[0] += 1
                ins.then_inc(dve_step, 1)
                dve.wait_ge(dve_step, steps[0])

            dve.wait_ge(params_loaded, PARAMS)
            dve.wait_ge(constants_set, 1)
            dve.wait_ge(split_hi_done, START["turn"] + 1)
            silu_c = small[:, 104:104 + 2 * DC].rearrange("p (c s) -> p c s", s=2)
            settled(nc.vector.tensor_tensor(c_split[:, :, 2:4], silu_c, c_split[:, :, 0:2].bitcast(F32), ALU.subtract))

            def split(seg, it, j):
                q, k, m, opens, closes, width, source = seg.units[j]
                n = m * width
                dve.wait_ge(hi_ready, seg.unit(it, j) + 1)
                dve.wait_ge(units_used, seg.unit(it, j) - HL + 1)
                nc.vector.tensor_tensor(w_lo[:, j % HL, 0:n], raw[:, j % RAW, 0:n], w_hi[:, j % HL, 0:n].bitcast(F32),
                                        ALU.subtract).then_inc(lo_ready, 1)

            def save(seg, it, j):
                q, k, m, opens, closes, width, source = seg.units[j]
                if not closes or seg.evac in ("fm", "tm", "v_heads", "gqa_kv", "rows", "mod"):
                    return
                r = seg.result(it, q)
                b = 4 * (q % 2)
                if seg.evac == "residual":
                    dve.wait_ge(units_used, seg.unit(it, j) + 1)
                    x = x_tm[:, 0:seg.tiles, q * NT:(q + 1) * NT]
                    nc.vector.tensor_tensor(x, ps[:, b:b + seg.tiles, :], x, ALU.add).then_inc(results_saved, 1)
                elif seg.evac == "merge":
                    if q % 2 == 0:
                        return
                    dve.wait_ge(results_saved, r)
                    dve.wait_ge(units_used, seg.unit(it, j) + 1)
                    dst = merged[:, 0:seg.tiles, (q // 2) * NT:(q // 2 + 1) * NT]
                    g = seg.gates[:, 0:seg.tiles, :]
                    if seg.n_branch == 0:
                        nc.vector.tensor_tensor(dst, ps[:, b:b + seg.tiles, :], g, ALU.mult).then_inc(results_saved, 1)
                    else:
                        settled(nc.vector.tensor_tensor(g, ps[:, b:b + seg.tiles, :], g, ALU.mult))
                        nc.vector.tensor_tensor(dst, dst, g, ALU.add).then_inc(results_saved, 1)
                elif seg.evac == "ml_gate":
                    dve.wait_ge(gate_ready, seg.at["gate"] + 1)
                    nc.vector.tensor_tensor(seg.dst, seg.dst, seg.gates[:, 0:seg.tiles, :]
                                            .rearrange("p t (h e) -> p t h e", e=ML_D), ALU.mult).then_inc(results_saved, 1)
                elif q >= FB:
                    dve.wait_ge(units_used, seg.unit(it, j) + 1)
                    half = slice((q - FB) * NT, (q - FB + 1) * NT)
                    src = ps[:, b:b + seg.tiles, :]
                    if seg.evac == "conv":
                        dst = seg.o[:, 0:seg.tiles, half]
                        ins = nc.vector.tensor_copy(dst, src) if it == 0 else nc.vector.tensor_tensor(dst, src, dst, ALU.add)
                    elif seg.route is None:
                        dst = x_tm[:, 0:seg.tiles, half]
                        ins = nc.vector.tensor_tensor(dst, src, dst, ALU.add)
                    else:
                        for t in range(seg.tiles):
                            dst = x_tm[:, t, half]
                            ins = nc.vector.scalar_tensor_tensor(dst, ps[:, b + t, :], seg.route[:, t, bass.ds(it, 1)], dst,
                                                                 ALU.mult, ALU.add)
                    ins.then_inc(results_saved, 1)
                elif seg.evac == "swiglu":
                    v = seg.tmp[:, 2 + q % 2, 0:seg.N]
                    dve.wait_ge(taps_ready, it * FB + (seg.at["tap"] + q + 1))
                    nc.vector.tensor_tensor(v, ps[:, b + 1, 0:seg.N], seg.tmp[:, q % 2, 0:seg.N], ALU.mult)\
                        .then_inc(results_saved, 1)
                else:
                    for part in range(2):
                        c = it * FB + q + part * (COL_CONV // 2)
                        dve.wait_ge(taps_ready, 2 * (it * FB + q) + seg.at["tap"] + part + 1)
                        src = ps[:, b + part, 0:seg.N].rearrange("p (s t) -> p s t", t=T)
                        u = seg.tmp[:, 2 * (q % 2) + part, 0:seg.N].rearrange("p (s t) -> p s t", t=T)
                        settled(nc.vector.scalar_tensor_tensor(u[:, :, 1:T], src[:, :, 0:T - 1],
                                                               cols[:, seg.cw + c:seg.cw + c + 1], u[:, :, 1:T],
                                                               ALU.mult, ALU.add))
                        ins = nc.vector.scalar_tensor_tensor(u[:, :, 0:T - 1], src[:, :, 1:T],
                                                             cols[:, seg.cw + 2 * COL_CONV + c:seg.cw + 2 * COL_CONV + c + 1],
                                                             u[:, :, 0:T - 1], ALU.mult, ALU.add)
                    ins.then_inc(results_saved, 1)

            def save_late(seg, it, j):
                q, k, m, opens, closes, width, source = seg.units[j]
                if not closes or seg.mode != "ffn" or q >= FB:
                    return
                n = it * FB + (seg.at["act"] + q)
                if seg.evac == "swiglu":
                    v = seg.tmp[:, 2 + q % 2, 0:seg.N]
                    dve.wait_ge(act_hi_done, n + 1)
                    nc.vector.tensor_tensor(act_lo[:, q * seg.N:(q + 1) * seg.N], v,
                                            act_hi[:, q * seg.N:(q + 1) * seg.N].bitcast(F32), ALU.subtract)\
                        .then_inc(act_done, 1)
                else:
                    dve.wait_ge(gate_ready, it * FB + q + seg.at["gate"] + 1)
                    v, g = seg.tmp[:, 2 * (q % 2), 0:seg.N], seg.tmp[:, 2 * (q % 2) + 1, 0:seg.N]
                    nc.vector.tensor_tensor(v, v, g, ALU.mult).then_inc(act_value, 1)
                    dve.wait_ge(act_hi_done, n + 1)
                    nc.vector.tensor_tensor(act_lo[:, q * seg.N:(q + 1) * seg.N], v,
                                            act_hi[:, q * seg.N:(q + 1) * seg.N].bitcast(F32), ALU.subtract)\
                        .then_inc(act_done, 1)

            def stream(seg):
                def body(it, before, first):
                    for j in range(seg.n):
                        if not (first and j == 0):
                            split(seg, it, j)
                        if j:
                            save(seg, it, j - 1)
                        elif not first:
                            save(seg, before, seg.n - 1)
                        if j > 1:
                            save_late(seg, it, j - 2)

                body(0, None, True)
                if seg.iters > 2:
                    with dve.Fori(1, seg.iters) as it:
                        body(it, it - 1, False)
                elif seg.iters == 2:
                    body(1, 0, False)
                if seg.next:
                    split(seg.next, 0, 0)
                save(seg, seg.iters - 1, seg.n - 1)

            def attend(st):
                k0 = st.at["item"]
                n = len(st.items)

                def begin(i):
                    e, i0 = st.items[i], k0 + i
                    nk = e["nk"]
                    z = ps[:, i0 % 2, 0:nk]
                    if st.mode == "soft":
                        dve.wait_ge(scores_done, i0 + 1)
                        dve.wait_ge(exp_done, i0 - 1)
                        nc.vector.tensor_reduce(small[:, i0 % 2:i0 % 2 + 1], z, AX.X, ALU.max, negate=True).then_inc(max_done, 1)
                    elif st.mode == "stick":
                        dve.wait_ge(scores_done, i0 + 1)
                        dve.wait_ge(exp_done, i0 - 1)
                        nc.vector.scalar_tensor_tensor(st.tmp[:, i0 % 2, 0:nk], z, -BOUND, e["cap"], ALU.max, ALU.min)\
                            .then_inc(bounded, 1)

                def finish(i):
                    e, i0 = st.items[i], k0 + i
                    nk = e["nk"]
                    w = prob[:, i0 % 2, 0:nk]
                    dve.wait_ge(exp_done, i0 + 1)
                    if st.mode == "soft":
                        inv = small[:, 4 + i0 % 2:5 + i0 % 2]
                        settled(nc.vector.reciprocal(inv, small[:, 2 + i0 % 2:3 + i0 % 2]))
                        nc.vector.tensor_scalar(w, w, inv, None, ALU.mult).then_inc(probs_done, 1)
                    elif st.mode == "stick":
                        keep, beta = st.tmp[:, 2 + i0 % 2, 0:nk], st.tmp[:, 4 + i0 % 2, 0:nk]
                        tail = st.tmp[:, 6:8, :].rearrange("p a b -> p (a b)")[:, T - nk:T + 1]
                        settled(nc.vector.reciprocal(beta, beta))
                        settled(nc.vector.tensor_tensor(keep, keep, beta, ALU.mult))
                        settled(nc.vector.tensor_tensor_scan(tail[:, 0:nk][:, ::-1], keep[:, ::-1],
                                                             ones[:, 0:1].to_broadcast([P, nk]), 1.0, ALU.mult, ALU.mult))
                        dve.wait_ge(pt_done, i0 - 1)
                        nc.vector.tensor_tensor(w, beta, tail[:, 1:nk + 1], ALU.mult).then_inc(probs_done, 1)
                    else:
                        z = ps[:, i0 % 2, 0:nk]
                        den, inv = small[:, 0:2], small[:, 4:6]
                        for d in range(2):
                            s = st.decay[:, d, 0:nk]
                            settled(nc.vector.scalar_tensor_tensor(s, z, 1.0, s, ALU.mult, ALU.mult, accum_out=den[:, d:d + 1]))
                        settled(nc.vector.scalar_tensor_tensor(inv, den, -1.0, den, ALU.mult, ALU.max))
                        settled(nc.vector.tensor_tensor(inv, inv, st.mcols[:, e["t"], 0:2, e["h"]], ALU.max))
                        settled(nc.vector.reciprocal(inv, inv))
                        s = st.decay[:, 0, 0:nk]
                        settled(nc.vector.tensor_scalar(s, s, inv[:, 0:1], None, ALU.mult))
                        dve.wait_ge(pt_done, i0 - 1)
                        nc.vector.scalar_tensor_tensor(w, st.decay[:, 1, 0:nk], inv[:, 1:2], s, ALU.mult, ALU.add)\
                            .then_inc(probs_done, 1)

                def output(i):
                    e, i0 = st.items[i], k0 + i
                    if st.mode != "mlstm" and e["hh"]:
                        pr, t = e["y"]
                        pair = st.at["pair"] + i // 2
                        dve.wait_ge(y_hi_done, pair + 1)
                        nc.vector.tensor_tensor(y_lo[:, pr, t * P:(t + 1) * P], ps[:, 4 + pair % 2, 0:P],
                                                y_hi[:, pr, t * P:(t + 1) * P].bitcast(F32), ALU.subtract).then_inc(y_saved, 1)

                if st.mode == "stick":
                    settled(nc.vector.memset(st.tmp[:, 7, 0:1], 1.0))
                for i in range(n + 3):
                    if i < n:
                        begin(i)
                    if st.mode == "mlstm" and i < n:
                        finish(i)
                    if st.mode != "mlstm" and 1 <= i <= n:
                        finish(i - 1)
                    if i >= 3:
                        output(i - 3)

            def inverse_root(st, n):
                dve.wait_ge(root_done, st.at["root"] + 1)
                settled(nc.vector.reciprocal(small[:, 64:64 + n], small[:, 64:64 + n]))

            def head_norm(st):
                t, n = st.tiles, st.n
                x = st.src.rearrange("p t (h d) -> p (t h) d", d=HD)
                settled(nc.vector.tensor_tensor(st.sq, st.src, st.src, ALU.mult))
                nc.vector.tensor_reduce(small[:, 0:t * n], st.sq.rearrange("p t (h d) -> p (t h) d", d=HD), AX.X, ALU.add)\
                    .then_inc(sums_done, 1)
                inverse_root(st, t * n)
                settled(nc.vector.tensor_tensor(x, x, small[:, 64:64 + t * n].unsqueeze(2).to_broadcast([P, t * n, HD]), ALU.mult))
                for i in range(t):
                    heads = st.src[:, i, :].rearrange("p (h d) -> p h d", d=HD)
                    for h0, h1, g, scale in st.parts:
                        part = heads[:, h0:h1, :]
                        ins = nc.vector.scalar_tensor_tensor(part, part, scale, g_rows[:, g:g + 1, :].to_broadcast([P, h1 - h0, HD]),
                                                             ALU.mult, ALU.mult)
                settled(ins)
                if not st.rope:
                    return
                rot = st.sq
                for i in range(TT):
                    heads = st.src[:, i, :].rearrange("p (h d) -> p h d", d=HD)
                    quarters = st.src[:, i, :].rearrange("p (h r s e) -> p h r s e", h=n, r=2, s=2)
                    out_q = rot[:, i, :].rearrange("p (h r s e) -> p h r s e", h=n, r=2, s=2)
                    sin_q = rope_sin[:, i:i + 1, :].rearrange("p o (r s e) -> p o r s e", r=2, s=2)
                    for s in range(2):
                        ins = nc.vector.tensor_tensor(out_q[:, :, :, s, :], quarters[:, :, :, 1 - s, :],
                                                      sin_q[:, :, :, s, :].to_broadcast([P, n, 2, HD // 4]), ALU.mult)
                    settled(ins)
                    settled(nc.vector.tensor_tensor(heads, heads, rope_cos[:, i:i + 1, :].to_broadcast([P, n, HD]), ALU.mult))
                    settled(nc.vector.tensor_tensor(st.src[:, i, :], st.src[:, i, :], rot[:, i, :], ALU.add))
                for side in range(2):
                    nc.vector.tensor_copy(st.kd[:, :, :, side, :],
                                          st.src[:, :, W_HEADS:].rearrange("p t (g d) -> p t g d", d=HD))

            def ml_rows(st):
                n = 4 * ML_H
                u, l, lf = st.rows[0:n, 0, :], st.arows[0:n, 0, :], st.rows[0:n, 1, :]
                dve.wait_ge(stage_act, st.at["a"] + 1)
                nc.vector.scalar_tensor_tensor(lf, u, 0.0, l, ALU.min, ALU.subtract).then_inc(stage_dve, 1)
                dve.wait_ge(stage_pe, st.at["pe"] + 1)
                one = ones[0:ML_H, 0:1].to_broadcast([ML_H, T])
                for d in range(2):
                    ig, fg = ps[0:ML_H, 2 * d, :], ps[0:ML_H, 2 * d + 1, :]
                    b, m, av = st.d[0:ML_H, d, :], st.d[0:ML_H, 2 + d, :], st.arows[0:ML_H, d, :]
                    ctx_, x_ = (slice(T, 2 * T), slice(0, T))
                    step = -1 if d else 1
                    carry = slice(T, T + 1) if d else slice(2 * T - 1, 2 * T)
                    settled(nc.vector.tensor_tensor_scan(b[:, ctx_][:, ::step], one, fg[:, ctx_][:, ::step], 0.0,
                                                         ALU.mult, ALU.add))
                    settled(nc.vector.tensor_tensor_scan(b[:, x_][:, ::step], one, fg[:, x_][:, ::step], b[:, carry],
                                                         ALU.mult, ALU.add))
                    settled(nc.vector.tensor_tensor(av, ig, b, ALU.subtract))
                    settled(nc.vector.tensor_tensor_scan(m[:, ctx_][:, ::step], av[:, ctx_][:, ::step], av[:, ctx_][:, ::step],
                                                         0.0, ALU.max, ALU.max))
                    settled(nc.vector.tensor_tensor_scan(m[:, x_][:, ::step], av[:, x_][:, ::step], av[:, x_][:, ::step],
                                                         m[:, carry], ALU.max, ALU.max))
                    ins = nc.vector.tensor_tensor(b, b, m, ALU.add)
                ins.then_inc(stage_dve, 1)

            def route(st):
                r = st.route
                dve.wait_ge(stage_pe, st.at["pe"] + 1)
                settled(nc.vector.tensor_copy(r[:, :, 16:24], ps[:, 0, 0:TT * N_EXP].rearrange("p (t e) -> p t e", e=N_EXP)))
                for t in range(TT):
                    settled(nc.vector.max(r[:, t, 24:32], r[:, t, 16:24]))
                    settled(nc.vector.max_index(r[:, t, 32:40].bitcast(U32), r[:, t, 24:32], r[:, t, 16:24]))
                    settled(nc.vector.tensor_copy(r[:, t, 40:48], r[:, t, 32:40].bitcast(U32)))
                nc.vector.tensor_tensor(r[:, :, 48:49], r[:, :, 25:26], r[:, :, 24:25], ALU.subtract).then_inc(stage_dve, 1)
                dve.wait_ge(stage_act, st.at["a"] + 1)
                settled(nc.vector.tensor_scalar(r[:, :, 50:51], r[:, :, 49:50], 1.0, None, ALU.add))
                settled(nc.vector.reciprocal(r[:, :, 50:51], r[:, :, 50:51]))
                settled(nc.vector.tensor_tensor(r[:, :, 51:52], r[:, :, 49:50], r[:, :, 50:51], ALU.mult))
                for t in range(TT):
                    for c in range(2):
                        ins = nc.vector.tensor_scalar(r[:, t, 8 * c:8 * c + 8], expert_no[:, :], r[:, t, 40 + c:41 + c],
                                                      r[:, t, 50 + c:51 + c], ALU.is_equal, ALU.mult)
                settled(ins)
                nc.vector.tensor_tensor(r[:, :, 0:8], r[:, :, 0:8], r[:, :, 8:16], ALU.add)

            def mod_cols(st):
                dve.wait_ge(stage_pe, st.at["pe"] + 1)
                n = MOD_W // P
                bc = col_second(st.l, "b_mod")
                settled(nc.vector.tensor_tensor(mod[:, :, :], ps[:, 0, 0:2 * n].rearrange("p (b s) -> p b s", s=2),
                                                cols[:, bc:bc + n].unsqueeze(2).to_broadcast([P, n, 2]), ALU.add))
                for i, (pre, post) in enumerate((("g_pre_mix", "g_post_mix"), ("g_pre_ffn", "g_post_ffn"))):
                    at = 3 * i * DC
                    g = cols[:, col_second(st.l, pre):][:, 0:DC].unsqueeze(2).to_broadcast([P, DC, 2])
                    nc.vector.scalar_tensor_tensor(mod_gain[:, i, :, :], mod[:, at + DC:at + 2 * DC, :], 1.0, g, ALU.add, ALU.mult)
                    g = cols[:, col_second(st.l, post):][:, 0:DC].unsqueeze(2).to_broadcast([P, DC, 2])
                    nc.vector.tensor_tensor(mod_post[:, i, :, :], mod[:, at + 2 * DC:at + 3 * DC, :], g, ALU.mult)

            def post(st):
                for s in range(2):
                    for c in range(DC):
                        ins = nc.vector.tensor_scalar(st.diag[:, s, c, :], ident[:, :], mod_post[:, st.which, c, s:s + 1], None,
                                                      ALU.mult)
                ins.then_inc(stage_dve, 1)
                dve.wait_ge(stage_pe, st.at["pe"] + 1)
                inverse_root(st, st.nq)
                for t in range(st.nq):
                    s = t // TT
                    gain = ps[:, 2 * s:2 * s + 2, :].rearrange("p b n -> p (b n)")
                    settled(nc.vector.scalar_tensor_tensor(st.o[:, t, :], st.o[:, t, :], small[:, 64 + t:65 + t], gain,
                                                           ALU.mult, ALU.mult))
                    nc.vector.tensor_tensor(x_tm[:, t, :], x_tm[:, t, :], st.o[:, t, :], ALU.add)

            def ml_norm(st):
                n = ML_H * st.nq
                settled(nc.vector.tensor_tensor(st.sq, st.mh, st.mh, ALU.mult))
                nc.vector.tensor_reduce(small[:, 0:n], st.sq.rearrange("p h t e -> p (h t) e"), AX.X, ALU.add).then_inc(sums_done, 1)
                inverse_root(st, n)
                rs = small[:, 64:64 + n].rearrange("p (h t) -> p h t", t=st.nq).unsqueeze(3).to_broadcast([P, ML_H, st.nq, ML_D])
                nc.vector.tensor_tensor(st.mh, st.mh, rs, ALU.mult)

            first = True
            for st in plan:
                if st.kind == "segment":
                    if first:
                        split(st.seg, 0, 0)
                        first = False
                    stream(st.seg)
                elif st.kind == "barrier":
                    dve.drain().then_inc(at_barrier, 1)
                    dve.wait_ge(at_barrier, 4 * (st.at["barrier"] + 1))
                elif st.kind == "norm":
                    inverse_root(st, st.tiles)
                    for t in range(st.tiles):
                        nc.vector.tensor_scalar(XN[:, t, :], x_tm[:, t, :], small[:, 64 + t:65 + t], None, ALU.mult)
                elif st.kind == "turn":
                    def value(i):
                        src, gain, shift, hi, lo = st.items[i]
                        i0 = st.at["turn"] + i
                        v = turn_value[:, i0 % 2, :].rearrange("p (c t) -> p c t", t=P)
                        t_ = ps[:, i0 % 4, :].rearrange("p (c t) -> p c t", t=P)
                        dve.wait_ge(turned, i0 + 1)
                        dve.wait_ge(split_done, i0 - 1)
                        if gain is None:
                            ins = nc.vector.tensor_copy(v, t_)
                        else:
                            ins = nc.vector.tensor_tensor(v, t_, gain.unsqueeze(2).to_broadcast([P, 4, P]), ALU.mult)
                            if shift is not None:
                                settled(ins)
                                ins = nc.vector.tensor_tensor(v, v, shift.unsqueeze(2).to_broadcast([P, 4, P]), ALU.add)
                        ins.then_inc(value_ready, 1)

                    def lower(i):
                        src, gain, shift, hi, lo = st.items[i]
                        i0 = st.at["turn"] + i
                        dve.wait_ge(split_hi_done, i0 + 2)
                        nc.vector.tensor_tensor(lo, turn_value[:, i0 % 2, :].rearrange("p (c t) -> p c t", t=P),
                                                hi.bitcast(F32), ALU.subtract).then_inc(split_done, 1)

                    for i in range(len(st.items) + 1):
                        if i < len(st.items):
                            value(i)
                        if i:
                            lower(i - 1)
                elif st.kind == "attend":
                    attend(st)
                elif st.kind == "fox_rows":
                    u, lf, l, neg = (st.rows[0:NH, i, 0:T] for i in range(4))
                    dve.wait_ge(stage_act, st.at["a"] + 1)
                    settled(nc.vector.scalar_tensor_tensor(lf, u, 0.0, l, ALU.min, ALU.subtract))
                    settled(nc.vector.tensor_tensor_scan(l, ones[0:NH, 0:1].to_broadcast([NH, T]), lf, 0.0, ALU.mult, ALU.add))
                    nc.vector.tensor_scalar(neg, l, -1.0, None, ALU.mult)
                elif st.kind in ("head_norm", "ml_rows", "route", "mod_cols", "post", "ml_norm"):
                    {"head_norm": head_norm, "ml_rows": ml_rows, "route": route, "mod_cols": mod_cols, "post": post,
                     "ml_norm": ml_norm}[st.kind](st)

        @block.tensor
        def _(pe):
            pe.wait_ge(params_loaded, PARAMS)
            pe.wait_ge(constants_set, 1)
            mm = nc.tensor.matmul

            def use(seg, it, j):
                q, k, m, opens, closes, width, source = seg.units[j]
                b = 4 * (q % 2)
                if opens:
                    pe.wait_ge(results_saved, seg.result(it, q) - (1 if q else 0))
                if seg.mode == "ffn" and q == FB:
                    pe.wait_ge(act_done, it * FB + (seg.at["act"] + k + m))
                pe.wait_ge(hi_ready, seg.unit(it, j) + 1)
                wh, wl = w_hi[:, j % HL, :], w_lo[:, j % HL, :]
                for w in (wh, wl):
                    upper = w is wh
                    if not upper:
                        ins.then_inc(hi_used, 1)
                        pe.wait_ge(lo_ready, seg.unit(it, j) + 1)
                    if seg.mode == "mod":
                        for c in range(m):
                            ins = mm(ps[0:4, b, :], c_split[:, k + c, :], w[:, c * width:(c + 1) * width],
                                     start=upper and opens and c == 0, stop=not upper and closes and c == m - 1)
                    elif seg.mode == "fm" or (seg.mode == "ffn" and q < FB):
                        ah, al = seg.A
                        M = min(width, P)
                        for f in range(width // M):
                            bank = b + f if seg.mode == "fm" else b + (0 if opens else 1)
                            dst = ps[0:M, bank, 0:seg.N]
                            for c in range(m):
                                f0 = c * width + f * P
                                for x in ((ah, al) if upper else (ah,)):
                                    ins = mm(dst, w[:, f0:f0 + M], x[:, k + c, 0:seg.N], start=upper and k + c == 0 and x is ah,
                                             stop=not upper and k + c == DC - 1)
                    else:
                        branch = seg.evac == "merge" and q % 2
                        biased = seg.evac == "merge" and not branch and seg.bias_layer is not None
                        for t in range(seg.tiles):
                            dst = ps[:, b + t, 0:width]
                            for c in range(m):
                                if seg.mode == "ffn":
                                    at = (k + c) * seg.N + t * P
                                    xh, xl = act_hi[:, at:at + P], act_lo[:, at:at + P]
                                else:
                                    ah, al = seg.B if branch else seg.A
                                    xh, xl = ah[:, k + c, t * P:(t + 1) * P], al[:, k + c, t * P:(t + 1) * P]
                                last = not upper and closes and c == m - 1
                                for x in ((xh, xl) if upper else (xh,)):
                                    ins = mm(dst, x, w[:, c * width:(c + 1) * width], start=upper and opens and c == 0 and x is xh,
                                             stop=last and not biased)
                                if last and biased:
                                    row = 2 * seg.n_branch + q // 2
                                    ins = mm(dst, row_of[0:4, row, :], bias_rows[0:4, seg.bias_layer, :], start=False, stop=True)
                ins.then_inc(units_used, 1)

            def attend(st):
                k0 = st.at["item"]
                n = len(st.items)

                def scores(i):
                    e, i0 = st.items[i], k0 + i
                    nk = e["nk"]
                    if st.mode == "mlstm":
                        pe.wait_ge(probs_done, i0 - 1)
                        pe.wait_ge(ml_saved, st.at["ml"] + i - 1)
                        for d in range(2):
                            dst = ps[:, 4 + 2 * (i0 % 2) + d, :]
                            row = row_of[0:ML_H, e["h"], :]
                            mm(dst[:, 0:T], row, st.arows[0:ML_H, d, e["k0"]:e["k0"] + T], start=True, stop=False)
                            mm(dst[:, 0:T], ident[:, :], e["masks"][d], start=False, stop=True)
                            if nk > T:
                                mm(dst[:, T:nk], row, st.arows[0:ML_H, d, T:2 * T], start=True, stop=True)
                        mm(ps[:, i0 % 2, 0:nk], e["q"], e["k"], start=True, stop=True).then_inc(scores_done, 1)
                        return
                    pe.wait_ge(exp_done, i0 - 1)
                    n_add = T if e["add"] and nk > T else nk
                    ins = mm(ps[:, i0 % 2, 0:n_add], e["q"], e["k"][:, 0:n_add], start=True, stop=not e["add"])
                    for j, (lhs, rhs, ready) in enumerate(e["add"]):
                        if ready is not None:
                            pe.wait_ge(bias_ready, ready)
                        ins = mm(ps[:, i0 % 2, 0:n_add], lhs, rhs, start=False, stop=j == len(e["add"]) - 1)
                    if n_add < nk:
                        ins = mm(ps[:, i0 % 2, n_add:nk], e["q"], e["k"][:, n_add:nk], start=True, stop=True)
                    ins.then_inc(scores_done, 1)

                def turn(i):
                    e, i0 = st.items[i], k0 + i
                    pe.wait_ge(probs_done, i0 + 1)
                    pe.wait_ge(pt_saved, i0 - 1)
                    for c in range(e["nk"] // P):
                        ins = nc.tensor.transpose(ps[:, 2 + i0 % 2, c * P:(c + 1) * P], prob[:, i0 % 2, c * P:(c + 1) * P],
                                                  ident[:, :])
                    ins.then_inc(pt_done, 1)

                def gather(i):
                    e, i0 = st.items[i], k0 + i
                    chunks = e["nk"] // P
                    pe.wait_ge(pt_saved, i0 + 1)
                    if st.mode == "mlstm":
                        for c in range(chunks):
                            ins = mm(ps[:, 4 + 2 * (i0 % 2), 0:P], prob_t[:, i0 % 2, c * P:(c + 1) * P], e["v"][c],
                                     start=c == 0, stop=c == chunks - 1)
                    else:
                        pair = st.at["pair"] + i // 2
                        if not e["hh"]:
                            pe.wait_ge(y_saved, pair - 1)
                        for c in range(chunks):
                            ins = mm(ps[:, 4 + pair % 2, 0:P], e["v"][c], prob_t[:, i0 % 2, c * P:(c + 1) * P],
                                     start=c == 0 and not e["hh"], stop=c == chunks - 1 and e["hh"] == 1)
                    ins.then_inc(pv_done, 1)

                if st.mode == "mlstm":
                    for i in range(n + 2):
                        if i >= 2:
                            gather(i - 2)
                        if i < n:
                            scores(i)
                        if 1 <= i <= n:
                            turn(i - 1)
                else:
                    for i in range(n + 3):
                        if i < n:
                            scores(i)
                        if 2 <= i <= n + 1:
                            turn(i - 2)
                        if i >= 3:
                            gather(i - 3)

            for st in plan:
                if st.kind == "segment":
                    seg = st.seg
                    if seg.iters > 2:
                        with pe.Fori(0, seg.iters) as it:
                            for j in range(seg.n):
                                use(seg, it, j)
                    else:
                        for it in range(seg.iters):
                            for j in range(seg.n):
                                use(seg, it, j)
                elif st.kind == "barrier":
                    pe.drain().then_inc(at_barrier, 1)
                    pe.wait_ge(at_barrier, 4 * (st.at["barrier"] + 1))
                elif st.kind == "turn":
                    for i, (src, gain, shift, hi, lo) in enumerate(st.items):
                        i0 = st.at["turn"] + i
                        pe.wait_ge(value_ready, i0 - 3)
                        for c in range(4):
                            ins = nc.tensor.transpose(ps[:, i0 % 4, c * P:(c + 1) * P], src[c], ident[:, :])
                        ins.then_inc(turned, 1)
                elif st.kind == "turn_heads":
                    for i, (src, dst) in enumerate(st.jobs):
                        if i >= 4:
                            pe.wait_ge(stage_act, st.at["a"] + i - 3)
                        for c, s in enumerate(src):
                            ins = nc.tensor.transpose(ps[:, i % 4, c * P:(c + 1) * P], s, ident[:, :])
                        ins.then_inc(stage_pe, 1)
                elif st.kind == "attend":
                    attend(st)
                elif st.kind == "ml_rows":
                    n = 4 * ML_H
                    pe.wait_ge(stage_dve, st.at["d"] + 1)
                    for kind in range(4):
                        ins = mm(ps[0:ML_H, kind, :], ident[0:n, kind * ML_H:(kind + 1) * ML_H], st.rows[0:n, kind % 2, :],
                                 start=True, stop=True)
                    ins.then_inc(stage_pe, 1)
                    pe.wait_ge(stage_dve, st.at["d"] + 2)
                    for t in range(2 * TT):
                        for kind in range(4):
                            at = (t * 4 + kind) * ML_H
                            ins = nc.tensor.transpose(ps[:, 4, at:at + ML_H], st.d[0:ML_H, kind, t * P:(t + 1) * P],
                                                      ident[0:ML_H, 0:ML_H])
                    ins.then_inc(stage_pe, 1)
                elif st.kind == "route":
                    for t in range(TT):
                        ins = nc.tensor.transpose(ps[:, 0, t * N_EXP:(t + 1) * N_EXP], st.logits[:, t * P:(t + 1) * P],
                                                  ident[0:N_EXP, 0:N_EXP])
                    ins.then_inc(stage_pe, 1)
                elif st.kind == "mod_cols":
                    for c in range(MOD_W // P):
                        ins = mm(ps[:, 0, 2 * c:2 * c + 2], st.rows[0:4, c * P:(c + 1) * P], pair_sum[:, :], start=True, stop=True)
                    ins.then_inc(stage_pe, 1)
                elif st.kind == "post":
                    pe.wait_ge(stage_dve, st.at["d"] + 1)
                    for s in range(2):
                        for c in range(DC):
                            ins = mm(ps[:, 2 * s + c // 4, (c % 4) * P:(c % 4 + 1) * P], ones[:, :], st.diag[:, s, c, :],
                                     start=True, stop=True)
                    ins.then_inc(stage_pe, 1)


_WEIGHTS = ["w_in", "w_o_sb", "w_o_fox", "w_out", "w_gu_dense", "w_dn_dense", "w_router", "w_gu_exp", "w_dn_exp", "w_mod_2",
            "w_in_2", "w_branch_2", "w_out_2", "w_up_2", "w_down_2", "x", "ctx_2"]


def _constants():
    t, s = np.arange(T)[:, None], np.arange(T)[None, :]

    def tiles(m):
        return np.ascontiguousarray(m.astype(np.float32).reshape(TT, P, -1).transpose(1, 0, 2))

    c0 = np.clip(t % GRID_W - NA_C // 2, 0, GRID_W - NA_C)
    inside = (s % GRID_W >= c0) & (s % GRID_W < c0 + NA_C)
    half = HD // 2
    inv = np.float32(ROPE_THETA) ** (-np.arange(0, half, 2, dtype=np.float32) / np.float32(half))
    n = np.arange(T)
    ang_r, ang_c = ((n // GRID_W).astype(np.float32)[:, None] * inv, (n % GRID_W).astype(np.float32)[:, None] * inv)
    ang = np.concatenate([ang_r, ang_r, ang_c, ang_c], axis=-1)
    sign = np.repeat(np.array([-1, 1, -1, 1], np.float32), HD // 4)
    row_of = np.zeros((NH, NH, P), np.float32)
    row_of[np.arange(NH), np.arange(NH)] = 1
    return {
        "ident": np.eye(P, dtype=np.float32), "row_of": row_of,
        "causal": tiles(np.where(s <= t, 0, NEG)), "anti": tiles(np.where(s >= t, 0, NEG)),
        "strict": tiles(np.where(s < t, -NEG, -BOUND)), "window": tiles(np.where(inside, 0, NEG)),
        "rope_cos": tiles(np.cos(ang)), "rope_sin": tiles(np.sin(ang) * sign),
        "pair_sum": np.array([[1, 0], [0, 1], [1, 0], [0, 1]], np.float32),
        "expert_no": np.arange(N_EXP, dtype=np.float32),
    }


def _laid_out(v):
    def columns(x):
        return np.asarray(x).reshape(-1, P).T

    parts = []
    for l in range(DEPTH):
        parts += [columns(v["g_mix"][l]), columns(v["g_ffn"][l])]
    for l in range(DEPTH):
        parts += [columns(v[n + "_2"][l]) for n in ("g_pre_mix", "g_pre_ffn", "g_post_mix", "g_post_ffn", "g_ml_out", "b_mod",
                                                    "conv_b", "conv_w")]
    parts.append(np.stack([columns(v["c_2"][0]), columns(v["c_ctx_2"])], axis=-1).reshape(P, -1))
    gate_bias = np.zeros((4 * ML_H, 2 * DEPTH), np.float32)
    gate_bias[0:NH, 0:DEPTH] = np.asarray(v["b_f"]).T
    gate_bias[:, DEPTH:] = np.asarray(v["b_ml_gates_2"]).T
    rpb = np.asarray(v["na_rpb_2"])
    padded = np.zeros(rpb.shape[:3] + (2 * GRID_W,), np.float32)
    padded[..., GRID_W - NA_C:GRID_W - NA_C + 2 * NA_C - 1] = rpb
    bias = np.zeros(rpb.shape[:2] + (ROWS, GRID_W, ROWS, GRID_W), np.float32)
    for r in range(ROWS):
        for c in range(GRID_W):
            bias[:, :, r, c] = padded[:, :, NA_R - 1 - r:NA_R - 1 - r + ROWS, GRID_W - 1 - c:2 * GRID_W - 1 - c]
    rows = [np.asarray(v[n])[l] for sfx in ("", "_2") for l in range(DEPTH) for n in ("g_q" + sfx, "g_k" + sfx)]
    return {"cols": np.ascontiguousarray(np.concatenate(parts, axis=1)), "gate_bias": gate_bias, "position_bias": bias.reshape(DEPTH, NH, T, T),
            "g_rows": np.stack(rows), "bias_rows": np.ascontiguousarray(np.asarray(v["b_gate"]).reshape(DEPTH, 4, NT).transpose(1, 0, 2))}


def kernel(**inputs):
    import concourse.bacc as bacc
    from concourse.bass_utils import run_bass_kernel_spmd

    given = {n: np.ascontiguousarray(inputs[n]) for n in _WEIGHTS}
    given.update(_laid_out(inputs))
    given.update(_constants())
    nc = bacc.Bacc("TRN2", target_bir_lowering=False, num_devices=1)
    arrays = {f"in_{n}": x for n, x in given.items()}
    aps = {n: nc.dram_tensor(f"in_{n}", x.shape, F32, kind="ExternalInput").ap() for n, x in given.items()}
    out = nc.dram_tensor("out", (1, T, D), F32, kind="ExternalOutput").ap()
    build(nc, aps, out)
    r = run_bass_kernel_spmd(nc, [arrays], core_ids=[0])
    return r.results[0]["out"]
```

```python
import concourse.bass as bass
from concourse import mybir
from contextlib import ExitStack
import numpy as np

F32 = mybir.dt.float32
F32R = mybir.dt.float32r
U32 = mybir.dt.uint32
I32 = mybir.dt.int32
ALU = mybir.AluOpType
ACT = mybir.ActivationFunctionType
AX = mybir.AxisListType

P = 128
D = 1024
T = 256
TT = T // P
DC = D // P
DEPTH = 2
HD = 64
NH = 8
W_HEADS = NH * HD
BC = W_HEADS // P
KV = 2
ML_H, ML_D = 4, 128
D_FF = 2816
FE = 1408
FB = FE // P
N_EXP = 8
NB2 = 3
GROUPS = [(f, min(512, FE - f)) for f in range(0, FE, 512)]
DOWN = 2 * len(GROUPS)
UPS = DOWN * DC // 2
SEL_T, TURN, GATHER, SCATTER = 5, [(i + 1) * DC + 1 for i in range(len(GROUPS))], UPS + 3, (UPS + 8, 1)
PLACE, TAKES = 64, 80
GRID_W, NA_R, NA_C = 64, 8, 16
ROWS = T // GRID_W
EPS = 1e-6
NEG = -1e30
ROPE_THETA = 10000.0
BOUND = 85.0
NT = 512
M = 4
UNIT = 1024
RAW, HL = 4, 3
QK_SB, V_SB, QK_FX, V_FX, F_FX, G_1 = 0, 1024, 1536, 2560, 3072, 3080
MQ, MK, MV, MO, MG, AQ, NQ, NK, NV, G_2 = 0, 512, 1024, 1536, 2048, 2064, 2832, 3344, 3856, 4368
MOD_W = 6 * D
MOD_N = 3
BANKS = 8

COL_FIRST = 2 * DC
COL_CONV = 2 * D_FF // P
COL_SECOND = 4 * DC + BC + MOD_W // P + 4 * COL_CONV
COL_C = DEPTH * (COL_FIRST + COL_SECOND)
COLS = COL_C + 2 * DC


def col_first(layer, name):
    return layer * COL_FIRST + {"g_mix": 0, "g_ffn": DC}[name]


def col_second(layer, name):
    at = 0
    for known, n in (("g_pre_mix", DC), ("g_pre_ffn", DC), ("g_post_mix", DC), ("g_post_ffn", DC), ("g_ml_out", BC),
                     ("b_mod", MOD_W // P), ("conv_b", COL_CONV), ("conv_w", 3 * COL_CONV)):
        if known == name:
            return DEPTH * COL_FIRST + layer * COL_SECOND + at
        at += n
    raise KeyError(name)


class Stream:

    def __init__(self, sem, name):
        self.raw_loaded = [sem(f"{name}raw_loaded_{i}") for i in range(RAW)]
        self.hi_ready = sem(f"{name}hi_ready")
        self.lo_ready = sem(f"{name}lo_ready")
        self.hi_used = sem(f"{name}hi_used")
        self.units_used = sem(f"{name}units_used")
        self.results_saved = sem(f"{name}results_saved")


class Experts:

    def __init__(self, sem, name):
        self.sel_ready = sem(f"{name}sel_ready")
        self.gathered = sem(f"{name}gathered")
        self.xg_value = sem(f"{name}xg_value")
        self.xg_hi = sem(f"{name}xg_hi")
        self.xg_done = sem(f"{name}xg_done")
        self.selt_turned = sem(f"{name}selt_turned")
        self.selt_saved = sem(f"{name}selt_saved")
        self.act_turned = sem(f"{name}act_turned")
        self.act_hi_done = sem(f"{name}act_hi_done")
        self.act_done = sem(f"{name}act_done")
        self.scattered = sem(f"{name}scattered")
        self.accumulated = sem(f"{name}accumulated")
        self.all = [self.sel_ready, self.gathered, self.xg_value, self.xg_hi, self.xg_done, self.selt_turned, self.selt_saved,
                    self.act_turned, self.act_hi_done, self.act_done, self.scattered, self.accumulated]


class Segment:

    def __init__(self, units, iters, mode, at, evac, A=None, B=None, N=None, tiles=None, dst=None, scale=None, bias=None,
                 M=None, tmp=None, route=None, n_branch=None, gates=None, bias_layer=None, vp=None, o=None, cw=None, cb=None,
                 down=None, ex=None, half=None, buf=None):
        self.units, self.iters, self.n = units, iters, len(units)
        self.looped = iters > 2
        assert not self.looped or self.n % RAW == 0 and self.n % HL == 0
        self.results = max(u[0] for u in units) + 1
        self.next, self.first = None, False
        self.alone = mode == "moe"
        self.sig = self.unit0 = self.result0 = self.flag = self.before = self.ready = None
        self.down = down if down is not None else self.results
        self.ex, self.half, self.buf = ex, half, buf
        self.mode, self.at, self.evac = mode, at, evac
        self.A, self.B, self.N, self.tiles = A, B, N, tiles
        self.dst, self.scale, self.bias, self.M = dst, scale, bias, M
        self.tmp, self.route, self.o, self.cw, self.cb = tmp, route, o, cw, cb
        self.n_branch, self.gates, self.bias_layer, self.vp = n_branch, gates, bias_layer, vp

    def unit(self, it, j):
        return it * self.n + (self.unit0 + j)

    def result(self, it, q):
        return it * self.results + (self.result0 + q)

    def slot(self, it, j, slots):
        return (self.unit0 + j + (0 if self.looped else it * self.n)) % slots

    def loaded(self, it, j):
        if self.looped:
            return it * (16 * self.n // RAW) + 16 * ((self.unit0 + j) // RAW)
        return 16 * ((self.unit0 + it * self.n + j) // RAW)


class Step:

    def __init__(self, kind, at=None, seg=None, tiles=None, items=None, mode=None, bias=None, tmp=None, arows=None, mcols=None,
                 decay=None, src=None, sq=None, n=None, parts=None, rope=None, kd=None, jobs=None, dst=None, rows=None,
                 logits=None, route=None, l=None, d=None, mh=None, nq=None, o=None, which=None, diag=None, buf=None):
        self.kind, self.at, self.seg = kind, at, seg
        self.tiles, self.items, self.mode, self.jobs, self.dst = tiles, items, mode, jobs, dst
        self.bias, self.tmp, self.decay, self.arows, self.mcols = bias, tmp, decay, arows, mcols
        self.src, self.sq, self.n, self.parts, self.rope, self.kd = src, sq, n, parts, rope, kd
        self.rows, self.logits, self.route, self.l, self.d = rows, logits, route, l, d
        self.mh, self.nq, self.o, self.which, self.diag, self.buf = mh, nq, o, which, diag, buf


def build(nc, a, out):
    ctx = ExitStack()
    with ctx:
        def sb(name, shape, dt=F32):
            return ctx.enter_context(nc.sbuf_tensor(name, shape, dt))

        def sem(name):
            return ctx.enter_context(nc.semaphore(name))

        raw = sb("raw", [P, RAW, UNIT])
        w_hi = sb("w_hi", [P, HL, UNIT], F32R)
        w_lo = sb("w_lo", [P, HL, UNIT], F32R)
        x_tm = sb("x_tm", [P, 2 * TT, D])
        h_hi = sb("h_hi", [P, DC, 2 * T], F32R)
        h_lo = sb("h_lo", [P, DC, 2 * T], F32R)
        act_hi = sb("act_hi", [P, FB * 2 * T], F32R)
        act_lo = sb("act_lo", [P, FB * 2 * T], F32R)
        y_hi = act_hi[:, 0:BC * 2 * T].rearrange("p (c t) -> p c t", c=BC)
        y_lo = act_lo[:, 0:BC * 2 * T].rearrange("p (c t) -> p c t", c=BC)
        c_split = sb("c_split", [P, DC, 4], F32R)
        ident = sb("ident", [P, P])
        ones = sb("ones", [P, P])
        row_of = sb("row_of", [NH, NH, P])
        causal = sb("causal", [P, TT, T])
        anti = sb("anti", [P, TT, T])
        strict = sb("strict", [P, TT, T]) 
        window = sb("window", [P, TT, T])
        rope_cos = sb("rope_cos", [P, TT, HD])
        rope_sin = sb("rope_sin", [P, TT, HD])
        pair_sum = sb("pair_sum", [4, 2])
        expert_no = sb("expert_no", [P, N_EXP])
        cols = sb("cols", [P, COLS])
        mod = sb("mod", [P, MOD_W // P, 2])
        mod_gain = sb("mod_gain", [P, 2, DC, 2])
        mod_post = sb("mod_post", [P, 2, DC, 2])
        g_rows = sb("g_rows", [P, 4 * DEPTH, HD])
        gate_bias = sb("gate_bias", [4 * ML_H, 2 * DEPTH])
        bias_rows = sb("bias_rows", [4, DEPTH, NT])
        small = sb("small", [P, 192])
        eps = sb("eps", [P, 1])
        AR = 13312
        arena = sb("arena", [P, AR])
        ps = ctx.enter_context(nc.psum_tensor("ps", [P, BANKS, 512], F32))

        def view(at, *shape):
            n = int(np.prod(shape))
            assert at + n <= AR, (at, n, AR)
            names = "abcd"[:len(shape)]
            if len(shape) == 1:
                return arena[:, at:at + n]
            return arena[:, at:at + n].rearrange(f"p ({' '.join(names)}) -> p {' '.join(names)}",
                                                 **dict(zip(names, shape)))

        merged = view(0, 2 * TT, D)
        FREE = 2 * TT * D
        XN = view(FREE, 2 * TT, D)
        prob = view(FREE, 2, 512)
        prob_t = view(FREE + 1024, 2, 512)
        WORK = FREE + 2048
        turn_value = view(AR - 1024, 2, 512)

        main, over = Stream(sem, ""), Stream(sem, "over_")
        experts_main, experts_over = Experts(sem, "moe_"), Experts(sem, "over_moe_")
        params_loaded = sem("params_loaded")
        at_barrier = sem("at_barrier")
        sums_done = sem("sums_done")
        root_done = sem("root_done")
        turned = sem("turned")
        value_ready = sem("value_ready")
        split_hi_done = sem("split_hi_done")
        split_done = sem("split_done")
        scores_done = sem("scores_done")
        max_done = sem("max_done")
        bounded = sem("bounded")
        exp_done = sem("exp_done")
        probs_done = sem("probs_done")
        pt_done = sem("pt_done")
        pt_saved = sem("pt_saved")
        pv_done = sem("pv_done")
        ml_saved = sem("ml_saved")
        y_hi_done = sem("y_hi_done")
        y_saved = sem("y_saved")
        taps_ready = sem("taps_ready")
        gate_ready = sem("gate_ready")
        act_value = sem("act_value")
        act_hi_done = sem("act_hi_done")
        act_done = sem("act_done")
        stage_pe = sem("stage_pe")
        stage_act = sem("stage_act")
        stage_dve = sem("stage_dve")
        bias_loaded = sem("bias_loaded")
        bias_ready = sem("bias_ready")
        constants_set = sem("constants_set")
        act_step = sem("act_step")
        dve_step = sem("dve_step")
        stored = sem("stored")

        START = {"unit": RAW, "result": 2, "turn": 4, "item": 2, "pair": 2, "ml": 2}
        STARTS = [(x, n) for st in (main, over) for x, n in ((st.hi_ready, RAW), (st.lo_ready, RAW), (st.hi_used, RAW),
                                                             (st.units_used, RAW), (st.results_saved, 2))]
        STARTS += [(x, M) for e in (experts_main, experts_over) for x in e.all]
        STARTS += [(turned, 4), (value_ready, 4),
                  (split_hi_done, 4), (split_done, 4), (scores_done, 2), (exp_done, 2), (probs_done, 2), (pt_done, 2),
                  (pt_saved, 2), (pv_done, 2), (y_hi_done, 2), (y_saved, 2), (ml_saved, 2)]

        plan, segments = [], []
        count = {"barrier": 0, "sum": 0, "root": 0, "gate": 0, "tap": 0, "act": 0, "value": 0,
                 "pe": 0, "a": 0, "d": 0, "max": 0, "bounded": 0, "bias": 0, **START}

        def add(kind, **kw):
            plan.append(Step(kind, dict(count), **kw))

        def took(**kw):
            for name, n in kw.items():
                count[name] += n

        def add_segment(mode, units, iters=1, **kw):
            s = Segment(units, iters, mode, dict(count), **kw)
            s.sig, s.unit0, s.result0 = main, count["unit"], count["result"]
            took(unit=s.n * iters, result=s.results * iters)
            if segments and not segments[-1].alone:
                segments[-1].next = s
            else:
                s.first = True
            segments.append(s)
            plan.append(Step("segment", seg=s))
            return s

        def add_overflow(mode, units, iters, flag, **kw):
            s = Segment(units, iters, mode, dict(count), **kw)
            s.sig, s.unit0, s.result0 = over, START["unit"], START["result"]
            s.first = s.alone = True
            s.flag, s.before, s.ready = flag, segments[-1], count["d"]
            segments.append(s)
            plan.append(Step("overflow", seg=s))

        def meet():
            add("barrier")
            took(barrier=1)

        def tm_units(w, c0, q=0, chunks=DC, width=NT):
            n = UNIT // width
            return [(q, k, min(n, chunks - k), k == 0, k + n >= chunks, width,
                     lambda it, k=k: w[k * P:min(k + n, chunks) * P, c0:c0 + width].rearrange("(c p) n -> p c n", p=P))
                    for k in range(0, chunks, n)]

        def fm_units(w, c0, q=0, width=2 * P):
            n = UNIT // (2 * P)
            return [(q, k, n, k == 0, k + n == DC, width,
                     lambda it, k=k: w[k * P:(k + n) * P, c0:c0 + width].rearrange("(c p) n -> p c n", p=P))
                    for k in range(0, DC, n)]

        def ffn_units(w_up, w_down):
            def up(it, half, b):
                f0 = half * D_FF + it * FE + b * P
                return w_up[:, f0:f0 + P].rearrange("(c p) n -> p c n", p=P)

            def down(it, k, m, half):
                return w_down[it * FE + k * P:it * FE + (k + m) * P, half * NT:(half + 1) * NT].rearrange("(c p) n -> p c n", p=P)

            units = [(b, 0, DC, half == 0, half == 1, P, lambda it, half=half, b=b: up(it, half, b))
                     for b in range(FB) for half in range(2)]
            for half in range(2):
                for k in range(0, FB, 2):
                    m = min(2, FB - k)
                    units.append((FB + half, k, m, k == 0, k + m == FB, NT,
                                  lambda it, k=k, m=m, half=half: down(it, k, m, half)))
            return units

        def expert_units(w_up, w_down):
            units = []
            for q in range(2 * len(GROUPS)):
                f, n = GROUPS[q // 2]
                for k in range(0, DC, 2):
                    units.append((q, k, 2, k == 0, k + 2 == DC, n, lambda it, k=k, n=n, f0=(q % 2) * FE + f:
                                  w_up[bass.ds(it, 1), k * P:(k + 2) * P, f0:f0 + n].rearrange("e (c p) n -> p (e c) n", p=P)))
            for half in range(2):
                for k in range(0, FB, 2):
                    m = min(2, FB - k)
                    units.append((DOWN + half, k, m, k == 0, k + m == FB, NT, lambda it, k=k, m=m, half=half:
                                  w_down[bass.ds(it, 1), k * P:(k + m) * P, half * NT:(half + 1) * NT]
                                  .rearrange("e (c p) n -> p (e c) n", p=P)))
            return units

        def norm(tiles):
            add("norm", tiles=tiles)
            took(root=1)
            meet()

        def turn(items):
            add("turn", items=items)
            took(turn=len(items))
            meet()

        def turn_tokens(src, tiles, gain, shift):
            turn([([src[:, t, (4 * h + c) * P:(4 * h + c + 1) * P] for c in range(4)],
                   gain(t)[:, 4 * h:4 * h + 4] if gain else None, shift(t)[:, 4 * h:4 * h + 4] if shift else None,
                   h_hi[:, 4 * h:4 * h + 4, t * P:(t + 1) * P], h_lo[:, 4 * h:4 * h + 4, t * P:(t + 1) * P])
                  for t in range(tiles) for h in range(2)])

        def attend(kind, items, bias=None, tmp=None, arows=None, mcols=None, decay=None):
            add("attend", mode=kind, items=items, bias=bias, tmp=tmp, arows=arows, mcols=mcols, decay=decay)
            took(item=len(items))
            if kind == "mlstm":
                took(ml=len(items))
            else:
                took(pair=len(items) // 2, max=len(items) if kind == "soft" else 0, bounded=len(items) if kind == "stick" else 0)
            meet()

        def head_norm(**kw):
            add("head_norm", **kw)
            took(sum=1, root=1)
            meet()

        def turn_heads(jobs):
            add("turn_heads", jobs=jobs)
            took(pe=len(jobs), a=len(jobs))
            meet()

        def merge(n, w, g0, w_b, tiles, bias_layer):
            units = []
            for dt in range(2):
                units += tm_units(w, g0 + dt * NT, 2 * dt)
                units += tm_units(w_b, dt * NT, 2 * dt + 1, BC)
            add_segment("tm", units, A=(h_hi, h_lo), B=(y_hi, y_lo), tiles=tiles, evac="merge", n_branch=n,
                        gates=view(WORK, 2 * TT, NT), bias_layer=bias_layer)
            meet()

        def mixed_out(w, tiles, **kw):
            turn_tokens(merged, tiles, None, None)
            add_segment("tm", tm_units(w, 0, 0) + tm_units(w, NT, 1), A=(h_hi, h_lo), tiles=tiles, **kw)
            meet()

        def first_layer(l):
            w = a["w_in"][l]
            qk = view(WORK, 2 * BC, T)
            v = view(WORK + 2048, TT, W_HEADS)
            tmp = view(WORK + 3072, 8, T)
            pre = view(WORK + 3072, TT, 2 * W_HEADS)
            sq = view(WORK + 5120, TT, 2 * W_HEADS)
            rows = view(TT * D, 4, 2 * T)
            H = (h_hi, h_lo)
            norm(TT)
            turn_tokens(XN, TT, lambda t: cols[:, col_first(l, "g_mix"):][:, 0:DC], None)
            add_segment("fm", sum((fm_units(w, QK_SB + q * 2 * P, q) for q in range(4)), []), A=H, N=T, evac="fm", dst=qk,
                        scale=[HD ** -0.5] * 2 + [1.0] * 2)
            add_segment("tm", tm_units(w, V_SB), A=H, tiles=TT, evac="tm", dst=v)
            meet()

            def heads(hh, pr, t):
                return dict(q=qk[hh * HD:(hh + 1) * HD, pr, t * P:(t + 1) * P],
                            k=qk[hh * HD:(hh + 1) * HD, BC + pr, 0:(t + 1) * P], nk=(t + 1) * P, add=[],
                            v=[v[:, s, (2 * pr + hh) * HD:(2 * pr + hh + 1) * HD] for s in range(t + 1)], hh=hh, y=(pr, t))

            order = [(hh, pr, t) for pr in range(BC) for t in range(TT) for hh in range(2)]
            attend("stick", [dict(heads(*o), cap=strict[:, o[2], 0:(o[2] + 1) * P]) for o in order], tmp=tmp)
            merge(0, w, G_1, a["w_o_sb"][l], TT, l)
            add_segment("tm", tm_units(w, QK_FX, 0) + tm_units(w, QK_FX + NT, 1), A=H, tiles=TT, evac="tm", dst=pre)
            add_segment("tm", tm_units(w, V_FX), A=H, tiles=TT, evac="tm", dst=v)
            add_segment("fm", fm_units(w, F_FX, 0, NH), A=H, N=T, evac="rows", dst=rows[0:NH, 0, 0:T],
                        bias=gate_bias[0:NH, l:l + 1], M=NH)
            meet()
            add("fox_rows", rows=rows)
            took(a=1)
            head_norm(src=pre, sq=sq, tiles=TT, n=2 * NH, parts=[(0, NH, 2 * l, HD ** -0.5), (NH, 2 * NH, 2 * l + 1, 1.0)],
                      rope=False)
            turn_heads([([pre[:, t, (part * BC + c) * P:(part * BC + c + 1) * P] for c in range(BC)],
                         qk[:, part * BC:(part + 1) * BC, t * P:(t + 1) * P]) for t in range(TT) for part in range(2)])
            attend("soft", [dict(heads(hh, pr, t),
                                 add=[(row_of[:, 2 * pr + hh, :], rows[0:NH, 3, 0:(t + 1) * P], None),
                                      (ident[:, :], causal[:, t, 0:(t + 1) * P], None)]) for hh, pr, t in order])
            merge(1, w, G_1 + D, a["w_o_fox"][l], TT, l)
            mixed_out(a["w_out"][l], TT, evac="residual")
            norm(TT)
            turn_tokens(XN, TT, lambda t: cols[:, col_first(l, "g_ffn"):][:, 0:DC], None)
            if l % 2:
                logits = view(2048, 2, 512)[0:N_EXP, 0, 0:T]
                route = view(3072, TT, 96)
                buf = dict(silu=view(0, 512), value=view(512, 512), y=view(1024, 2, 512), sel_t=view(3328, 2 * P),
                           sel=view(3584, TT, P), slot_no=view(3840, 2 * P), tokens=XN, upto=view(FREE + TT * D, P),
                           flag=view(FREE + TT * D + P, 1)[0:1, :].bitcast(I32))
                add_segment("fm", fm_units(a["w_router"][l // 2], 0, 0, N_EXP), A=H, N=T, evac="rows", dst=logits, bias=None,
                            M=N_EXP)
                meet()
                add("route", logits=logits, route=route, buf=buf)
                took(pe=2, d=3, a=1)
                meet()
            if l % 2:
                units = expert_units(a["w_gu_exp"][l // 2], a["w_dn_exp"][l // 2])
                for half, ex in enumerate((experts_main, experts_over)):
                    kw = dict(A=(h_hi[:, :, T:T + P], h_lo[:, :, T:T + P]), N=P, tiles=1, evac="experts", route=route, down=DOWN,
                              ex=ex, half=half, buf=buf, scale=cols[:, col_first(l, "g_ffn"):][:, 0:DC])
                    if half == 0:
                        add_segment("moe", units, N_EXP, **kw)
                    else:
                        add_overflow("moe", units, N_EXP, buf["flag"], **kw)
                    meet()
                return
            n = D_FF // FE
            add_segment("ffn", ffn_units(a["w_gu_dense"][l // 2], a["w_dn_dense"][l // 2]), n, A=H, N=T, tiles=TT, evac="swiglu",
                        tmp=view(0, 4, 2 * T), down=FB)
            took(act=FB * n, tap=FB * n)
            meet()

        def second_layer(l):
            w = a["w_in_2"][l]
            nq = TT if l == DEPTH - 1 else 2 * TT
            nn = 2 * TT
            H = (h_hi, h_lo)
            rows4 = view(0, MOD_W)
            units = []
            for q in range(MOD_N):
                for k in range(0, DC, 2):
                    units.append((q, k, 2, k == 0, k + 2 == DC, NT, lambda it, q=q, k=k:
                                  a["w_mod_2"][l][k * P:(k + 2) * P, bass.ds(it * (MOD_N * NT) + q * NT, NT)]
                                  .rearrange("(c p) n -> p c n", p=P)))
            add_segment("mod", units, MOD_W // (MOD_N * NT), evac="mod", dst=rows4)
            meet()
            add("mod_cols", rows=rows4, l=l)
            took(pe=1)
            meet()
            norm(nn)
            turn_tokens(XN, nn, lambda t: mod_gain[:, 0, :, t // TT], lambda t: mod[:, 0:DC, t // TT])

            def span(t):
                return 0 if t < TT else T

            mqk = view(WORK, 2 * ML_H, 2 * T)
            mv = view(WORK + 4096, nn, W_HEADS)
            arows = view(0, 2, 2 * T)
            rows = view(1024, 2, 2 * T)
            drows = view(FREE, 4, 2 * T)
            mcols = small[:, 128:192].rearrange("p (t k h) -> p t k h", t=nn, k=4)
            add_segment("fm", sum((fm_units(w, MQ + q * 2 * P, q) for q in range(4)), []), A=H, N=2 * T, evac="fm", dst=mqk,
                        scale=[1.0] * 2 + [ML_D ** -0.5] * 2)
            add_segment("tm", tm_units(w, MV), A=H, tiles=nn, evac="tm", dst=mv)
            add_segment("fm", fm_units(w, MG, 0, 4 * ML_H), A=H, N=2 * T, evac="rows", dst=rows[0:4 * ML_H, 0, :],
                        bias=gate_bias[0:4 * ML_H, DEPTH + l:DEPTH + l + 1], M=4 * ML_H)
            meet()
            add("ml_rows", rows=rows, d=drows, arows=arows, mcols=mcols)
            took(a=2, d=2, pe=2)
            meet()
            attend("mlstm", [dict(q=mqk[:, h, t * P:(t + 1) * P], k=mqk[:, ML_H + h, span(t):2 * T], nk=2 * T - span(t),
                                  k0=span(t), t=t, h=h, masks=(causal[:, t % TT, :], anti[:, t % TT, :]),
                                  v=[mv[:, s, h * ML_D:(h + 1) * ML_D] for s in range(span(t) // P, nn)],
                                  dst=mqk[:, h, t * P:(t + 1) * P])
                             for t in range(nq) for h in range(ML_H)], arows=arows, mcols=mcols,
                   decay=view(1024, 2, 512))
            mh = mqk[:, 0:ML_H, 0:nq * P].rearrange("p h (t e) -> p h t e", e=P)
            add("ml_norm", mh=mh, sq=view(WORK + 4096, ML_H, nq, P), nq=nq)
            took(sum=1, root=1)
            meet()
            add_segment("tm", tm_units(w, MO), A=H, tiles=nq, evac="ml_gate", gates=view(WORK + 4096, 2 * TT, NT),
                        dst=mqk[:, 0:ML_H, 0:nq * P].rearrange("p h (t e) -> p t h e", e=P))
            took(gate=1)
            meet()
            g = cols[:, col_second(l, "g_ml_out"):][:, 0:BC]
            turn([([mqk[:, c, t * P:(t + 1) * P] for c in range(BC)], g, None, y_hi[:, :, t * P:(t + 1) * P],
                   y_lo[:, :, t * P:(t + 1) * P]) for t in range(nq)])
            merge(0, w, G_2, a["w_branch_2"][l, 0], nq, None)
            QKW = (NH + KV) * HD
            pre = view(WORK, nn, QKW)
            sq = view(WORK + nn * QKW, nn, QKW)
            kd = view(WORK + nn * QKW, nn, KV, 2, HD)
            qT = view(WORK + nn * QKW + 1024, BC, 2 * T)
            kT = view(WORK + nn * QKW + 3072, KV, 2 * T)
            v = view(WORK + nn * QKW + 4096, nn, KV, HD)
            add_segment("tm", tm_units(w, AQ), A=H, tiles=nn, evac="tm", dst=pre)
            add_segment("tm", tm_units(w, AQ + W_HEADS, 0, DC, 2 * KV * HD), A=H, tiles=nn, evac="gqa_kv", dst=pre, vp=v)
            meet()
            head_norm(src=pre, sq=sq, tiles=nn, n=NH + KV, rope=True, kd=kd,
                      parts=[(0, NH, 2 * DEPTH + 2 * l, HD ** -0.5), (NH, NH + KV, 2 * DEPTH + 2 * l + 1, 1.0)])
            turn_heads([j for t in range(nn) for j in
                        (([pre[:, t, c * P:(c + 1) * P] for c in range(BC)], qT[:, :, t * P:(t + 1) * P]),
                         ([kd[:, t, g, :, :].rearrange("p a d -> p (a d)") for g in range(KV)], kT[:, :, t * P:(t + 1) * P]))])

            def gqa(hh, pr, t):
                g = 2 * pr // (NH // KV)
                return dict(q=qT[hh * HD:(hh + 1) * HD, pr, t * P:(t + 1) * P], k=kT[hh * HD:(hh + 1) * HD, g, span(t):2 * T],
                            nk=2 * T - span(t), add=[], v=[v[:, s, g, :] for s in range(span(t) // P, nn)], hh=hh, y=(pr, t))

            order = [(hh, pr, t) for pr in range(BC) for t in range(nq) for hh in range(2)]
            attend("soft", [gqa(*o) for o in order])
            merge(1, w, G_2 + D, a["w_branch_2"][l, 1], nq, None)
            nqk = view(WORK, 2 * BC, 2 * T)
            nv = view(WORK + 4096, nn, W_HEADS)
            nbias = view(WORK + 6144, 2, TT, T)
            add_segment("fm", sum((fm_units(w, NQ + q * 2 * P, q) for q in range(4)), []), A=H, N=2 * T, evac="fm", dst=nqk,
                        scale=[HD ** -0.5] * 2 + [1.0] * 2)
            add_segment("tm", tm_units(w, NV), A=H, tiles=nn, evac="tm", dst=nv)
            meet()

            def na(hh, pr, t):
                h = 2 * pr + hh
                return dict(q=nqk[hh * HD:(hh + 1) * HD, pr, t * P:(t + 1) * P],
                            k=nqk[hh * HD:(hh + 1) * HD, BC + pr, span(t):2 * T], nk=2 * T - span(t),
                            add=[(ident[:, :], nbias[:, hh, t, :], count["bias"] + h + 1)] if t < TT else [],
                            v=[nv[:, s, h * HD:(h + 1) * HD] for s in range(span(t) // P, nn)], hh=hh, y=(pr, t))

            attend("soft", [na(*o) for o in order], bias=(nbias, l, 2 * nq))
            took(bias=NH)
            merge(2, w, G_2 + 2 * D, a["w_branch_2"][l, 2], nq, None)
            o = view(FREE, 2 * TT, D)
            diag = view(FREE + 4096, 2, DC, P)
            mixed_out(a["w_out_2"][l], nq, evac="tm", dst=o)

            def post(which):
                add("post", o=o, nq=nq, which=which, diag=diag)
                took(root=1, d=1, pe=1)
                meet()

            post(0)
            norm(nq)
            turn_tokens(XN, nq, lambda t: mod_gain[:, 1, :, t // TT], lambda t: mod[:, 3 * DC:4 * DC, t // TT])
            add_segment("ffn", ffn_units(a["w_up_2"][l], a["w_down_2"][l]), D_FF // FE, A=H, N=nq * P, tiles=nq,
                        evac="conv", tmp=view(FREE + 4096, 4, 2 * T), o=o, cw=col_second(l, "conv_w"),
                        cb=col_second(l, "conv_b"), down=FB)
            n = FB * (D_FF // FE)
            took(act=n, tap=2 * n, gate=n, value=n)
            meet()
            post(1)

        for l in range(DEPTH):
            first_layer(l)
        for l in range(DEPTH):
            second_layer(l)

        params = [(x_tm[:, 0:TT, :], a["x"][0].rearrange("(t p) d -> p t d", p=P)),
                  (x_tm[:, TT:2 * TT, :], a["ctx_2"][0].rearrange("(t p) d -> p t d", p=P)),
                  (cols[:, :], a["cols"]), (ident[:, :], a["ident"]), (row_of[:, :, :], a["row_of"]),
                  (causal[:, :, :], a["causal"]), (anti[:, :, :], a["anti"]), (strict[:, :, :], a["strict"]),
                  (window[:, :, :], a["window"]), (rope_cos[:, :, :], a["rope_cos"]), (rope_sin[:, :, :], a["rope_sin"]),
                  (pair_sum[:, :], a["pair_sum"]), (gate_bias[:, :], a["gate_bias"]), (bias_rows[:, :, :], a["bias_rows"]),
                  (expert_no[:, :], a["expert_no"].partition_broadcast(P)), (g_rows[:, :, :], a["g_rows"].partition_broadcast(P))]
        PARAMS = 16 * len(params)

        block = ctx.enter_context(nc.Block())

        @block.sync
        def _(sp):
            def load(seg, it, j):
                q, k, m, opens, closes, width, source = seg.units[j]
                sp.wait_ge(seg.sig.lo_ready, seg.unit(it, j) - RAW + 1)
                slot = seg.slot(it, j, RAW)
                dst = raw[:, slot, 0:m * width].rearrange("p (c n) -> p c n", c=m)
                sp.dma_start(dst, source(it)).then_inc(seg.sig.raw_loaded[slot], 16)

            def loads(seg):
                if seg.iters > 2:
                    with sp.Fori(0, seg.iters) as it:
                        for j in range(seg.n):
                            load(seg, it, j)
                else:
                    for it in range(seg.iters):
                        for j in range(seg.n):
                            load(seg, it, j)

            for seg in segments:
                if seg.flag is None:
                    loads(seg)
                    continue
                sp.wait_ge(stage_dve, seg.ready)
                most = sp.value_load(seg.flag, min_val=0, max_val=T)
                with sp.If(most > P):
                    sp.wait_ge(seg.before.sig.lo_ready, seg.before.unit(seg.iters, 0))
                    loads(seg)
                    sp.wait_ge(seg.sig.lo_ready, seg.unit(seg.iters, 0))
            sp.wait_ge(at_barrier, 4 * count["barrier"])
            sp.dma_start(out[0].rearrange("(t p) d -> p t d", p=P), x_tm[:, 0:TT, :]).then_inc(stored, 16)
            sp.wait_ge(stored, 16)

        @block.gpsimd
        def _(pool):
            for s, n in STARTS:
                pool.sem_inc(s, n)
            nc.gpsimd.memset(ones[:, :], 1.0)
            nc.gpsimd.memset(eps[:, :], EPS).then_inc(constants_set, 1)
            pool.wait_ge(params_loaded, PARAMS)

            for st in plan:
                if st.kind == "barrier":
                    pool.drain().then_inc(at_barrier, 1)
                    pool.wait_ge(at_barrier, 4 * (st.at["barrier"] + 1))
                elif st.kind == "attend" and st.bias is not None:
                    nbias, l, per_pair = st.bias
                    for pr in range(BC):
                        if pr:
                            pool.wait_ge(scores_done, st.at["item"] + pr * per_pair)
                        pool.dma_start(nbias.rearrange("p h t k -> p (h t) k"),
                                       a["position_bias"][l, 2 * pr:2 * pr + 2].rearrange("h (t p) k -> p (h t) k", p=P))\
                            .then_inc(bias_loaded, 16)
                        pool.wait_ge(bias_loaded, 16 * (st.at["bias"] // 2 + pr + 1))
                        for hh in range(2):
                            nc.gpsimd.tensor_tensor(nbias[:, hh, :, :], nbias[:, hh, :, :], window[:, :, :], ALU.add)\
                                .then_inc(bias_ready, 1)

        @block.scalar
        def _(act):
            steps = [0]

            def settled(ins):
                steps[0] += 1
                ins.then_inc(act_step, 1)
                act.wait_ge(act_step, steps[0])

            for dst, src in params:
                act.dma_start(dst, src).then_inc(params_loaded, 16)
            act.wait_ge(params_loaded, PARAMS)
            act.wait_ge(constants_set, 1)
            silu_c = small[:, 104:104 + 2 * DC].rearrange("p (c s) -> p c s", s=2)
            settled(nc.scalar.activation(silu_c, cols[:, COL_C:COL_C + 2 * DC].rearrange("p (c s) -> p c s", s=2), ACT.Silu))
            nc.scalar.activation(c_split[:, :, 0:2], silu_c, ACT.Copy).then_inc(split_hi_done, 1)

            def split(seg, it, j):
                q, k, m, opens, closes, width, source = seg.units[j]
                n = m * width
                slot, half = seg.slot(it, j, RAW), seg.slot(it, j, HL)
                act.wait_ge(seg.sig.raw_loaded[slot], seg.loaded(it, j))
                act.wait_ge(seg.sig.hi_used, seg.unit(it, j) - HL + 1)
                act.wait_ge(seg.sig.lo_ready, seg.unit(it, j) - HL + 1)
                nc.scalar.activation(w_hi[:, half, 0:n], raw[:, slot, 0:n], ACT.Copy).then_inc(seg.sig.hi_ready, 1)

            def save(seg, it, j):
                q, k, m, opens, closes, width, source = seg.units[j]
                if not closes or seg.evac == "residual":
                    return
                r = seg.result(it, q)
                b = 4 * (q % 2)
                if seg.mode == "ffn" and q >= FB:
                    return
                if seg.evac in ("merge", "experts") and q % 2 and q < seg.down:
                    return
                act.wait_ge(seg.sig.units_used, seg.unit(it, j) + 1)
                if seg.evac == "fm":
                    nc.scalar.activation(seg.dst[:, 2 * q:2 * q + 2, 0:seg.N], ps[:, b:b + 2, 0:seg.N], ACT.Copy,
                                         scale=seg.scale[q]).then_inc(seg.sig.results_saved, 1)
                elif seg.evac == "tm":
                    nc.scalar.activation(seg.dst[:, 0:seg.tiles, q * NT:(q + 1) * NT], ps[:, b:b + seg.tiles, :], ACT.Copy)\
                        .then_inc(seg.sig.results_saved, 1)
                elif seg.evac == "gqa_kv":
                    n = KV * HD
                    nc.scalar.activation(seg.dst[:, :, W_HEADS:W_HEADS + n], ps[:, b:b + seg.tiles, 0:n], ACT.Copy)
                    nc.scalar.activation(seg.vp, ps[:, b:b + seg.tiles, n:2 * n].rearrange("p t (g e) -> p t g e", e=HD), ACT.Copy)\
                        .then_inc(seg.sig.results_saved, 1)
                elif seg.evac == "rows":
                    if seg.bias is None:
                        ins = nc.scalar.activation(seg.dst, ps[0:seg.M, b, 0:seg.N], ACT.Copy)
                    else:
                        ins = nc.scalar.activation(seg.dst, ps[0:seg.M, b, 0:seg.N], ACT.Identity, bias=seg.bias)
                    ins.then_inc(seg.sig.results_saved, 1)
                elif seg.evac == "mod":
                    nc.scalar.activation(seg.dst[0:4, bass.ds(it * (MOD_N * NT) + q * NT, NT)], ps[0:4, b, :], ACT.Copy)\
                        .then_inc(seg.sig.results_saved, 1)
                elif seg.evac == "merge":
                    act.wait_ge(seg.sig.results_saved, r)
                    nc.scalar.activation(seg.gates[:, 0:seg.tiles, :], ps[:, b:b + seg.tiles, :], ACT.Sigmoid)\
                        .then_inc(seg.sig.results_saved, 1)
                elif seg.evac == "experts" and q < DOWN:
                    act.wait_ge(seg.sig.results_saved, r)
                    n = seg.units[j][5]
                    nc.scalar.activation(seg.buf["silu"][:, 0:n], ps[:, b, 0:n], ACT.Silu).then_inc(seg.sig.results_saved, 1)
                elif seg.evac == "experts":
                    act.wait_ge(seg.ex.scattered, 2 * it + (q - DOWN) + (M - 1))
                    act.wait_ge(seg.sig.results_saved, r)
                    nc.scalar.activation(seg.buf["y"][:, q - DOWN, :], ps[:, b, :], ACT.Copy).then_inc(seg.sig.results_saved, 1)
                elif seg.evac == "ml_gate":
                    nc.scalar.activation(seg.gates[:, 0:seg.tiles, :], ps[:, b:b + seg.tiles, :], ACT.Sigmoid)\
                        .then_inc(gate_ready, 1)
                elif seg.evac == "swiglu":
                    done = it * FB + (seg.at["act"] + q)
                    nc.scalar.activation(seg.tmp[:, q % 2, 0:seg.N], ps[:, b, 0:seg.N], ACT.Silu).then_inc(taps_ready, 1)
                elif seg.evac == "conv":
                    for part in range(2):
                        c = it * FB + q + part * (COL_CONV // 2)
                        nc.scalar.activation(seg.tmp[:, 2 * (q % 2) + part, 0:seg.N], ps[:, b + part, 0:seg.N], ACT.Identity,
                                             scale=cols[:, seg.cw + COL_CONV + c:seg.cw + COL_CONV + c + 1],
                                             bias=cols[:, seg.cb + c:seg.cb + c + 1]).then_inc(taps_ready, 1)

            def save_late(seg, it, j):
                q, k, m, opens, closes, width, source = seg.units[j]
                if not closes or seg.mode != "ffn" or q >= FB:
                    return
                r = seg.result(it, q)
                if seg.evac == "swiglu":
                    act.wait_ge(seg.sig.results_saved, r + 1)
                    nc.scalar.activation(act_hi[:, q * seg.N:(q + 1) * seg.N], seg.tmp[:, 2 + q % 2, 0:seg.N], ACT.Copy)\
                        .then_inc(act_hi_done, 1)
                elif seg.evac == "conv":
                    act.wait_ge(seg.sig.results_saved, r + 1)
                    g = seg.tmp[:, 2 * (q % 2) + 1, 0:seg.N]
                    nc.scalar.activation(g, g, ACT.Silu).then_inc(gate_ready, 1)
                    act.wait_ge(act_value, it * FB + q + seg.at["value"] + 1)
                    nc.scalar.activation(act_hi[:, q * seg.N:(q + 1) * seg.N], seg.tmp[:, 2 * (q % 2), 0:seg.N], ACT.Copy)\
                        .then_inc(act_hi_done, 1)

            def upper_half(seg, e, half):
                act.wait_ge(seg.ex.xg_value, 2 * e + (M + half + 1))
                nc.scalar.activation(h_hi[:, 4 * half:4 * half + 4, T:T + P],
                                     turn_value[:, half, :].rearrange("p (c t) -> p c t", t=P), ACT.Copy).then_inc(seg.ex.xg_hi, 1)

            def first_tokens(seg):
                for half in range(2):
                    upper_half(seg, 0, half)

            def between(seg, it, j, first):
                if j == SEL_T + 2:
                    act.wait_ge(seg.ex.selt_turned, it + (M + 1))
                    nc.scalar.activation(seg.buf["sel_t"], ps[:, 5, 0:2 * P], ACT.Copy).then_inc(seg.ex.selt_saved, 1)
                for i, (f, n) in enumerate(GROUPS):
                    if j == TURN[i] + 2:
                        act.wait_ge(seg.ex.act_turned, 3 * it + (M + i + 1))
                        nc.scalar.activation(act_hi[:, f:f + n], ps[:, 3, 0:n], ACT.Copy).then_inc(seg.ex.act_hi_done, 1)
                for half in range(2):
                    if j == GATHER + 3 + half:
                        act.wait_ge(seg.sig.units_used, seg.unit(it, UPS - 1) + 1)
                        upper_half(seg, it + 1, half)

            def stream(seg):
                def body(it, before, first):
                    for j in range(seg.n):
                        if not (first and j == 0):
                            split(seg, it, j)
                        if j:
                            save(seg, it, j - 1)
                        elif not first:
                            save(seg, before, seg.n - 1)
                        if j > 1:
                            save_late(seg, it, j - 2)
                        if seg.mode == "moe":
                            between(seg, it, j, first)

                if seg.first:
                    split(seg, 0, 0)
                if seg.mode == "moe":
                    first_tokens(seg)
                body(0, None, True)
                if seg.iters > 2:
                    with act.Fori(1, seg.iters) as it:
                        body(it, it - 1, False)
                elif seg.iters == 2:
                    body(1, 0, False)
                if seg.next:
                    split(seg.next, 0, 0)
                save(seg, seg.iters - 1, seg.n - 1)

            def root(n, width):
                nc.scalar.activation(small[:, 64:64 + n], small[:, 0:n], ACT.Sqrt, scale=1.0 / width, bias=eps[:, :])\
                    .then_inc(root_done, 1)

            def attend(st):
                k0 = st.at["item"]
                n = len(st.items)

                def weights(i):
                    e, i0 = st.items[i], k0 + i
                    nk = e["nk"]
                    z = ps[:, i0 % 2, 0:nk]
                    if st.mode == "soft":
                        act.wait_ge(max_done, st.at["max"] + i + 1)
                        act.wait_ge(pt_done, i0 - 1)
                        nc.scalar.activation(prob[:, i0 % 2, 0:nk], z, ACT.Exp, bias=small[:, i0 % 2:i0 % 2 + 1],
                                             accum_out=small[:, 2 + i0 % 2:3 + i0 % 2]).then_inc(exp_done, 1)
                    elif st.mode == "stick":
                        e_, e1 = st.tmp[:, 2 + i0 % 2, 0:nk], st.tmp[:, 4 + i0 % 2, 0:nk]
                        act.wait_ge(bounded, st.at["bounded"] + i + 1)
                        act.wait_ge(probs_done, i0 - 1)
                        settled(nc.scalar.activation(e_, st.tmp[:, i0 % 2, 0:nk], ACT.Exp, scale=-1.0))
                        nc.scalar.activation(e1, e_, ACT.Identity, bias=ones[:, 0:1]).then_inc(exp_done, 1)
                    else:
                        act.wait_ge(scores_done, i0 + 1)
                        act.wait_ge(probs_done, i0)
                        for d in range(2):
                            ins = nc.scalar.activation(st.decay[:, d, 0:nk], ps[:, 4 + 2 * (i0 % 2) + d, 0:nk], ACT.Exp,
                                                       bias=st.mcols[:, e["t"], 2 + d, e["h"]:e["h"] + 1])
                        ins.then_inc(exp_done, 1)

                def turned_weights(i):
                    e, i0 = st.items[i], k0 + i
                    act.wait_ge(pt_done, i0 + 1)
                    act.wait_ge(pv_done, i0 - 1)
                    nc.scalar.activation(prob_t[:, i0 % 2, 0:e["nk"]], ps[:, 2 + i0 % 2, 0:e["nk"]], ACT.Copy)\
                        .then_inc(pt_saved, 1)

                def output(i):
                    e, i0 = st.items[i], k0 + i
                    if st.mode == "mlstm":
                        act.wait_ge(pv_done, i0 + 1)
                        nc.scalar.activation(e["dst"], ps[:, 4 + 2 * (i0 % 2), 0:P], ACT.Copy).then_inc(ml_saved, 1)
                    elif e["hh"]:
                        pr, t = e["y"]
                        act.wait_ge(pv_done, i0 + 1)
                        nc.scalar.activation(y_hi[:, pr, t * P:(t + 1) * P], ps[:, 4 + (st.at["pair"] + i // 2) % 2, 0:P],
                                             ACT.Copy).then_inc(y_hi_done, 1)

                if st.mode == "mlstm":
                    for i in range(n + 2):
                        if i >= 2:
                            output(i - 2)
                        if i < n:
                            weights(i)
                        if 1 <= i <= n:
                            turned_weights(i - 1)
                else:
                    for i in range(n + 3):
                        if i < n:
                            weights(i)
                        if 2 <= i <= n + 1:
                            turned_weights(i - 2)
                        if i >= 3:
                            output(i - 3)

            for st in plan:
                if st.kind == "segment":
                    stream(st.seg)
                elif st.kind == "overflow":
                    most = act.value_load(st.seg.flag, min_val=0, max_val=T)
                    with act.If(most > P):
                        stream(st.seg)
                elif st.kind == "barrier":
                    act.drain().then_inc(at_barrier, 1)
                    act.wait_ge(at_barrier, 4 * (st.at["barrier"] + 1))
                elif st.kind == "norm":
                    for t in range(st.tiles):
                        ins = nc.scalar.activation(XN[:, t, :], x_tm[:, t, :], ACT.Square, accum_out=small[:, t:t + 1])
                    settled(ins)
                    root(st.tiles, D)
                elif st.kind == "post":
                    for t in range(st.nq):
                        ins = nc.scalar.activation(merged[:, t, :], st.o[:, t, :], ACT.Square, accum_out=small[:, t:t + 1])
                    settled(ins)
                    root(st.nq, D)
                elif st.kind == "head_norm":
                    act.wait_ge(sums_done, st.at["sum"] + 1)
                    root(st.tiles * st.n, HD)
                elif st.kind == "ml_norm":
                    act.wait_ge(sums_done, st.at["sum"] + 1)
                    root(st.nq * ML_H, ML_D)
                elif st.kind == "turn":
                    for i, (src, gain, shift, hi, lo) in enumerate(st.items):
                        i0 = st.at["turn"] + i
                        act.wait_ge(value_ready, i0 + 1)
                        nc.scalar.activation(hi, turn_value[:, i0 % 2, :].rearrange("p (c t) -> p c t", t=P), ACT.Copy)\
                            .then_inc(split_hi_done, 1)
                elif st.kind == "turn_heads":
                    for i, (src, dst) in enumerate(st.jobs):
                        act.wait_ge(stage_pe, st.at["pe"] + i + 1)
                        nc.scalar.activation(dst, ps[:, i % 4, 0:len(src) * P].rearrange("p (c t) -> p c t", t=P), ACT.Copy)\
                            .then_inc(stage_act, 1)
                elif st.kind == "attend":
                    attend(st)
                elif st.kind == "fox_rows":
                    u, e, sp_ = (st.rows[0:NH, i, 0:T] for i in range(3))
                    settled(nc.scalar.activation(e, u, ACT.Abs))
                    settled(nc.scalar.activation(e, e, ACT.Exp, scale=-1.0))
                    nc.scalar.activation(sp_, e, ACT.Ln, bias=1.0).then_inc(stage_act, 1)
                elif st.kind == "ml_rows":
                    n = 4 * ML_H
                    u, e = st.rows[0:n, 0, :], st.arows[0:n, 0, :]
                    settled(nc.scalar.activation(e, u, ACT.Abs))
                    settled(nc.scalar.activation(e, e, ACT.Exp, scale=-1.0))
                    nc.scalar.activation(e, e, ACT.Ln, bias=1.0).then_inc(stage_act, 1)
                    act.wait_ge(stage_pe, st.at["pe"] + 2)
                    m = ps[:, 4, 0:64].rearrange("p (t k h) -> p t k h", t=2 * TT, k=4)
                    nc.scalar.activation(st.mcols[:, :, 0:2, :], m[:, :, 0:2, :], ACT.Exp, scale=-1.0)
                    nc.scalar.activation(st.mcols[:, :, 2:4, :], m[:, :, 2:4, :], ACT.Copy, scale=-1.0).then_inc(stage_act, 1)
                elif st.kind == "route":
                    act.wait_ge(stage_dve, st.at["d"] + 1)
                    nc.scalar.activation(st.route[:, :, 49:50], st.route[:, :, 48:49], ACT.Exp).then_inc(stage_act, 1)

        @block.vector
        def _(dve):
            steps = [0]

            def settled(ins):
                steps[0] += 1
                ins.then_inc(dve_step, 1)
                dve.wait_ge(dve_step, steps[0])

            dve.wait_ge(params_loaded, PARAMS)
            dve.wait_ge(constants_set, 1)
            dve.wait_ge(split_hi_done, START["turn"] + 1)
            silu_c = small[:, 104:104 + 2 * DC].rearrange("p (c s) -> p c s", s=2)
            settled(nc.vector.tensor_tensor(c_split[:, :, 2:4], silu_c, c_split[:, :, 0:2].bitcast(F32), ALU.subtract))

            def split(seg, it, j):
                q, k, m, opens, closes, width, source = seg.units[j]
                n = m * width
                dve.wait_ge(seg.sig.hi_ready, seg.unit(it, j) + 1)
                dve.wait_ge(seg.sig.units_used, seg.unit(it, j) - HL + 1)
                slot, half = seg.slot(it, j, RAW), seg.slot(it, j, HL)
                nc.vector.tensor_tensor(w_lo[:, half, 0:n], raw[:, slot, 0:n], w_hi[:, half, 0:n].bitcast(F32),
                                        ALU.subtract).then_inc(seg.sig.lo_ready, 1)

            def save(seg, it, j):
                q, k, m, opens, closes, width, source = seg.units[j]
                if not closes or seg.evac in ("fm", "tm", "gqa_kv", "rows", "mod"):
                    return
                r = seg.result(it, q)
                b = 4 * (q % 2)
                if seg.evac == "residual":
                    dve.wait_ge(seg.sig.units_used, seg.unit(it, j) + 1)
                    x = x_tm[:, 0:seg.tiles, q * NT:(q + 1) * NT]
                    nc.vector.tensor_tensor(x, ps[:, b:b + seg.tiles, :], x, ALU.add).then_inc(seg.sig.results_saved, 1)
                elif seg.evac == "merge":
                    if q % 2 == 0:
                        return
                    dve.wait_ge(seg.sig.results_saved, r)
                    dve.wait_ge(seg.sig.units_used, seg.unit(it, j) + 1)
                    dst = merged[:, 0:seg.tiles, (q // 2) * NT:(q // 2 + 1) * NT]
                    g = seg.gates[:, 0:seg.tiles, :]
                    if seg.n_branch == 0:
                        nc.vector.tensor_tensor(dst, ps[:, b:b + seg.tiles, :], g, ALU.mult).then_inc(seg.sig.results_saved, 1)
                    else:
                        settled(nc.vector.tensor_tensor(g, ps[:, b:b + seg.tiles, :], g, ALU.mult))
                        nc.vector.tensor_tensor(dst, dst, g, ALU.add).then_inc(seg.sig.results_saved, 1)
                elif seg.evac == "ml_gate":
                    dve.wait_ge(gate_ready, seg.at["gate"] + 1)
                    nc.vector.tensor_tensor(seg.dst, seg.dst, seg.gates[:, 0:seg.tiles, :]
                                            .rearrange("p t (h e) -> p t h e", e=ML_D), ALU.mult).then_inc(seg.sig.results_saved, 1)
                elif seg.evac == "experts":
                    if q % 2 == 0 or q >= DOWN:
                        return
                    n = seg.units[j][5]
                    dve.wait_ge(seg.sig.results_saved, r)
                    dve.wait_ge(seg.sig.units_used, seg.unit(it, j) + 1)
                    dve.wait_ge(seg.ex.act_turned, 3 * it + (M + q // 2))
                    nc.vector.tensor_tensor(seg.buf["value"][:, 0:n], ps[:, b, 0:n], seg.buf["silu"][:, 0:n], ALU.mult)\
                        .then_inc(seg.sig.results_saved, 1)
                elif q >= FB:
                    dve.wait_ge(seg.sig.units_used, seg.unit(it, j) + 1)
                    half = slice((q - FB) * NT, (q - FB + 1) * NT)
                    src = ps[:, b:b + seg.tiles, :]
                    if seg.evac == "conv":
                        dst = seg.o[:, 0:seg.tiles, half]
                        ins = nc.vector.tensor_copy(dst, src) if it == 0 else nc.vector.tensor_tensor(dst, src, dst, ALU.add)
                    else:
                        dst = x_tm[:, 0:seg.tiles, half]
                        ins = nc.vector.tensor_tensor(dst, src, dst, ALU.add)
                    ins.then_inc(seg.sig.results_saved, 1)
                elif seg.evac == "swiglu":
                    v = seg.tmp[:, 2 + q % 2, 0:seg.N]
                    dve.wait_ge(taps_ready, it * FB + (seg.at["tap"] + q + 1))
                    nc.vector.tensor_tensor(v, ps[:, b + 1, 0:seg.N], seg.tmp[:, q % 2, 0:seg.N], ALU.mult)\
                        .then_inc(seg.sig.results_saved, 1)
                else:
                    for part in range(2):
                        c = it * FB + q + part * (COL_CONV // 2)
                        dve.wait_ge(taps_ready, 2 * (it * FB + q) + seg.at["tap"] + part + 1)
                        src = ps[:, b + part, 0:seg.N].rearrange("p (s t) -> p s t", t=T)
                        u = seg.tmp[:, 2 * (q % 2) + part, 0:seg.N].rearrange("p (s t) -> p s t", t=T)
                        settled(nc.vector.scalar_tensor_tensor(u[:, :, 1:T], src[:, :, 0:T - 1],
                                                               cols[:, seg.cw + c:seg.cw + c + 1], u[:, :, 1:T],
                                                               ALU.mult, ALU.add))
                        ins = nc.vector.scalar_tensor_tensor(u[:, :, 0:T - 1], src[:, :, 1:T],
                                                             cols[:, seg.cw + 2 * COL_CONV + c:seg.cw + 2 * COL_CONV + c + 1],
                                                             u[:, :, 0:T - 1], ALU.mult, ALU.add)
                    ins.then_inc(seg.sig.results_saved, 1)

            def save_late(seg, it, j):
                q, k, m, opens, closes, width, source = seg.units[j]
                if not closes or seg.mode != "ffn" or q >= FB:
                    return
                n = it * FB + (seg.at["act"] + q)
                if seg.evac == "swiglu":
                    v = seg.tmp[:, 2 + q % 2, 0:seg.N]
                    dve.wait_ge(act_hi_done, n + 1)
                    nc.vector.tensor_tensor(act_lo[:, q * seg.N:(q + 1) * seg.N], v,
                                            act_hi[:, q * seg.N:(q + 1) * seg.N].bitcast(F32), ALU.subtract)\
                        .then_inc(act_done, 1)
                else:
                    dve.wait_ge(gate_ready, it * FB + q + seg.at["gate"] + 1)
                    v, g = seg.tmp[:, 2 * (q % 2), 0:seg.N], seg.tmp[:, 2 * (q % 2) + 1, 0:seg.N]
                    nc.vector.tensor_tensor(v, v, g, ALU.mult).then_inc(act_value, 1)
                    dve.wait_ge(act_hi_done, n + 1)
                    nc.vector.tensor_tensor(act_lo[:, q * seg.N:(q + 1) * seg.N], v,
                                            act_hi[:, q * seg.N:(q + 1) * seg.N].bitcast(F32), ALU.subtract)\
                        .then_inc(act_done, 1)

            def select(seg, e):
                dve.wait_ge(seg.ex.selt_turned, e + M)
                for t in range(TT):
                    ins = nc.vector.tensor_scalar(seg.buf["sel"][:, t, :], seg.buf["slot_no"][:, seg.half * P:(seg.half + 1) * P],
                                                  seg.route[:, t, bass.ds(e + PLACE, 1)], seg.route[:, t, bass.ds(e + TAKES, 1)],
                                                  ALU.is_equal, ALU.mult)
                ins.then_inc(seg.ex.sel_ready, 1)

            def gain(seg, e, half):
                dve.wait_ge(seg.ex.gathered, 2 * e + (M + half + 1))
                dve.wait_ge(seg.ex.xg_hi, 2 * e + (M + half - 1))
                dve.wait_ge(seg.ex.xg_done, 2 * e + (M + half - 1))
                nc.vector.tensor_tensor(turn_value[:, half, :].rearrange("p (c t) -> p c t", t=P),
                                        ps[:, 1 + half, :].rearrange("p (c t) -> p c t", t=P),
                                        seg.scale[:, 4 * half:4 * half + 4].unsqueeze(2).to_broadcast([P, 4, P]), ALU.mult)\
                    .then_inc(seg.ex.xg_value, 1)

            def lower_half(seg, e, half):
                dve.wait_ge(seg.ex.xg_hi, 2 * e + (M + half + 1))
                nc.vector.tensor_tensor(h_lo[:, 4 * half:4 * half + 4, T:T + P],
                                        turn_value[:, half, :].rearrange("p (c t) -> p c t", t=P),
                                        h_hi[:, 4 * half:4 * half + 4, T:T + P].bitcast(F32), ALU.subtract)\
                    .then_inc(seg.ex.xg_done, 1)

            def first_tokens(seg):
                select(seg, 0)
                for half in range(2):
                    gain(seg, 0, half)
                for half in range(2):
                    lower_half(seg, 0, half)

            def accumulate(seg, e, half):
                dve.wait_ge(seg.ex.scattered, 2 * e + (M + half + 1))
                dve.wait_ge(seg.ex.accumulated, 2 * e + (M + half))
                for t in range(TT):
                    dst = x_tm[:, t, half * NT:(half + 1) * NT]
                    ins = nc.vector.scalar_tensor_tensor(dst, ps[:, 6 + t, :], seg.route[:, t, bass.ds(e, 1)], dst, ALU.mult, ALU.add)
                ins.then_inc(seg.ex.accumulated, 1)

            def between(seg, it, j, first):
                if j == SCATTER[1] + 2 and not first:
                    accumulate(seg, it - 1, 1)
                for i, (f, n) in enumerate(GROUPS):
                    if j == TURN[i] + 2:
                        dve.wait_ge(seg.ex.act_hi_done, 3 * it + (M + i + 1))
                        nc.vector.tensor_tensor(act_lo[:, f:f + n], ps[:, 3, 0:n], act_hi[:, f:f + n].bitcast(F32), ALU.subtract)\
                            .then_inc(seg.ex.act_done, 1)
                if j == GATHER - 4:
                    select(seg, it + 1)
                for half in range(2):
                    if j == GATHER + 2 + half:
                        gain(seg, it + 1, half)
                    if j == GATHER + 4 + half:
                        lower_half(seg, it + 1, half)
                if j == SCATTER[0] + 2:
                    accumulate(seg, it, 0)

            def stream(seg):
                def body(it, before, first):
                    for j in range(seg.n):
                        if not (first and j == 0):
                            split(seg, it, j)
                        if j:
                            save(seg, it, j - 1)
                        elif not first:
                            save(seg, before, seg.n - 1)
                        if j > 1:
                            save_late(seg, it, j - 2)
                        if seg.mode == "moe":
                            between(seg, it, j, first)

                if seg.first:
                    split(seg, 0, 0)
                if seg.mode == "moe":
                    first_tokens(seg)
                body(0, None, True)
                if seg.iters > 2:
                    with dve.Fori(1, seg.iters) as it:
                        body(it, it - 1, False)
                elif seg.iters == 2:
                    body(1, 0, False)
                if seg.next:
                    split(seg.next, 0, 0)
                save(seg, seg.iters - 1, seg.n - 1)
                if seg.mode == "moe":
                    accumulate(seg, seg.iters - 1, 1)

            def attend(st):
                k0 = st.at["item"]
                n = len(st.items)

                def begin(i):
                    e, i0 = st.items[i], k0 + i
                    nk = e["nk"]
                    z = ps[:, i0 % 2, 0:nk]
                    if st.mode == "soft":
                        dve.wait_ge(scores_done, i0 + 1)
                        dve.wait_ge(exp_done, i0 - 1)
                        nc.vector.tensor_reduce(small[:, i0 % 2:i0 % 2 + 1], z, AX.X, ALU.max, negate=True).then_inc(max_done, 1)
                    elif st.mode == "stick":
                        dve.wait_ge(scores_done, i0 + 1)
                        dve.wait_ge(exp_done, i0 - 1)
                        nc.vector.scalar_tensor_tensor(st.tmp[:, i0 % 2, 0:nk], z, -BOUND, e["cap"], ALU.max, ALU.min)\
                            .then_inc(bounded, 1)

                def finish(i):
                    e, i0 = st.items[i], k0 + i
                    nk = e["nk"]
                    w = prob[:, i0 % 2, 0:nk]
                    dve.wait_ge(exp_done, i0 + 1)
                    if st.mode == "soft":
                        inv = small[:, 4 + i0 % 2:5 + i0 % 2]
                        settled(nc.vector.reciprocal(inv, small[:, 2 + i0 % 2:3 + i0 % 2]))
                        nc.vector.tensor_scalar(w, w, inv, None, ALU.mult).then_inc(probs_done, 1)
                    elif st.mode == "stick":
                        keep, beta = st.tmp[:, 2 + i0 % 2, 0:nk], st.tmp[:, 4 + i0 % 2, 0:nk]
                        tail = st.tmp[:, 6:8, :].rearrange("p a b -> p (a b)")[:, T - nk:T + 1]
                        settled(nc.vector.reciprocal(beta, beta))
                        settled(nc.vector.tensor_tensor(keep, keep, beta, ALU.mult))
                        settled(nc.vector.tensor_tensor_scan(tail[:, 0:nk][:, ::-1], keep[:, ::-1],
                                                             ones[:, 0:1].to_broadcast([P, nk]), 1.0, ALU.mult, ALU.mult))
                        dve.wait_ge(pt_done, i0 - 1)
                        nc.vector.tensor_tensor(w, beta, tail[:, 1:nk + 1], ALU.mult).then_inc(probs_done, 1)
                    else:
                        z = ps[:, i0 % 2, 0:nk]
                        den, inv = small[:, 0:2], small[:, 4:6]
                        for d in range(2):
                            s = st.decay[:, d, 0:nk]
                            settled(nc.vector.scalar_tensor_tensor(s, z, 1.0, s, ALU.mult, ALU.mult, accum_out=den[:, d:d + 1]))
                        settled(nc.vector.scalar_tensor_tensor(inv, den, -1.0, den, ALU.mult, ALU.max))
                        settled(nc.vector.tensor_tensor(inv, inv, st.mcols[:, e["t"], 0:2, e["h"]], ALU.max))
                        settled(nc.vector.reciprocal(inv, inv))
                        s = st.decay[:, 0, 0:nk]
                        settled(nc.vector.tensor_scalar(s, s, inv[:, 0:1], None, ALU.mult))
                        dve.wait_ge(pt_done, i0 - 1)
                        nc.vector.scalar_tensor_tensor(w, st.decay[:, 1, 0:nk], inv[:, 1:2], s, ALU.mult, ALU.add)\
                            .then_inc(probs_done, 1)

                def output(i):
                    e, i0 = st.items[i], k0 + i
                    if st.mode != "mlstm" and e["hh"]:
                        pr, t = e["y"]
                        pair = st.at["pair"] + i // 2
                        dve.wait_ge(y_hi_done, pair + 1)
                        nc.vector.tensor_tensor(y_lo[:, pr, t * P:(t + 1) * P], ps[:, 4 + pair % 2, 0:P],
                                                y_hi[:, pr, t * P:(t + 1) * P].bitcast(F32), ALU.subtract).then_inc(y_saved, 1)

                if st.mode == "stick":
                    settled(nc.vector.memset(st.tmp[:, 7, 0:1], 1.0))
                for i in range(n + 3):
                    if i < n:
                        begin(i)
                    if st.mode == "mlstm" and i < n:
                        finish(i)
                    if st.mode != "mlstm" and 1 <= i <= n:
                        finish(i - 1)
                    if i >= 3:
                        output(i - 3)

            def inverse_root(st, n):
                dve.wait_ge(root_done, st.at["root"] + 1)
                settled(nc.vector.reciprocal(small[:, 64:64 + n], small[:, 64:64 + n]))

            def head_norm(st):
                t, n = st.tiles, st.n
                x = st.src.rearrange("p t (h d) -> p (t h) d", d=HD)
                settled(nc.vector.tensor_tensor(st.sq, st.src, st.src, ALU.mult))
                nc.vector.tensor_reduce(small[:, 0:t * n], st.sq.rearrange("p t (h d) -> p (t h) d", d=HD), AX.X, ALU.add)\
                    .then_inc(sums_done, 1)
                inverse_root(st, t * n)
                settled(nc.vector.tensor_tensor(x, x, small[:, 64:64 + t * n].unsqueeze(2).to_broadcast([P, t * n, HD]), ALU.mult))
                for i in range(t):
                    heads = st.src[:, i, :].rearrange("p (h d) -> p h d", d=HD)
                    for h0, h1, g, scale in st.parts:
                        part = heads[:, h0:h1, :]
                        ins = nc.vector.scalar_tensor_tensor(part, part, scale, g_rows[:, g:g + 1, :].to_broadcast([P, h1 - h0, HD]),
                                                             ALU.mult, ALU.mult)
                settled(ins)
                if not st.rope:
                    return
                rot = st.sq
                for i in range(TT):
                    heads = st.src[:, i, :].rearrange("p (h d) -> p h d", d=HD)
                    quarters = st.src[:, i, :].rearrange("p (h r s e) -> p h r s e", h=n, r=2, s=2)
                    out_q = rot[:, i, :].rearrange("p (h r s e) -> p h r s e", h=n, r=2, s=2)
                    sin_q = rope_sin[:, i:i + 1, :].rearrange("p o (r s e) -> p o r s e", r=2, s=2)
                    for s in range(2):
                        ins = nc.vector.tensor_tensor(out_q[:, :, :, s, :], quarters[:, :, :, 1 - s, :],
                                                      sin_q[:, :, :, s, :].to_broadcast([P, n, 2, HD // 4]), ALU.mult)
                    settled(ins)
                    settled(nc.vector.tensor_tensor(heads, heads, rope_cos[:, i:i + 1, :].to_broadcast([P, n, HD]), ALU.mult))
                    settled(nc.vector.tensor_tensor(st.src[:, i, :], st.src[:, i, :], rot[:, i, :], ALU.add))
                for side in range(2):
                    nc.vector.tensor_copy(st.kd[:, :, :, side, :],
                                          st.src[:, :, W_HEADS:].rearrange("p t (g d) -> p t g d", d=HD))

            def ml_rows(st):
                n = 4 * ML_H
                u, l, lf = st.rows[0:n, 0, :], st.arows[0:n, 0, :], st.rows[0:n, 1, :]
                dve.wait_ge(stage_act, st.at["a"] + 1)
                nc.vector.scalar_tensor_tensor(lf, u, 0.0, l, ALU.min, ALU.subtract).then_inc(stage_dve, 1)
                dve.wait_ge(stage_pe, st.at["pe"] + 1)
                one = ones[0:ML_H, 0:1].to_broadcast([ML_H, T])
                for d in range(2):
                    ig, fg = ps[0:ML_H, 2 * d, :], ps[0:ML_H, 2 * d + 1, :]
                    b, m, av = st.d[0:ML_H, d, :], st.d[0:ML_H, 2 + d, :], st.arows[0:ML_H, d, :]
                    ctx_, x_ = (slice(T, 2 * T), slice(0, T))
                    step = -1 if d else 1
                    carry = slice(T, T + 1) if d else slice(2 * T - 1, 2 * T)
                    settled(nc.vector.tensor_tensor_scan(b[:, ctx_][:, ::step], one, fg[:, ctx_][:, ::step], 0.0,
                                                         ALU.mult, ALU.add))
                    settled(nc.vector.tensor_tensor_scan(b[:, x_][:, ::step], one, fg[:, x_][:, ::step], b[:, carry],
                                                         ALU.mult, ALU.add))
                    settled(nc.vector.tensor_tensor(av, ig, b, ALU.subtract))
                    settled(nc.vector.tensor_tensor_scan(m[:, ctx_][:, ::step], av[:, ctx_][:, ::step], av[:, ctx_][:, ::step],
                                                         0.0, ALU.max, ALU.max))
                    settled(nc.vector.tensor_tensor_scan(m[:, x_][:, ::step], av[:, x_][:, ::step], av[:, x_][:, ::step],
                                                         m[:, carry], ALU.max, ALU.max))
                    ins = nc.vector.tensor_tensor(b, b, m, ALU.add)
                ins.then_inc(stage_dve, 1)

            def route(st):
                r = st.route
                dve.wait_ge(stage_pe, st.at["pe"] + 1)
                settled(nc.vector.tensor_copy(r[:, :, 16:24], ps[:, 0, 0:TT * N_EXP].rearrange("p (t e) -> p t e", e=N_EXP)))
                for t in range(TT):
                    settled(nc.vector.max(r[:, t, 24:32], r[:, t, 16:24]))
                    settled(nc.vector.max_index(r[:, t, 32:40].bitcast(U32), r[:, t, 24:32], r[:, t, 16:24]))
                    settled(nc.vector.tensor_copy(r[:, t, 40:48], r[:, t, 32:40].bitcast(U32)))
                nc.vector.tensor_tensor(r[:, :, 48:49], r[:, :, 25:26], r[:, :, 24:25], ALU.subtract).then_inc(stage_dve, 1)
                dve.wait_ge(stage_act, st.at["a"] + 1)
                settled(nc.vector.tensor_scalar(r[:, :, 50:51], r[:, :, 49:50], 1.0, None, ALU.add))
                settled(nc.vector.reciprocal(r[:, :, 50:51], r[:, :, 50:51]))
                settled(nc.vector.tensor_tensor(r[:, :, 51:52], r[:, :, 49:50], r[:, :, 50:51], ALU.mult))
                settled(nc.vector.memset(r[:, :, PLACE:PLACE + 32], 0.0))
                for t in range(TT):
                    for c in range(2):
                        nc.vector.tensor_scalar(r[:, t, 8 * c:8 * c + 8], expert_no[:, :], r[:, t, 40 + c:41 + c],
                                                r[:, t, 50 + c:51 + c], ALU.is_equal, ALU.mult)
                        ins = nc.vector.tensor_scalar(r[:, t, 16 + 8 * c:24 + 8 * c], expert_no[:, :], r[:, t, 40 + c:41 + c], None,
                                                      ALU.is_equal)
                settled(ins)
                nc.vector.tensor_tensor(r[:, :, TAKES:TAKES + 8], r[:, :, 16:24], r[:, :, 24:32], ALU.add)
                settled(nc.vector.tensor_tensor(r[:, :, 0:8], r[:, :, 0:8], r[:, :, 8:16], ALU.add))
                nc.vector.tensor_scalar(st.buf["upto"], anti[:, 0, 0:P], 0.0, None, ALU.is_equal)
                settled(nc.vector.memset(st.buf["sel"], 1.0))
                nc.vector.tensor_tensor_scan(st.buf["slot_no"], st.buf["sel"].rearrange("p t n -> p (t n)"),
                                             st.buf["sel"].rearrange("p t n -> p (t n)"), 0.0, ALU.mult, ALU.add)\
                    .then_inc(stage_dve, 1)
                dve.wait_ge(stage_pe, st.at["pe"] + 2)
                nc.vector.tensor_copy(r[:, :, PLACE:PLACE + 8], ps[:, 1, 0:TT * N_EXP].rearrange("p (t e) -> p t e", e=N_EXP))
                settled(nc.vector.tensor_reduce(r[0:1, 0, 48:49], ps[0:1, 2, 0:N_EXP], AX.X, ALU.max))
                nc.vector.tensor_copy(st.buf["flag"], r[0:1, 0, 48:49]).then_inc(stage_dve, 1)

            def mod_cols(st):
                dve.wait_ge(stage_pe, st.at["pe"] + 1)
                n = MOD_W // P
                bc = col_second(st.l, "b_mod")
                settled(nc.vector.tensor_tensor(mod[:, :, :], ps[:, 0, 0:2 * n].rearrange("p (b s) -> p b s", s=2),
                                                cols[:, bc:bc + n].unsqueeze(2).to_broadcast([P, n, 2]), ALU.add))
                for i, (pre, post) in enumerate((("g_pre_mix", "g_post_mix"), ("g_pre_ffn", "g_post_ffn"))):
                    at = 3 * i * DC
                    g = cols[:, col_second(st.l, pre):][:, 0:DC].unsqueeze(2).to_broadcast([P, DC, 2])
                    nc.vector.scalar_tensor_tensor(mod_gain[:, i, :, :], mod[:, at + DC:at + 2 * DC, :], 1.0, g, ALU.add, ALU.mult)
                    g = cols[:, col_second(st.l, post):][:, 0:DC].unsqueeze(2).to_broadcast([P, DC, 2])
                    nc.vector.tensor_tensor(mod_post[:, i, :, :], mod[:, at + 2 * DC:at + 3 * DC, :], g, ALU.mult)

            def post(st):
                for s in range(2):
                    for c in range(DC):
                        ins = nc.vector.tensor_scalar(st.diag[:, s, c, :], ident[:, :], mod_post[:, st.which, c, s:s + 1], None,
                                                      ALU.mult)
                ins.then_inc(stage_dve, 1)
                dve.wait_ge(stage_pe, st.at["pe"] + 1)
                inverse_root(st, st.nq)
                for t in range(st.nq):
                    s = t // TT
                    gain = ps[:, 2 * s:2 * s + 2, :].rearrange("p b n -> p (b n)")
                    settled(nc.vector.scalar_tensor_tensor(st.o[:, t, :], st.o[:, t, :], small[:, 64 + t:65 + t], gain,
                                                           ALU.mult, ALU.mult))
                    nc.vector.tensor_tensor(x_tm[:, t, :], x_tm[:, t, :], st.o[:, t, :], ALU.add)

            def ml_norm(st):
                n = ML_H * st.nq
                settled(nc.vector.tensor_tensor(st.sq, st.mh, st.mh, ALU.mult))
                nc.vector.tensor_reduce(small[:, 0:n], st.sq.rearrange("p h t e -> p (h t) e"), AX.X, ALU.add).then_inc(sums_done, 1)
                inverse_root(st, n)
                rs = small[:, 64:64 + n].rearrange("p (h t) -> p h t", t=st.nq).unsqueeze(3).to_broadcast([P, ML_H, st.nq, ML_D])
                nc.vector.tensor_tensor(st.mh, st.mh, rs, ALU.mult)

            for st in plan:
                if st.kind == "segment":
                    stream(st.seg)
                elif st.kind == "overflow":
                    most = dve.value_load(st.seg.flag, min_val=0, max_val=T)
                    with dve.If(most > P):
                        stream(st.seg)
                elif st.kind == "barrier":
                    dve.drain().then_inc(at_barrier, 1)
                    dve.wait_ge(at_barrier, 4 * (st.at["barrier"] + 1))
                elif st.kind == "norm":
                    inverse_root(st, st.tiles)
                    for t in range(st.tiles):
                        nc.vector.tensor_scalar(XN[:, t, :], x_tm[:, t, :], small[:, 64 + t:65 + t], None, ALU.mult)
                elif st.kind == "turn":
                    def value(i):
                        src, gain, shift, hi, lo = st.items[i]
                        i0 = st.at["turn"] + i
                        v = turn_value[:, i0 % 2, :].rearrange("p (c t) -> p c t", t=P)
                        t_ = ps[:, i0 % 4, :].rearrange("p (c t) -> p c t", t=P)
                        dve.wait_ge(turned, i0 + 1)
                        dve.wait_ge(split_done, i0 - 1)
                        if gain is None:
                            ins = nc.vector.tensor_copy(v, t_)
                        else:
                            ins = nc.vector.tensor_tensor(v, t_, gain.unsqueeze(2).to_broadcast([P, 4, P]), ALU.mult)
                            if shift is not None:
                                settled(ins)
                                ins = nc.vector.tensor_tensor(v, v, shift.unsqueeze(2).to_broadcast([P, 4, P]), ALU.add)
                        ins.then_inc(value_ready, 1)

                    def lower(i):
                        src, gain, shift, hi, lo = st.items[i]
                        i0 = st.at["turn"] + i
                        dve.wait_ge(split_hi_done, i0 + 2)
                        nc.vector.tensor_tensor(lo, turn_value[:, i0 % 2, :].rearrange("p (c t) -> p c t", t=P),
                                                hi.bitcast(F32), ALU.subtract).then_inc(split_done, 1)

                    for i in range(len(st.items) + 1):
                        if i < len(st.items):
                            value(i)
                        if i:
                            lower(i - 1)
                elif st.kind == "attend":
                    attend(st)
                elif st.kind == "fox_rows":
                    u, lf, l, neg = (st.rows[0:NH, i, 0:T] for i in range(4))
                    dve.wait_ge(stage_act, st.at["a"] + 1)
                    settled(nc.vector.scalar_tensor_tensor(lf, u, 0.0, l, ALU.min, ALU.subtract))
                    settled(nc.vector.tensor_tensor_scan(l, ones[0:NH, 0:1].to_broadcast([NH, T]), lf, 0.0, ALU.mult, ALU.add))
                    nc.vector.tensor_scalar(neg, l, -1.0, None, ALU.mult)
                elif st.kind in ("head_norm", "ml_rows", "route", "mod_cols", "post", "ml_norm"):
                    {"head_norm": head_norm, "ml_rows": ml_rows, "route": route, "mod_cols": mod_cols, "post": post,
                     "ml_norm": ml_norm}[st.kind](st)

        @block.tensor
        def _(pe):
            pe.wait_ge(params_loaded, PARAMS)
            pe.wait_ge(constants_set, 1)
            mm = nc.tensor.matmul

            def use(seg, it, j):
                q, k, m, opens, closes, width, source = seg.units[j]
                b = 4 * (q % 2)
                if opens:
                    pe.wait_ge(seg.sig.results_saved, seg.result(it, q) - (1 if q or seg.results % 2 == 0 else 0))
                if seg.mode == "moe" and q == 0 and opens:
                    pe.wait_ge(seg.ex.xg_done, 2 * it + (M + 2))
                if seg.mode == "moe" and q == DOWN:
                    pe.wait_ge(seg.ex.act_done, 3 * it + (M + (k + m + 3) // 4))
                if seg.mode == "ffn" and q == FB:
                    pe.wait_ge(act_done, it * FB + (seg.at["act"] + k + m))
                pe.wait_ge(seg.sig.hi_ready, seg.unit(it, j) + 1)
                half = seg.slot(it, j, HL)
                wh, wl = w_hi[:, half, :], w_lo[:, half, :]
                for w in (wh, wl):
                    upper = w is wh
                    if not upper:
                        ins.then_inc(seg.sig.hi_used, 1)
                        pe.wait_ge(seg.sig.lo_ready, seg.unit(it, j) + 1)
                    if seg.mode == "mod":
                        for c in range(m):
                            ins = mm(ps[0:4, b, :], c_split[:, k + c, :], w[:, c * width:(c + 1) * width],
                                     start=upper and opens and c == 0, stop=not upper and closes and c == m - 1)
                    elif seg.mode == "fm" or (seg.mode == "ffn" and q < FB):
                        ah, al = seg.A
                        wide = min(width, P)
                        for f in range(width // wide):
                            bank = b + f if seg.mode == "fm" else b + (0 if opens else 1)
                            dst = ps[0:wide, bank, 0:seg.N]
                            for c in range(m):
                                f0 = c * width + f * P
                                for x in ((ah, al) if upper else (ah,)):
                                    ins = mm(dst, w[:, f0:f0 + wide], x[:, k + c, 0:seg.N], start=upper and k + c == 0 and x is ah,
                                             stop=not upper and k + c == DC - 1)
                    else:
                        branch = seg.evac == "merge" and q % 2
                        biased = seg.evac == "merge" and not branch and seg.bias_layer is not None
                        for t in range(seg.tiles):
                            dst = ps[:, b + t, 0:width]
                            for c in range(m):
                                if q >= seg.down:
                                    at = (k + c) * seg.N + t * P
                                    xh, xl = act_hi[:, at:at + P], act_lo[:, at:at + P]
                                else:
                                    ah, al = seg.B if branch else seg.A
                                    xh, xl = ah[:, k + c, t * P:(t + 1) * P], al[:, k + c, t * P:(t + 1) * P]
                                last = not upper and closes and c == m - 1
                                for x in ((xh, xl) if upper else (xh,)):
                                    ins = mm(dst, x, w[:, c * width:(c + 1) * width], start=upper and opens and c == 0 and x is xh,
                                             stop=last and not biased)
                                if last and biased:
                                    row = 2 * seg.n_branch + q // 2
                                    ins = mm(dst, row_of[0:4, row, :], bias_rows[0:4, seg.bias_layer, :], start=False, stop=True)
                ins.then_inc(seg.sig.units_used, 1)

            def gather(seg, e, half):
                pe.wait_ge(seg.ex.sel_ready, e + (M + 1))
                pe.wait_ge(seg.ex.xg_value, 2 * e + (M + half - 1))
                for c in range(4):
                    d0 = (4 * half + c) * P
                    for t in range(TT):
                        ins = mm(ps[:, 1 + half, c * P:(c + 1) * P], seg.buf["tokens"][:, t, d0:d0 + P], seg.buf["sel"][:, t, :],
                                 start=t == 0, stop=t == TT - 1)
                ins.then_inc(seg.ex.gathered, 1)

            def scatter(seg, e, half):
                pe.wait_ge(seg.sig.results_saved, seg.result(e, DOWN + half) + 1)
                pe.wait_ge(seg.ex.selt_saved, e + (M + 1))
                pe.wait_ge(seg.ex.accumulated, 2 * e + (M + half))
                for t in range(TT):
                    ins = mm(ps[:, 6 + t, :], seg.buf["sel_t"][:, t * P:(t + 1) * P], seg.buf["y"][:, half, :], start=True, stop=True)
                ins.then_inc(seg.ex.scattered, 1)

            def between(seg, it, j, first):
                if j == SCATTER[1] and not first:
                    scatter(seg, it - 1, 1)
                if j == SEL_T:
                    pe.wait_ge(seg.ex.selt_saved, it + M)
                    for t in range(TT):
                        ins = nc.tensor.transpose(ps[:, 5, t * P:(t + 1) * P], seg.buf["sel"][:, t, :], ident[:, :])
                    ins.then_inc(seg.ex.selt_turned, 1)
                for i, (f, n) in enumerate(GROUPS):
                    if j == TURN[i]:
                        pe.wait_ge(seg.sig.results_saved, seg.result(it, 2 * i + 1) + 1)
                        pe.wait_ge(seg.ex.act_done, 3 * it + (M + i))
                        for c in range(n // P):
                            ins = nc.tensor.transpose(ps[:, 3, c * P:(c + 1) * P], seg.buf["value"][:, c * P:(c + 1) * P], ident[:, :])
                        ins.then_inc(seg.ex.act_turned, 1)
                for half in range(2):
                    if j == GATHER + half:
                        gather(seg, it + 1, half)
                if j == SCATTER[0]:
                    scatter(seg, it, 0)

            def stream(seg):
                def body(it, first):
                    for j in range(seg.n):
                        use(seg, it, j)
                        if seg.mode == "moe":
                            between(seg, it, j, first)

                if seg.mode == "moe":
                    for half in range(2):
                        gather(seg, 0, half)
                body(0, True)
                if seg.iters > 2:
                    with pe.Fori(1, seg.iters) as it:
                        body(it, False)
                elif seg.iters == 2:
                    body(1, False)
                if seg.mode == "moe":
                    scatter(seg, seg.iters - 1, 1)

            def attend(st):
                k0 = st.at["item"]
                n = len(st.items)

                def scores(i):
                    e, i0 = st.items[i], k0 + i
                    nk = e["nk"]
                    if st.mode == "mlstm":
                        pe.wait_ge(probs_done, i0 - 1)
                        pe.wait_ge(ml_saved, st.at["ml"] + i - 1)
                        for d in range(2):
                            dst = ps[:, 4 + 2 * (i0 % 2) + d, :]
                            row = row_of[0:ML_H, e["h"], :]
                            mm(dst[:, 0:T], row, st.arows[0:ML_H, d, e["k0"]:e["k0"] + T], start=True, stop=False)
                            mm(dst[:, 0:T], ident[:, :], e["masks"][d], start=False, stop=True)
                            if nk > T:
                                mm(dst[:, T:nk], row, st.arows[0:ML_H, d, T:2 * T], start=True, stop=True)
                        mm(ps[:, i0 % 2, 0:nk], e["q"], e["k"], start=True, stop=True).then_inc(scores_done, 1)
                        return
                    pe.wait_ge(exp_done, i0 - 1)
                    n_add = T if e["add"] and nk > T else nk
                    ins = mm(ps[:, i0 % 2, 0:n_add], e["q"], e["k"][:, 0:n_add], start=True, stop=not e["add"])
                    for j, (lhs, rhs, ready) in enumerate(e["add"]):
                        if ready is not None:
                            pe.wait_ge(bias_ready, ready)
                        ins = mm(ps[:, i0 % 2, 0:n_add], lhs, rhs, start=False, stop=j == len(e["add"]) - 1)
                    if n_add < nk:
                        ins = mm(ps[:, i0 % 2, n_add:nk], e["q"], e["k"][:, n_add:nk], start=True, stop=True)
                    ins.then_inc(scores_done, 1)

                def turn(i):
                    e, i0 = st.items[i], k0 + i
                    pe.wait_ge(probs_done, i0 + 1)
                    pe.wait_ge(pt_saved, i0 - 1)
                    for c in range(e["nk"] // P):
                        ins = nc.tensor.transpose(ps[:, 2 + i0 % 2, c * P:(c + 1) * P], prob[:, i0 % 2, c * P:(c + 1) * P],
                                                  ident[:, :])
                    ins.then_inc(pt_done, 1)

                def gather(i):
                    e, i0 = st.items[i], k0 + i
                    chunks = e["nk"] // P
                    pe.wait_ge(pt_saved, i0 + 1)
                    if st.mode == "mlstm":
                        for c in range(chunks):
                            ins = mm(ps[:, 4 + 2 * (i0 % 2), 0:P], prob_t[:, i0 % 2, c * P:(c + 1) * P], e["v"][c],
                                     start=c == 0, stop=c == chunks - 1)
                    else:
                        pair = st.at["pair"] + i // 2
                        if not e["hh"]:
                            pe.wait_ge(y_saved, pair - 1)
                        for c in range(chunks):
                            ins = mm(ps[e["hh"] * HD:(e["hh"] + 1) * HD, 4 + pair % 2, 0:P], e["v"][c],
                                     prob_t[:, i0 % 2, c * P:(c + 1) * P], start=c == 0, stop=c == chunks - 1)
                    ins.then_inc(pv_done, 1)

                if st.mode == "mlstm":
                    for i in range(n + 2):
                        if i >= 2:
                            gather(i - 2)
                        if i < n:
                            scores(i)
                        if 1 <= i <= n:
                            turn(i - 1)
                else:
                    for i in range(n + 3):
                        if i < n:
                            scores(i)
                        if 2 <= i <= n + 1:
                            turn(i - 2)
                        if i >= 3:
                            gather(i - 3)

            for st in plan:
                if st.kind == "segment":
                    stream(st.seg)
                elif st.kind == "overflow":
                    most = pe.value_load(st.seg.flag, min_val=0, max_val=T)
                    with pe.If(most > P):
                        stream(st.seg)
                elif st.kind == "barrier":
                    pe.drain().then_inc(at_barrier, 1)
                    pe.wait_ge(at_barrier, 4 * (st.at["barrier"] + 1))
                elif st.kind == "turn":
                    for i, (src, gain, shift, hi, lo) in enumerate(st.items):
                        i0 = st.at["turn"] + i
                        pe.wait_ge(value_ready, i0 - 3)
                        for c in range(4):
                            ins = nc.tensor.transpose(ps[:, i0 % 4, c * P:(c + 1) * P], src[c], ident[:, :])
                        ins.then_inc(turned, 1)
                elif st.kind == "turn_heads":
                    for i, (src, dst) in enumerate(st.jobs):
                        if i >= 4:
                            pe.wait_ge(stage_act, st.at["a"] + i - 3)
                        for c, s in enumerate(src):
                            ins = nc.tensor.transpose(ps[:, i % 4, c * P:(c + 1) * P], s, ident[:, :])
                        ins.then_inc(stage_pe, 1)
                elif st.kind == "attend":
                    attend(st)
                elif st.kind == "ml_rows":
                    n = 4 * ML_H
                    pe.wait_ge(stage_dve, st.at["d"] + 1)
                    for kind in range(4):
                        ins = mm(ps[0:ML_H, kind, :], ident[0:n, kind * ML_H:(kind + 1) * ML_H], st.rows[0:n, kind % 2, :],
                                 start=True, stop=True)
                    ins.then_inc(stage_pe, 1)
                    pe.wait_ge(stage_dve, st.at["d"] + 2)
                    for t in range(2 * TT):
                        for kind in range(4):
                            at = (t * 4 + kind) * ML_H
                            ins = nc.tensor.transpose(ps[:, 4, at:at + ML_H], st.d[0:ML_H, kind, t * P:(t + 1) * P],
                                                      ident[0:ML_H, 0:ML_H])
                    ins.then_inc(stage_pe, 1)
                elif st.kind == "route":
                    for t in range(TT):
                        ins = nc.tensor.transpose(ps[:, 0, t * N_EXP:(t + 1) * N_EXP], st.logits[:, t * P:(t + 1) * P],
                                                  ident[0:N_EXP, 0:N_EXP])
                    ins.then_inc(stage_pe, 1)
                    pe.wait_ge(stage_dve, st.at["d"] + 2)
                    takes = [st.route[:, t, TAKES:TAKES + N_EXP] for t in range(TT)]
                    for t in range(TT):
                        for before in range(t):
                            mm(ps[:, 1, t * N_EXP:(t + 1) * N_EXP], ones[:, :], takes[before], start=before == 0, stop=False)
                        mm(ps[:, 1, t * N_EXP:(t + 1) * N_EXP], st.buf["upto"], takes[t], start=t == 0, stop=True)
                    for t in range(TT):
                        ins = mm(ps[:, 2, 0:N_EXP], ones[:, :], takes[t], start=t == 0, stop=t == TT - 1)
                    ins.then_inc(stage_pe, 1)
                elif st.kind == "mod_cols":
                    for c in range(MOD_W // P):
                        ins = mm(ps[:, 0, 2 * c:2 * c + 2], st.rows[0:4, c * P:(c + 1) * P], pair_sum[:, :], start=True, stop=True)
                    ins.then_inc(stage_pe, 1)
                elif st.kind == "post":
                    pe.wait_ge(stage_dve, st.at["d"] + 1)
                    for s in range(2):
                        for c in range(DC):
                            ins = mm(ps[:, 2 * s + c // 4, (c % 4) * P:(c % 4 + 1) * P], ones[:, :], st.diag[:, s, c, :],
                                     start=True, stop=True)
                    ins.then_inc(stage_pe, 1)


_WEIGHTS = ["w_in", "w_o_sb", "w_o_fox", "w_out", "w_gu_dense", "w_dn_dense", "w_router", "w_gu_exp", "w_dn_exp", "w_mod_2",
            "w_in_2", "w_branch_2", "w_out_2", "w_up_2", "w_down_2", "x", "ctx_2"]


def _constants():
    t, s = np.arange(T)[:, None], np.arange(T)[None, :]

    def tiles(m):
        return np.ascontiguousarray(m.astype(np.float32).reshape(TT, P, -1).transpose(1, 0, 2))

    c0 = np.clip(t % GRID_W - NA_C // 2, 0, GRID_W - NA_C)
    inside = (s % GRID_W >= c0) & (s % GRID_W < c0 + NA_C)
    half = HD // 2
    inv = np.float32(ROPE_THETA) ** (-np.arange(0, half, 2, dtype=np.float32) / np.float32(half))
    n = np.arange(T)
    ang_r, ang_c = ((n // GRID_W).astype(np.float32)[:, None] * inv, (n % GRID_W).astype(np.float32)[:, None] * inv)
    ang = np.concatenate([ang_r, ang_r, ang_c, ang_c], axis=-1)
    sign = np.repeat(np.array([-1, 1, -1, 1], np.float32), HD // 4)
    row_of = np.zeros((NH, NH, P), np.float32)
    row_of[np.arange(NH), np.arange(NH)] = 1
    return {
        "ident": np.eye(P, dtype=np.float32), "row_of": row_of,
        "causal": tiles(np.where(s <= t, 0, NEG)), "anti": tiles(np.where(s >= t, 0, NEG)),
        "strict": tiles(np.where(s < t, -NEG, -BOUND)), "window": tiles(np.where(inside, 0, NEG)),
        "rope_cos": tiles(np.cos(ang)), "rope_sin": tiles(np.sin(ang) * sign),
        "pair_sum": np.array([[1, 0], [0, 1], [1, 0], [0, 1]], np.float32),
        "expert_no": np.arange(N_EXP, dtype=np.float32),
    }


def _laid_out(v):
    def columns(x):
        return np.asarray(x).reshape(-1, P).T

    parts = []
    for l in range(DEPTH):
        parts += [columns(v["g_mix"][l]), columns(v["g_ffn"][l])]
    for l in range(DEPTH):
        parts += [columns(v[n + "_2"][l]) for n in ("g_pre_mix", "g_pre_ffn", "g_post_mix", "g_post_ffn", "g_ml_out", "b_mod",
                                                    "conv_b", "conv_w")]
    parts.append(np.stack([columns(v["c_2"][0]), columns(v["c_ctx_2"])], axis=-1).reshape(P, -1))
    gate_bias = np.zeros((4 * ML_H, 2 * DEPTH), np.float32)
    gate_bias[0:NH, 0:DEPTH] = np.asarray(v["b_f"]).T
    gate_bias[:, DEPTH:] = np.asarray(v["b_ml_gates_2"]).T
    rpb = np.asarray(v["na_rpb_2"])
    padded = np.zeros(rpb.shape[:3] + (2 * GRID_W,), np.float32)
    padded[..., GRID_W - NA_C:GRID_W - NA_C + 2 * NA_C - 1] = rpb
    bias = np.zeros(rpb.shape[:2] + (ROWS, GRID_W, ROWS, GRID_W), np.float32)
    for r in range(ROWS):
        for c in range(GRID_W):
            bias[:, :, r, c] = padded[:, :, NA_R - 1 - r:NA_R - 1 - r + ROWS, GRID_W - 1 - c:2 * GRID_W - 1 - c]
    rows = [np.asarray(v[n])[l] for sfx in ("", "_2") for l in range(DEPTH) for n in ("g_q" + sfx, "g_k" + sfx)]
    return {"cols": np.ascontiguousarray(np.concatenate(parts, axis=1)), "gate_bias": gate_bias, "position_bias": bias.reshape(DEPTH, NH, T, T),
            "g_rows": np.stack(rows), "bias_rows": np.ascontiguousarray(np.asarray(v["b_gate"]).reshape(DEPTH, 4, NT).transpose(1, 0, 2))}


def kernel(**inputs):
    import concourse.bacc as bacc
    from concourse.bass_utils import run_bass_kernel_spmd

    given = {n: np.ascontiguousarray(inputs[n]) for n in _WEIGHTS}
    given.update(_laid_out(inputs))
    given.update(_constants())
    nc = bacc.Bacc("TRN2", target_bir_lowering=False, num_devices=1)
    arrays = {f"in_{n}": x for n, x in given.items()}
    aps = {n: nc.dram_tensor(f"in_{n}", x.shape, F32, kind="ExternalInput").ap() for n, x in given.items()}
    out = nc.dram_tensor("out", (1, T, D), F32, kind="ExternalOutput").ap()
    build(nc, aps, out)
    r = run_bass_kernel_spmd(nc, [arrays], core_ids=[0])
    return r.results[0]["out"]
```

```python
import concourse.bass as bass
from concourse import mybir
from contextlib import ExitStack
import numpy as np

F32 = mybir.dt.float32
F32R = mybir.dt.float32r
U32 = mybir.dt.uint32
I32 = mybir.dt.int32
ALU = mybir.AluOpType
ACT = mybir.ActivationFunctionType
AX = mybir.AxisListType

P = 128
D = 1024
T = 256
TT = T // P
DC = D // P
DEPTH = 2
HD = 64
NH = 8
W_HEADS = NH * HD
BC = W_HEADS // P
KV = 2
ML_H, ML_D = 4, 128
KINDS = (2, 3, 6, 7)
D_FF = 2816
FE = 1408
FB = FE // P
N_EXP = 8
NB2 = 3
GROUPS = [(f, min(512, FE - f)) for f in range(0, FE, 512)]
DOWN = 2 * len(GROUPS)
UPS = DOWN * DC // 2
SEL_T, TURN, GATHER, SCATTER = 5, [(i + 1) * DC + 1 for i in range(len(GROUPS))], UPS + 3, (UPS + 8, 1)
PLACE, TAKES = 64, 80
GRID_W, NA_R, NA_C = 64, 8, 16
ROWS = T // GRID_W
EPS = 1e-6
NEG = -1e30
ROPE_THETA = 10000.0
BOUND = 85.0
NT = 512
M = 4
UNIT = 1024
AHEAD = 2
RAW, HL = 4, 3
QK_SB, V_SB, QK_FX, V_FX, F_FX, G_1 = 0, 1024, 1536, 2560, 3072, 3080
MQ, MK, MV, MO, MG, AQ, NQ, NK, NV, G_2 = 0, 512, 1024, 1536, 2048, 2064, 2832, 3344, 3856, 4368
MOD_W = 6 * D
MOD_RESULTS = MOD_W // NT // 2
BANKS = 8

COL_FIRST = 2 * DC
COL_CONV = 2 * D_FF // P
COL_SECOND = 4 * DC + BC + MOD_W // P + 4 * COL_CONV
COL_C = DEPTH * (COL_FIRST + COL_SECOND)
COLS = COL_C + 2 * DC


def col_first(layer, name):
    return layer * COL_FIRST + {"g_mix": 0, "g_ffn": DC}[name]


def col_second(layer, name):
    at = 0
    for known, n in (("g_pre_mix", DC), ("g_pre_ffn", DC), ("g_post_mix", DC), ("g_post_ffn", DC), ("g_ml_out", BC),
                     ("b_mod", MOD_W // P), ("conv_b", COL_CONV), ("conv_w", 3 * COL_CONV)):
        if known == name:
            return DEPTH * COL_FIRST + layer * COL_SECOND + at
        at += n
    raise KeyError(name)


class Stream:

    def __init__(self, sem, name):
        self.raw_loaded = [sem(f"{name}raw_loaded_{i}") for i in range(RAW)]
        self.hi_ready = sem(f"{name}hi_ready")
        self.lo_ready = sem(f"{name}lo_ready")
        self.hi_used = sem(f"{name}hi_used")
        self.units_used = sem(f"{name}units_used")
        self.results_saved = sem(f"{name}results_saved")


class Experts:

    def __init__(self, sem, name):
        self.sel_ready = sem(f"{name}sel_ready")
        self.gathered = sem(f"{name}gathered")
        self.xg_value = sem(f"{name}xg_value")
        self.xg_hi = sem(f"{name}xg_hi")
        self.xg_done = sem(f"{name}xg_done")
        self.selt_turned = sem(f"{name}selt_turned")
        self.selt_saved = sem(f"{name}selt_saved")
        self.act_turned = sem(f"{name}act_turned")
        self.act_hi_done = sem(f"{name}act_hi_done")
        self.act_done = sem(f"{name}act_done")
        self.scattered = sem(f"{name}scattered")
        self.accumulated = sem(f"{name}accumulated")
        self.all = [self.sel_ready, self.gathered, self.xg_value, self.xg_hi, self.xg_done, self.selt_turned, self.selt_saved,
                    self.act_turned, self.act_hi_done, self.act_done, self.scattered, self.accumulated]


class Segment:

    def __init__(self, units, iters, mode, at, evac, A=None, B=None, N=None, tiles=None, dst=None, scale=None, bias=None,
                 M=None, tmp=None, route=None, n_branch=None, gates=None, bias_layer=None, o=None, cw=None, cb=None,
                 down=None, ex=None, half=None, buf=None, aside=None, mod_rows=None):
        self.units, self.iters, self.n = units, iters, len(units)
        self.looped = iters > 2
        assert not self.looped or self.n % RAW == 0 and self.n % HL == 0
        self.results = max(u[0] for u in units) + 1
        self.next, self.first = None, False
        self.alone = mode == "moe"
        self.sig = self.unit0 = self.result0 = self.flag = self.before = self.ready = None
        self.aside = aside
        self.mods = sum(u[0] < 0 and u[4] for u in units)
        self.mod_rows = mod_rows
        self.down = down if down is not None else self.results
        self.ex, self.half, self.buf = ex, half, buf
        self.mode, self.at, self.evac = mode, at, evac
        self.A, self.B, self.N, self.tiles = A, B, N, tiles
        self.dst, self.scale, self.bias, self.M = dst, scale, bias, M
        self.tmp, self.route, self.o, self.cw, self.cb = tmp, route, o, cw, cb
        self.n_branch, self.gates, self.bias_layer = n_branch, gates, bias_layer

    def unit(self, it, j):
        return it * self.n + (self.unit0 + j)

    def result(self, it, q):
        return it * self.results + (self.result0 + q)

    def slot(self, it, j, slots):
        return (self.unit0 + j + (0 if self.looped else it * self.n)) % slots

    def loaded(self, it, j):
        if self.looped:
            return it * (16 * self.n // RAW) + 16 * ((self.unit0 + j) // RAW)
        return 16 * ((self.unit0 + it * self.n + j) // RAW)


class Step:

    def __init__(self, kind, at=None, seg=None, tiles=None, items=None, mode=None, bias=None, tmp=None, arows=None, mcols=None,
                 decay=None, src=None, sq=None, n=None, parts=None, rope=None, kd=None, jobs=None, dst=None, rows=None,
                 logits=None, route=None, l=None, d=None, mh=None, nq=None, o=None, which=None, diag=None, buf=None):
        self.kind, self.at, self.seg = kind, at, seg
        self.tiles, self.items, self.mode, self.jobs, self.dst = tiles, items, mode, jobs, dst
        self.bias, self.tmp, self.decay, self.arows, self.mcols = bias, tmp, decay, arows, mcols
        self.src, self.sq, self.n, self.parts, self.rope, self.kd = src, sq, n, parts, rope, kd
        self.rows, self.logits, self.route, self.l, self.d = rows, logits, route, l, d
        self.mh, self.nq, self.o, self.which, self.diag, self.buf = mh, nq, o, which, diag, buf


def build(nc, a, out):
    ctx = ExitStack()
    with ctx:
        def sb(name, shape, dt=F32):
            return ctx.enter_context(nc.sbuf_tensor(name, shape, dt))

        def sem(name):
            return ctx.enter_context(nc.semaphore(name))

        raw = sb("raw", [P, RAW, UNIT])
        w_hi = sb("w_hi", [P, HL, UNIT], F32R)
        w_lo = sb("w_lo", [P, HL, UNIT], F32R)
        x_tm = sb("x_tm", [P, 2 * TT, D])
        h_hi = sb("h_hi", [P, DC, 2 * T], F32R)
        h_lo = sb("h_lo", [P, DC, 2 * T], F32R)
        act_hi = sb("act_hi", [P, FB * 2 * T], F32R)
        act_lo = sb("act_lo", [P, FB * 2 * T], F32R)
        y_hi = act_hi[:, 0:BC * 2 * T].rearrange("p (c t) -> p c t", c=BC)
        y_lo = act_lo[:, 0:BC * 2 * T].rearrange("p (c t) -> p c t", c=BC)
        ml_hi = act_hi[0:ML_H, BC * 2 * T:(BC + 2) * 2 * T].rearrange("p (d t) -> p d t", d=2)
        row_of_r = act_hi[0:ML_H, (BC + 2) * 2 * T:(BC + 3) * 2 * T].rearrange("p (h e) -> p h e", e=P)
        ml_lo = act_lo[0:ML_H, BC * 2 * T:(BC + 2) * 2 * T].rearrange("p (d t) -> p d t", d=2)
        c_split = sb("c_split", [P, DC, 4], F32R)
        ident = sb("ident", [P, P])
        ones = sb("ones", [P, P])
        row_of = sb("row_of", [NH, NH, P])
        causal = sb("causal", [P, TT, T], F32R)
        anti = sb("anti", [P, TT, T], F32R)
        ident_r = sb("ident_r", [P, P], F32R)
        strict = sb("strict", [P, TT, T]) 
        window = sb("window", [P, TT, T])
        rope_cos = sb("rope_cos", [P, TT, HD])
        rope_sin = sb("rope_sin", [P, TT, HD])
        expert_no = sb("expert_no", [P, N_EXP])
        cols = sb("cols", [P, COLS])
        mod = sb("mod", [P, MOD_W // P, 2])
        mod_gain = sb("mod_gain", [P, 2, DC, 2])
        mod_post = sb("mod_post", [P, 2, DC, 2])
        g_rows = sb("g_rows", [P, 4 * DEPTH, HD])
        gate_bias = sb("gate_bias", [4 * ML_H, 2 * DEPTH])
        bias_rows = sb("bias_rows", [4 * DEPTH, NT])
        small = sb("small", [P, 192])
        eps = sb("eps", [P, 1])
        fullest = sb("fullest", [1, 1], I32)
        AR = 13312
        arena = sb("arena", [P, AR])
        ps = ctx.enter_context(nc.psum_tensor("ps", [P, BANKS, 512], F32))

        def view(at, *shape):
            n = int(np.prod(shape))
            assert at + n <= AR, (at, n, AR)
            names = "abcd"[:len(shape)]
            if len(shape) == 1:
                return arena[:, at:at + n]
            return arena[:, at:at + n].rearrange(f"p ({' '.join(names)}) -> p {' '.join(names)}",
                                                 **dict(zip(names, shape)))

        merged = view(0, 2 * TT, D)
        FREE = 2 * TT * D
        XN = view(FREE, 2 * TT, D)
        prob = view(FREE, 2, 512)
        prob_t = view(FREE + 1024, 2, 512)
        WORK = FREE + 2048
        turn_value = view(AR - 1024, 2, 512)

        main, over = Stream(sem, ""), Stream(sem, "over_")
        experts_main, experts_over = Experts(sem, "moe_"), Experts(sem, "over_moe_")
        params_loaded = sem("params_loaded")
        at_barrier = sem("at_barrier")
        sums_done = sem("sums_done")
        root_done = sem("root_done")
        turned = sem("turned")
        value_ready = sem("value_ready")
        split_hi_done = sem("split_hi_done")
        split_done = sem("split_done")
        scores_done = sem("scores_done")
        max_done = sem("max_done")
        bounded = sem("bounded")
        exp_done = sem("exp_done")
        probs_done = sem("probs_done")
        pt_done = sem("pt_done")
        pt_saved = sem("pt_saved")
        pv_done = sem("pv_done")
        ml_saved = sem("ml_saved")
        y_hi_done = sem("y_hi_done")
        y_saved = sem("y_saved")
        taps_ready = sem("taps_ready")
        gate_ready = sem("gate_ready")
        mod_saved = sem("mod_saved")
        act_value = sem("act_value")
        act_hi_done = sem("act_hi_done")
        act_done = sem("act_done")
        stage_pe = sem("stage_pe")
        stage_act = sem("stage_act")
        stage_dve = sem("stage_dve")
        bias_loaded = sem("bias_loaded")
        bias_ready = sem("bias_ready")
        constants_set = sem("constants_set")
        act_step = sem("act_step")
        dve_step = sem("dve_step")
        stored = sem("stored")

        START = {"unit": RAW, "result": 2, "turn": 4, "item": 2, "pair": 2, "ml": 2}
        STARTS = [(x, n) for st in (main, over) for x, n in ((st.hi_ready, RAW), (st.lo_ready, RAW), (st.hi_used, RAW),
                                                             (st.units_used, RAW), (st.results_saved, 2))]
        STARTS += [(x, M) for e in (experts_main, experts_over) for x in e.all]
        STARTS += [(turned, 4), (value_ready, 4),
                  (split_hi_done, 4), (split_done, 4), (scores_done, 2), (exp_done, 2), (probs_done, 2), (pt_done, 2),
                  (pt_saved, 2), (pv_done, 2), (y_hi_done, 2), (y_saved, 2), (ml_saved, 2), (mod_saved, 2)]

        plan, segments = [], []
        count = {"barrier": 0, "sum": 0, "root": 0, "gate": 0, "tap": 0, "act": 0, "value": 0,
                 "pe": 0, "a": 0, "d": 0, "max": 0, "bounded": 0, "bias": 0, "mod": 2, **START}

        def add(kind, **kw):
            plan.append(Step(kind, dict(count), **kw))

        def took(**kw):
            for name, n in kw.items():
                count[name] += n

        def add_segment(mode, units, iters=1, **kw):
            s = Segment(units, iters, mode, dict(count), **kw)
            s.sig, s.unit0, s.result0 = main, count["unit"], count["result"]
            took(unit=s.n * iters, result=s.results * iters)
            if segments and not segments[-1].alone:
                segments[-1].next = s
            else:
                s.first = True
            segments.append(s)
            plan.append(Step("segment", seg=s))
            return s

        def add_overflow(mode, units, iters, flag, **kw):
            s = Segment(units, iters, mode, dict(count), **kw)
            s.sig, s.unit0, s.result0 = over, START["unit"], START["result"]
            s.first = s.alone = True
            s.flag, s.before, s.ready = flag, segments[-1], count["d"]
            segments.append(s)
            plan.append(Step("overflow", seg=s))

        def meet():
            add("barrier")
            took(barrier=1)

        def tm_units(w, c0, q=0, chunks=DC, width=NT):
            n = UNIT // width
            return [(q, k, min(n, chunks - k), k == 0, k + n >= chunks, width,
                     lambda it, k=k: w[k * P:min(k + n, chunks) * P, c0:c0 + width].rearrange("(c p) n -> p c n", p=P))
                    for k in range(0, chunks, n)]

        def fm_units(w, c0, q=0, width=2 * P):
            n = UNIT // (2 * P)
            return [(q, k, n, k == 0, k + n == DC, width,
                     lambda it, k=k: w[k * P:(k + n) * P, c0:c0 + width].rearrange("(c p) n -> p c n", p=P))
                    for k in range(0, DC, n)]

        def ffn_units(w_up, w_down, w_mod=None):
            def up(it, half, b):
                f0 = half * D_FF + it * FE + b * P
                return w_up[:, f0:f0 + P].rearrange("(c p) n -> p c n", p=P)

            def down(it, k, m, half):
                return w_down[it * FE + k * P:it * FE + (k + m) * P, half * NT:(half + 1) * NT].rearrange("(c p) n -> p c n", p=P)

            def mod_weights(it, k, r):
                c0 = (it * MOD_RESULTS + r) * NT
                return w_mod[k * P:(k + 2) * P, c0:c0 + NT].rearrange("(c p) n -> p c n", p=P)

            mods = [] if w_mod is None else [(-1 - r, k, 2, k == 0, k + 2 == DC, NT, lambda it, k=k, r=r: mod_weights(it, k, r))
                                             for r in range(MOD_RESULTS) for k in range(0, DC, 2)]
            units = []
            for b in range(FB):
                halves = [(b, 0, DC, half == 0, half == 1, P, lambda it, half=half, b=b: up(it, half, b)) for half in range(2)]
                units += halves[:1] + mods[len(mods) * b // FB:len(mods) * (b + 1) // FB] + halves[1:]
            for half in range(2):
                for k in range(0, FB, 2):
                    m = min(2, FB - k)
                    units.append((FB + half, k, m, k == 0, k + m == FB, NT,
                                  lambda it, k=k, m=m, half=half: down(it, k, m, half)))
            return units

        def expert_units(w_up, w_down):
            units = []
            for q in range(2 * len(GROUPS)):
                f, n = GROUPS[q // 2]
                for k in range(0, DC, 2):
                    units.append((q, k, 2, k == 0, k + 2 == DC, n, lambda it, k=k, n=n, f0=(q % 2) * FE + f:
                                  w_up[bass.ds(it, 1), k * P:(k + 2) * P, f0:f0 + n].rearrange("e (c p) n -> p (e c) n", p=P)))
            for half in range(2):
                for k in range(0, FB, 2):
                    m = min(2, FB - k)
                    units.append((DOWN + half, k, m, k == 0, k + m == FB, NT, lambda it, k=k, m=m, half=half:
                                  w_down[bass.ds(it, 1), k * P:(k + m) * P, half * NT:(half + 1) * NT]
                                  .rearrange("e (c p) n -> p (e c) n", p=P)))
            return units

        def norm(tiles):
            add("norm", tiles=tiles)
            took(root=1)
            meet()

        def turn(items):
            add("turn", items=items)
            took(turn=len(items))
            meet()

        def turn_tokens(src, tiles, gain, shift):
            turn([([src[:, t, (4 * h + c) * P:(4 * h + c + 1) * P] for c in range(4)],
                   gain(t)[:, 4 * h:4 * h + 4] if gain else None, shift(t)[:, 4 * h:4 * h + 4] if shift else None,
                   h_hi[:, 4 * h:4 * h + 4, t * P:(t + 1) * P], h_lo[:, 4 * h:4 * h + 4, t * P:(t + 1) * P])
                  for t in range(tiles) for h in range(2)])

        def attend(kind, items, bias=None, tmp=None, arows=None, mcols=None, decay=None):
            add("attend", mode=kind, items=items, bias=bias, tmp=tmp, arows=arows, mcols=mcols, decay=decay)
            took(item=len(items))
            if kind == "mlstm":
                took(ml=len(items))
            else:
                took(pair=len(items) // 2, max=len(items) if kind == "soft" else 0, bounded=len(items) if kind == "stick" else 0)
            meet()

        def beside(kind, **kw):
            step = Step(kind, dict(count), **kw)
            if kind == "head_norm":
                took(sum=1, root=1, a=0 if step.rows is None else 1)
            else:
                took(a=2, d=2, pe=2)
            return step

        def turn_heads(jobs):
            add("turn_heads", jobs=jobs)
            took(pe=len(jobs), a=len(jobs))
            meet()

        def merge(n, w, g0, w_b, tiles, bias_layer, aside=None):
            units = []
            for dt in range(2):
                units += tm_units(w, g0 + dt * NT, 2 * dt)
                units += tm_units(w_b, dt * NT, 2 * dt + 1, BC)
            add_segment("tm", units, A=(h_hi, h_lo), B=(y_hi, y_lo), tiles=tiles, evac="merge", n_branch=n,
                        gates=view(WORK, 2 * TT, NT), bias_layer=bias_layer, aside=aside)
            meet()

        def mixed_out(w, tiles, **kw):
            turn_tokens(merged, tiles, None, None)
            add_segment("tm", tm_units(w, 0, 0) + tm_units(w, NT, 1), A=(h_hi, h_lo), tiles=tiles, **kw)
            meet()

        def modulation(rows, l):
            add("mod_cols", rows=rows, l=l)
            took(pe=1)
            meet()

        def first_layer(l):
            w = a["w_in"][l]
            qk = view(WORK, 2 * BC, T)
            v = view(WORK + 2048, TT, W_HEADS)
            tmp = view(WORK + 3072, 8, T)
            pre = view(WORK + 3072, TT, 2 * W_HEADS)
            sq = view(WORK + 5120, TT, 2 * W_HEADS)
            rows = view(TT * D, 4, 2 * T)
            H = (h_hi, h_lo)
            norm(TT)
            turn_tokens(XN, TT, lambda t: cols[:, col_first(l, "g_mix"):][:, 0:DC], None)
            add_segment("fm", sum((fm_units(w, QK_SB + q * 2 * P, q) for q in range(4)), []), A=H, N=T, evac="fm", dst=qk,
                        scale=[HD ** -0.5] * 2 + [1.0] * 2)
            add_segment("tm", tm_units(w, V_SB), A=H, tiles=TT, evac="tm", dst=v)
            meet()

            def heads(hh, pr, t):
                return dict(q=qk[hh * HD:(hh + 1) * HD, pr, t * P:(t + 1) * P],
                            k=qk[hh * HD:(hh + 1) * HD, BC + pr, 0:(t + 1) * P], nk=(t + 1) * P, add=[],
                            v=[v[:, s, (2 * pr + hh) * HD:(2 * pr + hh + 1) * HD] for s in range(t + 1)], hh=hh, y=(pr, t))

            order = [(hh, pr, t) for pr in range(BC) for t in range(TT) for hh in range(2)]
            attend("stick", [dict(heads(*o), cap=strict[:, o[2], 0:(o[2] + 1) * P]) for o in order], tmp=tmp)
            add_segment("tm", tm_units(w, QK_FX, 0) + tm_units(w, QK_FX + NT, 1), A=H, tiles=TT, evac="tm", dst=pre)
            add_segment("tm", tm_units(w, V_FX), A=H, tiles=TT, evac="tm", dst=v)
            add_segment("fm", fm_units(w, F_FX, 0, NH), A=H, N=T, evac="rows", dst=rows[0:NH, 0, 0:T],
                        bias=gate_bias[0:NH, l:l + 1], M=NH)
            meet()
            merge(0, w, G_1, a["w_o_sb"][l], TT, l,
                  beside("head_norm", src=pre, sq=sq, tiles=TT, n=2 * NH, rope=False, rows=rows,
                         parts=[(0, NH, 2 * l, HD ** -0.5), (NH, 2 * NH, 2 * l + 1, 1.0)]))
            turn_heads([([pre[:, t, (part * BC + c) * P:(part * BC + c + 1) * P] for c in range(BC)],
                         qk[:, part * BC:(part + 1) * BC, t * P:(t + 1) * P]) for t in range(TT) for part in range(2)])
            attend("soft", [dict(heads(hh, pr, t),
                                 add=[(row_of[:, 2 * pr + hh, :], rows[0:NH, 3, 0:(t + 1) * P], None),
                                      (ident_r[:, :], causal[:, t, 0:(t + 1) * P], None)]) for hh, pr, t in order])
            merge(1, w, G_1 + D, a["w_o_fox"][l], TT, l)
            mixed_out(a["w_out"][l], TT, evac="residual")
            norm(TT)
            turn_tokens(XN, TT, lambda t: cols[:, col_first(l, "g_ffn"):][:, 0:DC], None)
            if l % 2:
                logits = view(2048, 2, 512)[0:N_EXP, 0, 0:T]
                route = view(3072, TT, 96)
                buf = dict(silu=view(0, 512), value=view(512, 512), y=view(1024, 2, 512), sel_t=view(3328, 2 * P),
                           sel=view(3584, TT, P), slot_no=view(3840, 2 * P), tokens=XN, upto=view(FREE + TT * D, P),
                           flag=fullest[:, :])
                add_segment("fm", fm_units(a["w_router"][l // 2], 0, 0, N_EXP), A=H, N=T, evac="rows", dst=logits, bias=None,
                            M=N_EXP)
                meet()
                add("route", logits=logits, route=route, buf=buf)
                took(pe=2, d=3, a=1)
                meet()
            if l % 2:
                units = expert_units(a["w_gu_exp"][l // 2], a["w_dn_exp"][l // 2])
                for half, ex in enumerate((experts_main, experts_over)):
                    kw = dict(A=(h_hi[:, :, T:T + P], h_lo[:, :, T:T + P]), N=P, tiles=1, evac="experts", route=route, down=DOWN,
                              ex=ex, half=half, buf=buf, scale=cols[:, col_first(l, "g_ffn"):][:, 0:DC])
                    if half == 0:
                        add_segment("moe", units, N_EXP, **kw)
                    else:
                        add_overflow("moe", units, N_EXP, buf["flag"], **kw)
                    meet()
                return
            n = D_FF // FE
            mod_rows = (view(2048, MOD_W // 2), view(2048 + MOD_W // 2, MOD_W // 2))
            add_segment("ffn", ffn_units(a["w_gu_dense"][l // 2], a["w_dn_dense"][l // 2], a["w_mod_2"][0]), n, A=H, N=T, tiles=TT,
                        evac="swiglu", tmp=view(0, 4, 2 * T), down=FB, mod_rows=mod_rows)
            took(act=FB * n, tap=FB * n, mod=MOD_W // NT)
            meet()
            modulation(mod_rows, 0)

        def second_layer(l):
            w = a["w_in_2"][l]
            nq = TT if l == DEPTH - 1 else 2 * TT
            nn = 2 * TT
            H = (h_hi, h_lo)
            norm(nn)
            turn_tokens(XN, nn, lambda t: mod_gain[:, 0, :, t // TT], lambda t: mod[:, 0:DC, t // TT])

            def span(t):
                return 0 if t < TT else T

            mqk = view(WORK, 2 * ML_H, 2 * T)
            mv = view(WORK + 4096, nn, W_HEADS)
            arows = view(0, 2, 2 * T)
            rows = view(1024, 2, 2 * T)
            drows = view(FREE, 4, 2 * T)
            mcols = small[:, 128:192].rearrange("p (t k h) -> p t k h", t=nn, k=4)
            add_segment("fm", fm_units(w, MG, 0, 4 * ML_H), A=H, N=2 * T, evac="rows", dst=rows[0:4 * ML_H, 0, :],
                        bias=gate_bias[0:4 * ML_H, DEPTH + l:DEPTH + l + 1], M=4 * ML_H)
            add_segment("fm", sum((fm_units(w, MQ + q * 2 * P, q) for q in range(4)), []), A=H, N=2 * T, evac="fm", dst=mqk,
                        scale=[1.0] * 2 + [ML_D ** -0.5] * 2,
                        aside=beside("ml_rows", rows=rows, d=drows, arows=arows, mcols=mcols))
            add_segment("tm", tm_units(w, MV), A=H, tiles=nn, evac="tm", dst=mv)
            meet()
            attend("mlstm", [dict(q=mqk[:, h, t * P:(t + 1) * P], k=mqk[:, ML_H + h, span(t):2 * T], nk=2 * T - span(t),
                                  k0=span(t), t=t, h=h, masks=(causal[:, t % TT, :], anti[:, t % TT, :]),
                                  v=[mv[:, s, h * ML_D:(h + 1) * ML_D] for s in range(span(t) // P, nn)],
                                  dst=mqk[:, h, t * P:(t + 1) * P])
                             for t in range(nq) for h in range(ML_H)], arows=arows, mcols=mcols,
                   decay=view(1024, 2, 2, 512))
            mh = mqk[:, 0:ML_H, 0:nq * P].rearrange("p h (t e) -> p h t e", e=P)
            add("ml_norm", mh=mh, sq=view(WORK + 4096, ML_H, nq, P), nq=nq)
            took(sum=1, root=1)
            meet()
            add_segment("tm", tm_units(w, MO), A=H, tiles=nq, evac="ml_gate", gates=view(WORK + 4096, 2 * TT, NT),
                        dst=mqk[:, 0:ML_H, 0:nq * P].rearrange("p h (t e) -> p t h e", e=P))
            took(gate=1)
            meet()
            g = cols[:, col_second(l, "g_ml_out"):][:, 0:BC]
            turn([([mqk[:, c, t * P:(t + 1) * P] for c in range(BC)], g, None, y_hi[:, :, t * P:(t + 1) * P],
                   y_lo[:, :, t * P:(t + 1) * P]) for t in range(nq)])
            QKW, QKV = (NH + KV) * HD, (NH + 2 * KV) * HD
            pre = view(WORK + 2048, nn, QKV)
            v = pre[:, :, QKW:QKV].rearrange("p t (g d) -> p t g d", d=HD)
            sq = view(WORK + 2048 + nn * QKV, TT, QKW)
            kd = view(WORK + 2048 + nn * QKV, nn, KV, 2, HD)
            qT = view(WORK, BC, 2 * T)
            kT = view(AR - KV * 2 * T, KV, 2 * T)
            add_segment("tm", tm_units(w, AQ), A=H, tiles=nn, evac="tm", dst=pre)
            add_segment("tm", tm_units(w, AQ + W_HEADS, 0, DC, 2 * KV * HD), A=H, tiles=nn, evac="tm", dst=pre[:, :, W_HEADS:QKV])
            meet()
            merge(0, w, G_2, a["w_branch_2"][l, 0], nq, None,
                  beside("head_norm", src=pre[:, :, 0:QKW], sq=sq, tiles=nn, n=NH + KV, rope=True, kd=kd,
                         parts=[(0, NH, 2 * DEPTH + 2 * l, HD ** -0.5), (NH, NH + KV, 2 * DEPTH + 2 * l + 1, 1.0)]))
            turn_heads([j for t in range(nn) for j in
                        (([pre[:, t, c * P:(c + 1) * P] for c in range(BC)], qT[:, :, t * P:(t + 1) * P]),
                         ([kd[:, t, g, :, :].rearrange("p a d -> p (a d)") for g in range(KV)], kT[:, :, t * P:(t + 1) * P]))])

            def gqa(hh, pr, t):
                g = 2 * pr // (NH // KV)
                return dict(q=qT[hh * HD:(hh + 1) * HD, pr, t * P:(t + 1) * P], k=kT[hh * HD:(hh + 1) * HD, g, span(t):2 * T],
                            nk=2 * T - span(t), add=[], v=[v[:, s, g, :] for s in range(span(t) // P, nn)], hh=hh, y=(pr, t))

            order = [(hh, pr, t) for pr in range(BC) for t in range(nq) for hh in range(2)]
            attend("soft", [gqa(*o) for o in order])
            merge(1, w, G_2 + D, a["w_branch_2"][l, 1], nq, None)
            nqk = view(WORK, 2 * BC, 2 * T)
            nv = view(WORK + 4096, nn, W_HEADS)
            nbias = [view(WORK + 6144, 2, TT, T)]
            if nq == TT:
                nbias.append(view(TT * D, 2, TT, T))
            add_segment("fm", sum((fm_units(w, NQ + q * 2 * P, q) for q in range(4)), []), A=H, N=2 * T, evac="fm", dst=nqk,
                        scale=[HD ** -0.5] * 2 + [1.0] * 2)
            add_segment("tm", tm_units(w, NV), A=H, tiles=nn, evac="tm", dst=nv)
            meet()

            def na(hh, pr, t):
                h = 2 * pr + hh
                return dict(q=nqk[hh * HD:(hh + 1) * HD, pr, t * P:(t + 1) * P],
                            k=nqk[hh * HD:(hh + 1) * HD, BC + pr, span(t):2 * T], nk=2 * T - span(t),
                            add=[(ident[:, :], nbias[pr % len(nbias)][:, hh, t, :], count["bias"] + h + 1)] if t < TT else [],
                            v=[nv[:, s, h * HD:(h + 1) * HD] for s in range(span(t) // P, nn)], hh=hh, y=(pr, t))

            attend("soft", [na(*o) for o in order], bias=(nbias, l, 2 * nq))
            took(bias=NH)
            merge(2, w, G_2 + 2 * D, a["w_branch_2"][l, 2], nq, None)
            o = view(FREE, 2 * TT, D)
            diag = view(FREE + 4096, 2, DC, P)
            mixed_out(a["w_out_2"][l], nq, evac="tm", dst=o)

            def post(which):
                add("post", o=o, nq=nq, which=which, diag=diag)
                took(root=1, d=1, pe=1)
                meet()

            post(0)
            norm(nq)
            turn_tokens(XN, nq, lambda t: mod_gain[:, 1, :, t // TT], lambda t: mod[:, 3 * DC:4 * DC, t // TT])
            mod_rows = (view(0, MOD_W // 2), view(FREE + 6144, MOD_W // 2))
            more = l + 1 < DEPTH
            add_segment("ffn", ffn_units(a["w_up_2"][l], a["w_down_2"][l], a["w_mod_2"][l + 1] if more else None), D_FF // FE,
                        A=H, N=nq * P, tiles=nq, mod_rows=mod_rows,
                        evac="conv", tmp=view(FREE + 4096, 4, 2 * T), o=o, cw=col_second(l, "conv_w"),
                        cb=col_second(l, "conv_b"), down=FB)
            n = FB * (D_FF // FE)
            took(act=n, tap=2 * n, gate=n, value=n, mod=MOD_W // NT if more else 0)
            meet()
            post(1)
            if more:
                modulation(mod_rows, l + 1)

        for l in range(DEPTH):
            first_layer(l)
        for l in range(DEPTH):
            second_layer(l)

        params = [(x_tm[:, 0:TT, :], a["x"][0].rearrange("(t p) d -> p t d", p=P)),
                  (x_tm[:, TT:2 * TT, :], a["ctx_2"][0].rearrange("(t p) d -> p t d", p=P)),
                  (cols[:, :], a["cols"]), (ident[:, :], a["ident"]), (row_of[:, :, :], a["row_of"]),
                  (view(0, TT, T), a["causal"]), (view(TT * T, TT, T), a["anti"]), (strict[:, :, :], a["strict"]),
                  (window[:, :, :], a["window"]), (rope_cos[:, :, :], a["rope_cos"]), (rope_sin[:, :, :], a["rope_sin"]),
                  (gate_bias[:, :], a["gate_bias"]), (bias_rows[:, :], a["bias_rows"]),
                  (expert_no[:, :], a["expert_no"].partition_broadcast(P)), (g_rows[:, :, :], a["g_rows"].partition_broadcast(P))]
        PARAMS = 16 * len(params)

        block = ctx.enter_context(nc.Block())

        @block.sync
        def _(sp):
            def load(seg, it, j):
                q, k, m, opens, closes, width, source = seg.units[j]
                sp.wait_ge(seg.sig.lo_ready, seg.unit(it, j) - RAW + 1)
                slot = seg.slot(it, j, RAW)
                dst = raw[:, slot, 0:m * width].rearrange("p (c n) -> p c n", c=m)
                sp.dma_start(dst, source(it)).then_inc(seg.sig.raw_loaded[slot], 16)

            def loads(seg):
                if seg.iters > 2:
                    with sp.Fori(0, seg.iters) as it:
                        for j in range(seg.n):
                            load(seg, it, j)
                else:
                    for it in range(seg.iters):
                        for j in range(seg.n):
                            load(seg, it, j)

            for seg in segments:
                if seg.flag is None:
                    loads(seg)
                    continue
                sp.wait_ge(stage_dve, seg.ready)
                most = sp.value_load(seg.flag, min_val=0, max_val=T)
                with sp.If(most > P):
                    sp.wait_ge(seg.before.sig.lo_ready, seg.before.unit(seg.iters, 0))
                    loads(seg)
                    sp.wait_ge(seg.sig.lo_ready, seg.unit(seg.iters, 0))
            sp.wait_ge(at_barrier, 4 * count["barrier"])
            sp.dma_start(out[0].rearrange("(t p) d -> p t d", p=P), x_tm[:, 0:TT, :]).then_inc(stored, 16)
            sp.wait_ge(stored, 16)

        @block.gpsimd
        def _(pool):
            for s, n in STARTS:
                pool.sem_inc(s, n)
            nc.gpsimd.memset(ones[:, :], 1.0)
            nc.gpsimd.memset(eps[:, :], EPS).then_inc(constants_set, 1)
            pool.wait_ge(params_loaded, PARAMS)

            for st in plan:
                if st.kind == "barrier":
                    pool.drain().then_inc(at_barrier, 1)
                    pool.wait_ge(at_barrier, 4 * (st.at["barrier"] + 1))
                elif st.kind == "attend" and st.bias is not None:
                    nbias, l, per_pair = st.bias
                    for pr in range(BC):
                        buf = nbias[pr % len(nbias)]
                        if pr >= len(nbias):
                            pool.wait_ge(scores_done, st.at["item"] + (pr - len(nbias)) * per_pair + 2 * TT)
                        pool.dma_start(buf.rearrange("p h t k -> p (h t) k"),
                                       a["position_bias"][l, 2 * pr:2 * pr + 2].rearrange("h (t p) k -> p (h t) k", p=P))\
                            .then_inc(bias_loaded, 16)
                        pool.wait_ge(bias_loaded, 16 * (st.at["bias"] // 2 + pr + 1))
                        for hh in range(2):
                            nc.gpsimd.tensor_tensor(buf[:, hh, :, :], buf[:, hh, :, :], window[:, :, :], ALU.add)\
                                .then_inc(bias_ready, 1)

        @block.scalar
        def _(act):
            steps = [0]

            def settled(ins):
                steps[0] += 1
                ins.then_inc(act_step, 1)
                act.wait_ge(act_step, steps[0])

            for dst, src in params:
                act.dma_start(dst, src).then_inc(params_loaded, 16)
            act.wait_ge(params_loaded, PARAMS)
            act.wait_ge(constants_set, 1)
            for dst, src in ((causal[:, :, :], view(0, TT, T)), (anti[:, :, :], view(TT * T, TT, T)), (ident_r[:, :], ident[:, :])):
                nc.scalar.activation(dst, src, ACT.Copy)
            silu_c = small[:, 104:104 + 2 * DC].rearrange("p (c s) -> p c s", s=2)
            settled(nc.scalar.activation(silu_c, cols[:, COL_C:COL_C + 2 * DC].rearrange("p (c s) -> p c s", s=2), ACT.Silu))
            nc.scalar.activation(c_split[:, :, 0:2], silu_c, ACT.Copy).then_inc(split_hi_done, 1)

            def split(seg, it, j):
                q, k, m, opens, closes, width, source = seg.units[j]
                n = m * width
                slot, half = seg.slot(it, j, RAW), seg.slot(it, j, HL)
                act.wait_ge(seg.sig.raw_loaded[slot], seg.loaded(it, j))
                act.wait_ge(seg.sig.hi_used, seg.unit(it, j) - HL + 1)
                act.wait_ge(seg.sig.lo_ready, seg.unit(it, j) - HL + 1)
                nc.scalar.activation(w_hi[:, half, 0:n], raw[:, slot, 0:n], ACT.Copy).then_inc(seg.sig.hi_ready, 1)

            def save(seg, it, j):
                q, k, m, opens, closes, width, source = seg.units[j]
                if not closes or seg.evac == "residual" and q >= 0:
                    return
                if q < 0:
                    act.wait_ge(seg.sig.units_used, seg.unit(it, j) + 1)
                    nc.scalar.activation(seg.mod_rows[it][0:4, (-1 - q) * NT:-q * NT], ps[0:4, 2 + q % 2, :], ACT.Copy)\
                        .then_inc(mod_saved, 1)
                    return
                r = seg.result(it, q)
                b = 4 * (q % 2)
                if seg.mode == "ffn" and q >= FB:
                    return
                if seg.evac in ("merge", "experts") and q % 2 and q < seg.down:
                    return
                act.wait_ge(seg.sig.units_used, seg.unit(it, j) + 1)
                if seg.evac == "fm":
                    nc.scalar.activation(seg.dst[:, 2 * q:2 * q + 2, 0:seg.N], ps[:, b:b + 2, 0:seg.N], ACT.Copy,
                                         scale=seg.scale[q]).then_inc(seg.sig.results_saved, 1)
                elif seg.evac == "tm":
                    nc.scalar.activation(seg.dst[:, 0:seg.tiles, q * NT:q * NT + width], ps[:, b:b + seg.tiles, 0:width], ACT.Copy)\
                        .then_inc(seg.sig.results_saved, 1)
                elif seg.evac == "rows":
                    if seg.bias is None:
                        ins = nc.scalar.activation(seg.dst, ps[0:seg.M, b, 0:seg.N], ACT.Copy)
                    else:
                        ins = nc.scalar.activation(seg.dst, ps[0:seg.M, b, 0:seg.N], ACT.Identity, bias=seg.bias)
                    ins.then_inc(seg.sig.results_saved, 1)
                elif seg.evac == "merge":
                    act.wait_ge(seg.sig.results_saved, r)
                    nc.scalar.activation(seg.gates[:, 0:seg.tiles, :], ps[:, b:b + seg.tiles, :], ACT.Sigmoid)\
                        .then_inc(seg.sig.results_saved, 1)
                elif seg.evac == "experts" and q < DOWN:
                    act.wait_ge(seg.sig.results_saved, r)
                    n = seg.units[j][5]
                    nc.scalar.activation(seg.buf["silu"][:, 0:n], ps[:, b, 0:n], ACT.Silu).then_inc(seg.sig.results_saved, 1)
                elif seg.evac == "experts":
                    act.wait_ge(seg.ex.scattered, 2 * it + (q - DOWN) + (M - 1))
                    act.wait_ge(seg.sig.results_saved, r)
                    nc.scalar.activation(seg.buf["y"][:, q - DOWN, :], ps[:, b, :], ACT.Copy).then_inc(seg.sig.results_saved, 1)
                elif seg.evac == "ml_gate":
                    nc.scalar.activation(seg.gates[:, 0:seg.tiles, :], ps[:, b:b + seg.tiles, :], ACT.Sigmoid)\
                        .then_inc(gate_ready, 1)
                elif seg.evac == "swiglu":
                    done = it * FB + (seg.at["act"] + q)
                    nc.scalar.activation(seg.tmp[:, q % 2, 0:seg.N], ps[:, b, 0:seg.N], ACT.Silu).then_inc(taps_ready, 1)
                elif seg.evac == "conv":
                    for part in range(2):
                        c = it * FB + q + part * (COL_CONV // 2)
                        nc.scalar.activation(seg.tmp[:, 2 * (q % 2) + part, 0:seg.N], ps[:, b + part, 0:seg.N], ACT.Identity,
                                             scale=cols[:, seg.cw + COL_CONV + c:seg.cw + COL_CONV + c + 1],
                                             bias=cols[:, seg.cb + c:seg.cb + c + 1]).then_inc(taps_ready, 1)

            def save_late(seg, it, j):
                q, k, m, opens, closes, width, source = seg.units[j]
                if not closes or seg.mode != "ffn" or not 0 <= q < FB:
                    return
                r = seg.result(it, q)
                if seg.evac == "swiglu":
                    act.wait_ge(seg.sig.results_saved, r + 1)
                    nc.scalar.activation(act_hi[:, q * seg.N:(q + 1) * seg.N], seg.tmp[:, 2 + q % 2, 0:seg.N], ACT.Copy)\
                        .then_inc(act_hi_done, 1)
                elif seg.evac == "conv":
                    act.wait_ge(seg.sig.results_saved, r + 1)
                    g = seg.tmp[:, 2 * (q % 2) + 1, 0:seg.N]
                    nc.scalar.activation(g, g, ACT.Silu).then_inc(gate_ready, 1)
                    act.wait_ge(act_value, it * FB + q + seg.at["value"] + 1)
                    nc.scalar.activation(act_hi[:, q * seg.N:(q + 1) * seg.N], seg.tmp[:, 2 * (q % 2), 0:seg.N], ACT.Copy)\
                        .then_inc(act_hi_done, 1)

            def upper_half(seg, e, half):
                act.wait_ge(seg.ex.xg_value, 2 * e + (M + half + 1))
                nc.scalar.activation(h_hi[:, 4 * half:4 * half + 4, T:T + P],
                                     turn_value[:, half, :].rearrange("p (c t) -> p c t", t=P), ACT.Copy).then_inc(seg.ex.xg_hi, 1)

            def first_tokens(seg):
                for half in range(2):
                    upper_half(seg, 0, half)

            def between(seg, it, j, first):
                if j == SEL_T + 2:
                    act.wait_ge(seg.ex.selt_turned, it + (M + 1))
                    nc.scalar.activation(seg.buf["sel_t"], ps[:, 5, 0:2 * P], ACT.Copy).then_inc(seg.ex.selt_saved, 1)
                for i, (f, n) in enumerate(GROUPS):
                    if j == TURN[i] + 2:
                        act.wait_ge(seg.ex.act_turned, 3 * it + (M + i + 1))
                        nc.scalar.activation(act_hi[:, f:f + n], ps[:, 3, 0:n], ACT.Copy).then_inc(seg.ex.act_hi_done, 1)
                for half in range(2):
                    if j == GATHER + 3 + half:
                        act.wait_ge(seg.sig.units_used, seg.unit(it, UPS - 1) + 1)
                        upper_half(seg, it + 1, half)

            def root(n, width):
                nc.scalar.activation(small[:, 64:64 + n], small[:, 0:n], ACT.Sqrt, scale=1.0 / width, bias=eps[:, :])\
                    .then_inc(root_done, 1)

            def softplus(u, e):
                settled(nc.scalar.activation(e, u, ACT.Abs))
                settled(nc.scalar.activation(e, e, ACT.Exp, scale=-1.0))
                nc.scalar.activation(e, e, ACT.Ln, bias=1.0).then_inc(stage_act, 1)

            def aside(seg, st, j):
                if st.kind == "head_norm":
                    if j == 3:
                        act.wait_ge(sums_done, st.at["sum"] + 1)
                        root(st.tiles * st.n, HD)
                    if j == 6 and st.rows is not None:
                        softplus(st.rows[0:NH, 0, 0:T], st.rows[0:NH, 2, 0:T])
                if st.kind == "ml_rows":
                    n = 4 * ML_H
                    if j == 1:
                        act.wait_ge(seg.sig.results_saved, seg.result(0, 0))
                        softplus(st.rows[0:n, 0, :], st.arows[0:n, 0, :])
                        nc.scalar.activation(row_of_r, row_of[0:ML_H, 0:ML_H, :], ACT.Copy)
                    if j == 7:
                        act.wait_ge(stage_pe, st.at["pe"] + 2)
                        m = ps[:, 6, 0:64].rearrange("p (t k h) -> p t k h", t=2 * TT, k=4)
                        nc.scalar.activation(st.mcols[:, :, 0:2, :], m[:, :, 0:2, :], ACT.Exp, scale=-1.0)
                        nc.scalar.activation(st.mcols[:, :, 2:4, :], m[:, :, 2:4, :], ACT.Copy, scale=-1.0).then_inc(stage_act, 1)

            def stream(seg):
                def body(it, before, first):
                    for j in range(seg.n):
                        if not first or j >= AHEAD:
                            split(seg, it, j)
                        if j >= AHEAD:
                            save(seg, it, j - AHEAD)
                        elif not first:
                            save(seg, before, seg.n + j - AHEAD)
                        if j > AHEAD:
                            save_late(seg, it, j - AHEAD - 1)
                        if seg.mode == "moe":
                            between(seg, it, j, first)
                        if seg.aside is not None:
                            aside(seg, seg.aside, j)

                if seg.first:
                    for j in range(AHEAD):
                        split(seg, 0, j)
                if seg.mode == "moe":
                    first_tokens(seg)
                body(0, None, True)
                if seg.iters > 2:
                    with act.Fori(1, seg.iters) as it:
                        body(it, it - 1, False)
                elif seg.iters == 2:
                    body(1, 0, False)
                for j in range(AHEAD):
                    if seg.next:
                        split(seg.next, 0, j)
                    save(seg, seg.iters - 1, seg.n + j - AHEAD)

            def attend(st):
                k0 = st.at["item"]
                n = len(st.items)

                def weights(i):
                    e, i0 = st.items[i], k0 + i
                    nk = e["nk"]
                    z = ps[:, i0 % 2, 0:nk]
                    if st.mode == "soft":
                        act.wait_ge(max_done, st.at["max"] + i + 1)
                        act.wait_ge(pt_done, i0 - 1)
                        nc.scalar.activation(prob[:, i0 % 2, 0:nk], z, ACT.Exp, bias=small[:, i0 % 2:i0 % 2 + 1],
                                             accum_out=small[:, 2 + i0 % 2:3 + i0 % 2]).then_inc(exp_done, 1)
                    elif st.mode == "stick":
                        e_, e1 = st.tmp[:, 2 + i0 % 2, 0:nk], st.tmp[:, 4 + i0 % 2, 0:nk]
                        act.wait_ge(bounded, st.at["bounded"] + i + 1)
                        act.wait_ge(probs_done, i0 - 1)
                        settled(nc.scalar.activation(e_, st.tmp[:, i0 % 2, 0:nk], ACT.Exp, scale=-1.0))
                        nc.scalar.activation(e1, e_, ACT.Identity, bias=ones[:, 0:1]).then_inc(exp_done, 1)
                    else:
                        act.wait_ge(scores_done, i0 + 1)
                        act.wait_ge(probs_done, i0 - 1)
                        for d in range(2):
                            ins = nc.scalar.activation(st.decay[:, i0 % 2, d, 0:nk], ps[:, 4 + 2 * (i0 % 2) + d, 0:nk], ACT.Exp,
                                                       bias=st.mcols[:, e["t"], 2 + d, e["h"]:e["h"] + 1])
                        ins.then_inc(exp_done, 1)

                def turned_weights(i):
                    e, i0 = st.items[i], k0 + i
                    act.wait_ge(pt_done, i0 + 1)
                    act.wait_ge(pv_done, i0 - 1)
                    nc.scalar.activation(prob_t[:, i0 % 2, 0:e["nk"]], ps[:, 2 + i0 % 2, 0:e["nk"]], ACT.Copy)\
                        .then_inc(pt_saved, 1)

                def output(i):
                    e, i0 = st.items[i], k0 + i
                    if st.mode == "mlstm":
                        act.wait_ge(pv_done, i0 + 1)
                        nc.scalar.activation(e["dst"], ps[:, 2 + i0 % 2, 0:P], ACT.Copy).then_inc(ml_saved, 1)
                    elif e["hh"]:
                        pr, t = e["y"]
                        act.wait_ge(pv_done, i0 + 1)
                        nc.scalar.activation(y_hi[:, pr, t * P:(t + 1) * P], ps[:, 4 + (st.at["pair"] + i // 2) % 2, 0:P],
                                             ACT.Copy).then_inc(y_hi_done, 1)

                for i in range(n + 3):
                    if i < n:
                        weights(i)
                    if 2 <= i <= n + 1:
                        turned_weights(i - 2)
                    if i >= 3:
                        output(i - 3)

            for st in plan:
                if st.kind == "segment":
                    stream(st.seg)
                elif st.kind == "overflow":
                    most = act.value_load(st.seg.flag, min_val=0, max_val=T)
                    with act.If(most > P):
                        stream(st.seg)
                elif st.kind == "barrier":
                    act.drain().then_inc(at_barrier, 1)
                    act.wait_ge(at_barrier, 4 * (st.at["barrier"] + 1))
                elif st.kind == "norm":
                    for t in range(st.tiles):
                        ins = nc.scalar.activation(XN[:, t, :], x_tm[:, t, :], ACT.Square, accum_out=small[:, t:t + 1])
                    settled(ins)
                    root(st.tiles, D)
                elif st.kind == "post":
                    for t in range(st.nq):
                        ins = nc.scalar.activation(ps[:, 4 + 2 * (t % 2):6 + 2 * (t % 2), :].rearrange("p b n -> p (b n)"), st.o[:, t, :],
                                                   ACT.Square, accum_out=small[:, t:t + 1])
                        if t % 2:
                            settled(ins)
                    root(st.nq, D)
                elif st.kind == "ml_norm":
                    act.wait_ge(sums_done, st.at["sum"] + 1)
                    root(st.nq * ML_H, ML_D)
                elif st.kind == "turn":
                    for i, (src, gain, shift, hi, lo) in enumerate(st.items):
                        i0 = st.at["turn"] + i
                        act.wait_ge(value_ready, i0 + 1)
                        nc.scalar.activation(hi, turn_value[:, i0 % 2, :].rearrange("p (c t) -> p c t", t=P), ACT.Copy)\
                            .then_inc(split_hi_done, 1)
                elif st.kind == "turn_heads":
                    for i, (src, dst) in enumerate(st.jobs):
                        act.wait_ge(stage_pe, st.at["pe"] + i + 1)
                        nc.scalar.activation(dst, ps[:, i % 4, 0:len(src) * P].rearrange("p (c t) -> p c t", t=P), ACT.Copy)\
                            .then_inc(stage_act, 1)
                elif st.kind == "attend":
                    attend(st)
                elif st.kind == "route":
                    act.wait_ge(stage_dve, st.at["d"] + 1)
                    nc.scalar.activation(st.route[:, :, 49:50], st.route[:, :, 48:49], ACT.Exp).then_inc(stage_act, 1)

        @block.vector
        def _(dve):
            steps = [0]

            def settled(ins):
                steps[0] += 1
                ins.then_inc(dve_step, 1)
                dve.wait_ge(dve_step, steps[0])

            dve.wait_ge(params_loaded, PARAMS)
            dve.wait_ge(constants_set, 1)
            dve.wait_ge(split_hi_done, START["turn"] + 1)
            silu_c = small[:, 104:104 + 2 * DC].rearrange("p (c s) -> p c s", s=2)
            settled(nc.vector.tensor_tensor(c_split[:, :, 2:4], silu_c, c_split[:, :, 0:2].bitcast(F32), ALU.subtract))

            def split(seg, it, j):
                q, k, m, opens, closes, width, source = seg.units[j]
                n = m * width
                dve.wait_ge(seg.sig.hi_ready, seg.unit(it, j) + 1)
                dve.wait_ge(seg.sig.units_used, seg.unit(it, j) - HL + 1)
                slot, half = seg.slot(it, j, RAW), seg.slot(it, j, HL)
                nc.vector.tensor_tensor(w_lo[:, half, 0:n], raw[:, slot, 0:n], w_hi[:, half, 0:n].bitcast(F32),
                                        ALU.subtract).then_inc(seg.sig.lo_ready, 1)

            def save(seg, it, j):
                q, k, m, opens, closes, width, source = seg.units[j]
                if not closes or seg.evac in ("fm", "tm", "rows") or q < 0:
                    return
                r = seg.result(it, q)
                b = 4 * (q % 2)
                if seg.evac == "residual":
                    dve.wait_ge(seg.sig.units_used, seg.unit(it, j) + 1)
                    x = x_tm[:, 0:seg.tiles, q * NT:(q + 1) * NT]
                    nc.vector.tensor_tensor(x, ps[:, b:b + seg.tiles, :], x, ALU.add).then_inc(seg.sig.results_saved, 1)
                elif seg.evac == "merge":
                    if q % 2 == 0:
                        return
                    dve.wait_ge(seg.sig.results_saved, r)
                    dve.wait_ge(seg.sig.units_used, seg.unit(it, j) + 1)
                    dst = merged[:, 0:seg.tiles, (q // 2) * NT:(q // 2 + 1) * NT]
                    g = seg.gates[:, 0:seg.tiles, :]
                    if seg.n_branch == 0:
                        nc.vector.tensor_tensor(dst, ps[:, b:b + seg.tiles, :], g, ALU.mult).then_inc(seg.sig.results_saved, 1)
                    else:
                        settled(nc.vector.tensor_tensor(g, ps[:, b:b + seg.tiles, :], g, ALU.mult))
                        nc.vector.tensor_tensor(dst, dst, g, ALU.add).then_inc(seg.sig.results_saved, 1)
                elif seg.evac == "ml_gate":
                    dve.wait_ge(gate_ready, seg.at["gate"] + 1)
                    nc.vector.tensor_tensor(seg.dst, seg.dst, seg.gates[:, 0:seg.tiles, :]
                                            .rearrange("p t (h e) -> p t h e", e=ML_D), ALU.mult).then_inc(seg.sig.results_saved, 1)
                elif seg.evac == "experts":
                    if q % 2 == 0 or q >= DOWN:
                        return
                    n = seg.units[j][5]
                    dve.wait_ge(seg.sig.results_saved, r)
                    dve.wait_ge(seg.sig.units_used, seg.unit(it, j) + 1)
                    dve.wait_ge(seg.ex.act_turned, 3 * it + (M + q // 2))
                    nc.vector.tensor_tensor(seg.buf["value"][:, 0:n], ps[:, b, 0:n], seg.buf["silu"][:, 0:n], ALU.mult)\
                        .then_inc(seg.sig.results_saved, 1)
                elif q >= FB:
                    dve.wait_ge(seg.sig.units_used, seg.unit(it, j) + 1)
                    half = slice((q - FB) * NT, (q - FB + 1) * NT)
                    src = ps[:, b:b + seg.tiles, :]
                    if seg.evac == "conv":
                        dst = seg.o[:, 0:seg.tiles, half]
                        ins = nc.vector.tensor_copy(dst, src) if it == 0 else nc.vector.tensor_tensor(dst, src, dst, ALU.add)
                    else:
                        dst = x_tm[:, 0:seg.tiles, half]
                        ins = nc.vector.tensor_tensor(dst, src, dst, ALU.add)
                    ins.then_inc(seg.sig.results_saved, 1)
                elif seg.evac == "swiglu":
                    v = seg.tmp[:, 2 + q % 2, 0:seg.N]
                    dve.wait_ge(taps_ready, it * FB + (seg.at["tap"] + q + 1))
                    nc.vector.tensor_tensor(v, ps[:, b + 1, 0:seg.N], seg.tmp[:, q % 2, 0:seg.N], ALU.mult)\
                        .then_inc(seg.sig.results_saved, 1)
                else:
                    for part in range(2):
                        c = it * FB + q + part * (COL_CONV // 2)
                        dve.wait_ge(taps_ready, 2 * (it * FB + q) + seg.at["tap"] + part + 1)
                        src = ps[:, b + part, 0:seg.N].rearrange("p (s t) -> p s t", t=T)
                        u = seg.tmp[:, 2 * (q % 2) + part, 0:seg.N].rearrange("p (s t) -> p s t", t=T)
                        settled(nc.vector.scalar_tensor_tensor(u[:, :, 1:T], src[:, :, 0:T - 1],
                                                               cols[:, seg.cw + c:seg.cw + c + 1], u[:, :, 1:T],
                                                               ALU.mult, ALU.add))
                        ins = nc.vector.scalar_tensor_tensor(u[:, :, 0:T - 1], src[:, :, 1:T],
                                                             cols[:, seg.cw + 2 * COL_CONV + c:seg.cw + 2 * COL_CONV + c + 1],
                                                             u[:, :, 0:T - 1], ALU.mult, ALU.add)
                    ins.then_inc(seg.sig.results_saved, 1)

            def save_late(seg, it, j):
                q, k, m, opens, closes, width, source = seg.units[j]
                if not closes or seg.mode != "ffn" or not 0 <= q < FB:
                    return
                n = it * FB + (seg.at["act"] + q)
                if seg.evac == "swiglu":
                    v = seg.tmp[:, 2 + q % 2, 0:seg.N]
                    dve.wait_ge(act_hi_done, n + 1)
                    nc.vector.tensor_tensor(act_lo[:, q * seg.N:(q + 1) * seg.N], v,
                                            act_hi[:, q * seg.N:(q + 1) * seg.N].bitcast(F32), ALU.subtract)\
                        .then_inc(act_done, 1)
                else:
                    dve.wait_ge(gate_ready, it * FB + q + seg.at["gate"] + 1)
                    v, g = seg.tmp[:, 2 * (q % 2), 0:seg.N], seg.tmp[:, 2 * (q % 2) + 1, 0:seg.N]
                    nc.vector.tensor_tensor(v, v, g, ALU.mult).then_inc(act_value, 1)
                    dve.wait_ge(act_hi_done, n + 1)
                    nc.vector.tensor_tensor(act_lo[:, q * seg.N:(q + 1) * seg.N], v,
                                            act_hi[:, q * seg.N:(q + 1) * seg.N].bitcast(F32), ALU.subtract)\
                        .then_inc(act_done, 1)

            def select(seg, e):
                dve.wait_ge(seg.ex.selt_turned, e + M)
                for t in range(TT):
                    ins = nc.vector.tensor_scalar(seg.buf["sel"][:, t, :], seg.buf["slot_no"][:, seg.half * P:(seg.half + 1) * P],
                                                  seg.route[:, t, bass.ds(e + PLACE, 1)], seg.route[:, t, bass.ds(e + TAKES, 1)],
                                                  ALU.is_equal, ALU.mult)
                ins.then_inc(seg.ex.sel_ready, 1)

            def gain(seg, e, half):
                dve.wait_ge(seg.ex.gathered, 2 * e + (M + half + 1))
                dve.wait_ge(seg.ex.xg_hi, 2 * e + (M + half - 1))
                dve.wait_ge(seg.ex.xg_done, 2 * e + (M + half - 1))
                nc.vector.tensor_tensor(turn_value[:, half, :].rearrange("p (c t) -> p c t", t=P),
                                        ps[:, 1 + half, :].rearrange("p (c t) -> p c t", t=P),
                                        seg.scale[:, 4 * half:4 * half + 4].unsqueeze(2).to_broadcast([P, 4, P]), ALU.mult)\
                    .then_inc(seg.ex.xg_value, 1)

            def lower_half(seg, e, half):
                dve.wait_ge(seg.ex.xg_hi, 2 * e + (M + half + 1))
                nc.vector.tensor_tensor(h_lo[:, 4 * half:4 * half + 4, T:T + P],
                                        turn_value[:, half, :].rearrange("p (c t) -> p c t", t=P),
                                        h_hi[:, 4 * half:4 * half + 4, T:T + P].bitcast(F32), ALU.subtract)\
                    .then_inc(seg.ex.xg_done, 1)

            def first_tokens(seg):
                select(seg, 0)
                for half in range(2):
                    gain(seg, 0, half)
                for half in range(2):
                    lower_half(seg, 0, half)

            def accumulate(seg, e, half):
                dve.wait_ge(seg.ex.scattered, 2 * e + (M + half + 1))
                dve.wait_ge(seg.ex.accumulated, 2 * e + (M + half))
                for t in range(TT):
                    dst = x_tm[:, t, half * NT:(half + 1) * NT]
                    ins = nc.vector.scalar_tensor_tensor(dst, ps[:, 6 + t, :], seg.route[:, t, bass.ds(e, 1)], dst, ALU.mult, ALU.add)
                ins.then_inc(seg.ex.accumulated, 1)

            def between(seg, it, j, first):
                if j == SCATTER[1] + 2 and not first:
                    accumulate(seg, it - 1, 1)
                for i, (f, n) in enumerate(GROUPS):
                    if j == TURN[i] + 2:
                        dve.wait_ge(seg.ex.act_hi_done, 3 * it + (M + i + 1))
                        nc.vector.tensor_tensor(act_lo[:, f:f + n], ps[:, 3, 0:n], act_hi[:, f:f + n].bitcast(F32), ALU.subtract)\
                            .then_inc(seg.ex.act_done, 1)
                if j == GATHER - 4:
                    select(seg, it + 1)
                for half in range(2):
                    if j == GATHER + 2 + half:
                        gain(seg, it + 1, half)
                    if j == GATHER + 4 + half:
                        lower_half(seg, it + 1, half)
                if j == SCATTER[0] + 2:
                    accumulate(seg, it, 0)

            def inverse_root(st, n):
                dve.wait_ge(root_done, st.at["root"] + 1)
                settled(nc.vector.reciprocal(small[:, 64:64 + n], small[:, 64:64 + n]))

            def head_norm(st, j):
                t, n = st.tiles, st.n
                w = n * HD

                def heads(i, h0=0, h1=n):
                    return st.src[:, i, h0 * HD:h1 * HD].rearrange("p (h d) -> p h d", d=HD)

                if 1 <= j <= t // TT:
                    pair = range(TT * (j - 1), TT * j)
                    if j > 1:
                        dve.wait_ge(dve_step, steps[0])
                    for i in pair:
                        ins = nc.vector.tensor_tensor(st.sq[:, i % TT, :], st.src[:, i, :], st.src[:, i, :], ALU.mult)
                    settled(ins)
                    ins = nc.vector.tensor_reduce(small[:, pair[0] * n:(pair[-1] + 1) * n],
                                                  st.sq.rearrange("p t (h d) -> p (t h) d", d=HD), AX.X, ALU.add)
                    if j == t // TT:
                        ins.then_inc(sums_done, 1)
                    else:
                        settled(ins)
                if j == 4:
                    inverse_root(st, t * n)
                if 4 <= j < 4 + t // TT:
                    for i in range(TT * (j - 4), TT * (j - 3)):
                        ins = nc.vector.tensor_tensor(heads(i), heads(i), small[:, 64 + i * n:64 + (i + 1) * n].unsqueeze(2)
                                                      .to_broadcast([P, n, HD]), ALU.mult)
                    settled(ins)
                if 6 <= j < 6 + t // TT:
                    for i in range(TT * (j - 6), TT * (j - 5)):
                        for h0, h1, g, scale in st.parts:
                            ins = nc.vector.scalar_tensor_tensor(heads(i, h0, h1), heads(i, h0, h1), scale,
                                                                 g_rows[:, g:g + 1, :].to_broadcast([P, h1 - h0, HD]), ALU.mult, ALU.mult)
                    settled(ins)
                if 8 <= j < 8 + TT and st.rope:
                    i = j - 8
                    quarters = st.src[:, i, :].rearrange("p (h r s e) -> p h r s e", h=n, r=2, s=2)
                    out_q = st.sq[:, i, :].rearrange("p (h r s e) -> p h r s e", h=n, r=2, s=2)
                    sin_q = rope_sin[:, i:i + 1, :].rearrange("p o (r s e) -> p o r s e", r=2, s=2)
                    for s in range(2):
                        ins = nc.vector.tensor_tensor(out_q[:, :, :, s, :], quarters[:, :, :, 1 - s, :],
                                                      sin_q[:, :, :, s, :].to_broadcast([P, n, 2, HD // 4]), ALU.mult)
                    settled(ins)
                    settled(nc.vector.tensor_tensor(heads(i), heads(i), rope_cos[:, i:i + 1, :].to_broadcast([P, n, HD]), ALU.mult))
                    settled(nc.vector.tensor_tensor(st.src[:, i, :], st.src[:, i, :], st.sq[:, i, :], ALU.add))
                if j == 10 and st.rope:
                    for side in range(2):
                        nc.vector.tensor_copy(st.kd[:, :, :, side, :], st.src[:, :, W_HEADS:].rearrange("p t (g d) -> p t g d", d=HD))
                if j == 8 and st.rows is not None:
                    u, lf, l, neg = (st.rows[0:NH, i, 0:T] for i in range(4))
                    dve.wait_ge(stage_act, st.at["a"] + 1)
                    settled(nc.vector.scalar_tensor_tensor(lf, u, 0.0, l, ALU.min, ALU.subtract))
                    settled(nc.vector.tensor_tensor_scan(l, ones[0:NH, 0:1].to_broadcast([NH, T]), lf, 0.0, ALU.mult, ALU.add))
                    nc.vector.tensor_scalar(neg, l, -1.0, None, ALU.mult)

            def ml_rows(st, j):
                n = 4 * ML_H
                if j == 1:
                    u, l, lf = st.rows[0:n, 0, :], st.arows[0:n, 0, :], st.rows[0:n, 1, :]
                    dve.wait_ge(stage_act, st.at["a"] + 1)
                    nc.vector.scalar_tensor_tensor(lf, u, 0.0, l, ALU.min, ALU.subtract).then_inc(stage_dve, 1)
                if j == 4:
                    dve.wait_ge(stage_pe, st.at["pe"] + 1)
                if j in (4, 5):
                    d = j - 4
                    one = ones[0:ML_H, 0:1].to_broadcast([ML_H, T])
                    ig, fg = ps[0:ML_H, KINDS[2 * d], :], ps[0:ML_H, KINDS[2 * d + 1], :]
                    b, m, av = st.d[0:ML_H, d, :], st.d[0:ML_H, 2 + d, :], st.arows[0:ML_H, d, :]
                    ctx_, x_ = (slice(T, 2 * T), slice(0, T))
                    step = -1 if d else 1
                    carry = slice(T, T + 1) if d else slice(2 * T - 1, 2 * T)
                    settled(nc.vector.tensor_tensor_scan(b[:, ctx_][:, ::step], one, fg[:, ctx_][:, ::step], 0.0,
                                                         ALU.mult, ALU.add))
                    settled(nc.vector.tensor_tensor_scan(b[:, x_][:, ::step], one, fg[:, x_][:, ::step], b[:, carry],
                                                         ALU.mult, ALU.add))
                    settled(nc.vector.tensor_tensor(av, ig, b, ALU.subtract))
                    settled(nc.vector.tensor_tensor_scan(m[:, ctx_][:, ::step], av[:, ctx_][:, ::step], av[:, ctx_][:, ::step],
                                                         0.0, ALU.max, ALU.max))
                    settled(nc.vector.tensor_tensor_scan(m[:, x_][:, ::step], av[:, x_][:, ::step], av[:, x_][:, ::step],
                                                         m[:, carry], ALU.max, ALU.max))
                    ins = nc.vector.tensor_tensor(b, b, m, ALU.add)
                    if d:
                        ins.then_inc(stage_dve, 1)
                    else:
                        settled(ins)
                if j == 7:
                    av = st.arows[0:ML_H, :, :]
                    settled(nc.vector.tensor_copy(ml_hi, av))
                    nc.vector.tensor_tensor(ml_lo, av, ml_hi.bitcast(F32), ALU.subtract)

            def aside(seg, st, j):
                if st.kind == "head_norm":
                    head_norm(st, j)
                else:
                    ml_rows(st, j)

            def stream(seg):
                def body(it, before, first):
                    for j in range(seg.n):
                        if not first or j >= AHEAD:
                            split(seg, it, j)
                        if j >= AHEAD:
                            save(seg, it, j - AHEAD)
                        elif not first:
                            save(seg, before, seg.n + j - AHEAD)
                        if j > AHEAD:
                            save_late(seg, it, j - AHEAD - 1)
                        if seg.mode == "moe":
                            between(seg, it, j, first)
                        if seg.aside is not None:
                            aside(seg, seg.aside, j)

                if seg.first:
                    for j in range(AHEAD):
                        split(seg, 0, j)
                if seg.mode == "moe":
                    first_tokens(seg)
                body(0, None, True)
                if seg.iters > 2:
                    with dve.Fori(1, seg.iters) as it:
                        body(it, it - 1, False)
                elif seg.iters == 2:
                    body(1, 0, False)
                for j in range(AHEAD):
                    if seg.next:
                        split(seg.next, 0, j)
                    save(seg, seg.iters - 1, seg.n + j - AHEAD)
                if seg.mode == "moe":
                    accumulate(seg, seg.iters - 1, 1)

            def attend(st):
                k0 = st.at["item"]
                n = len(st.items)

                def begin(i):
                    e, i0 = st.items[i], k0 + i
                    nk = e["nk"]
                    z = ps[:, i0 % 2, 0:nk]
                    if st.mode == "soft":
                        dve.wait_ge(scores_done, i0 + 1)
                        dve.wait_ge(exp_done, i0 - 1)
                        nc.vector.tensor_reduce(small[:, i0 % 2:i0 % 2 + 1], z, AX.X, ALU.max, negate=True).then_inc(max_done, 1)
                    elif st.mode == "stick":
                        dve.wait_ge(scores_done, i0 + 1)
                        dve.wait_ge(exp_done, i0 - 1)
                        nc.vector.scalar_tensor_tensor(st.tmp[:, i0 % 2, 0:nk], z, -BOUND, e["cap"], ALU.max, ALU.min)\
                            .then_inc(bounded, 1)

                def finish(i):
                    e, i0 = st.items[i], k0 + i
                    nk = e["nk"]
                    w = prob[:, i0 % 2, 0:nk]
                    dve.wait_ge(exp_done, i0 + 1)
                    if st.mode == "soft":
                        inv = small[:, 4 + i0 % 2:5 + i0 % 2]
                        settled(nc.vector.reciprocal(inv, small[:, 2 + i0 % 2:3 + i0 % 2]))
                        nc.vector.tensor_scalar(w, w, inv, None, ALU.mult).then_inc(probs_done, 1)
                    elif st.mode == "stick":
                        keep, beta = st.tmp[:, 2 + i0 % 2, 0:nk], st.tmp[:, 4 + i0 % 2, 0:nk]
                        tail = st.tmp[:, 6:8, :].rearrange("p a b -> p (a b)")[:, T - nk:T + 1]
                        settled(nc.vector.reciprocal(beta, beta))
                        settled(nc.vector.tensor_tensor(keep, keep, beta, ALU.mult))
                        settled(nc.vector.tensor_tensor_scan(tail[:, 0:nk][:, ::-1], keep[:, ::-1],
                                                             ones[:, 0:1].to_broadcast([P, nk]), 1.0, ALU.mult, ALU.mult))
                        dve.wait_ge(pt_done, i0 - 1)
                        nc.vector.tensor_tensor(w, beta, tail[:, 1:nk + 1], ALU.mult).then_inc(probs_done, 1)
                    else:
                        z = ps[:, i0 % 2, 0:nk]
                        den, inv = small[:, 0:2], small[:, 4:6]
                        for d in range(2):
                            s = st.decay[:, i0 % 2, d, 0:nk]
                            settled(nc.vector.scalar_tensor_tensor(s, z, 1.0, s, ALU.mult, ALU.mult, accum_out=den[:, d:d + 1]))
                        settled(nc.vector.scalar_tensor_tensor(inv, den, -1.0, den, ALU.mult, ALU.max))
                        settled(nc.vector.tensor_tensor(inv, inv, st.mcols[:, e["t"], 0:2, e["h"]], ALU.max))
                        settled(nc.vector.reciprocal(inv, inv))
                        s = st.decay[:, i0 % 2, 0, 0:nk]
                        settled(nc.vector.tensor_scalar(s, s, inv[:, 0:1], None, ALU.mult))
                        dve.wait_ge(pt_done, i0 - 1)
                        nc.vector.scalar_tensor_tensor(w, st.decay[:, i0 % 2, 1, 0:nk], inv[:, 1:2], s, ALU.mult, ALU.add)\
                            .then_inc(probs_done, 1)

                def output(i):
                    e, i0 = st.items[i], k0 + i
                    if st.mode != "mlstm" and e["hh"]:
                        pr, t = e["y"]
                        pair = st.at["pair"] + i // 2
                        dve.wait_ge(y_hi_done, pair + 1)
                        nc.vector.tensor_tensor(y_lo[:, pr, t * P:(t + 1) * P], ps[:, 4 + pair % 2, 0:P],
                                                y_hi[:, pr, t * P:(t + 1) * P].bitcast(F32), ALU.subtract).then_inc(y_saved, 1)

                if st.mode == "stick":
                    settled(nc.vector.memset(st.tmp[:, 7, 0:1], 1.0))
                for i in range(n + 3):
                    if i < n:
                        begin(i)
                    if 1 <= i <= n:
                        finish(i - 1)
                    if i >= 3:
                        output(i - 3)

            def route(st):
                r = st.route
                dve.wait_ge(stage_pe, st.at["pe"] + 1)
                settled(nc.vector.tensor_copy(r[:, :, 16:24], ps[:, 0, 0:TT * N_EXP].rearrange("p (t e) -> p t e", e=N_EXP)))
                for t in range(TT):
                    settled(nc.vector.max(r[:, t, 24:32], r[:, t, 16:24]))
                    settled(nc.vector.max_index(r[:, t, 32:40].bitcast(U32), r[:, t, 24:32], r[:, t, 16:24]))
                    settled(nc.vector.tensor_copy(r[:, t, 40:48], r[:, t, 32:40].bitcast(U32)))
                nc.vector.tensor_tensor(r[:, :, 48:49], r[:, :, 25:26], r[:, :, 24:25], ALU.subtract).then_inc(stage_dve, 1)
                dve.wait_ge(stage_act, st.at["a"] + 1)
                settled(nc.vector.tensor_scalar(r[:, :, 50:51], r[:, :, 49:50], 1.0, None, ALU.add))
                settled(nc.vector.reciprocal(r[:, :, 50:51], r[:, :, 50:51]))
                settled(nc.vector.tensor_tensor(r[:, :, 51:52], r[:, :, 49:50], r[:, :, 50:51], ALU.mult))
                settled(nc.vector.memset(r[:, :, PLACE:PLACE + 32], 0.0))
                for t in range(TT):
                    for c in range(2):
                        nc.vector.tensor_scalar(r[:, t, 8 * c:8 * c + 8], expert_no[:, :], r[:, t, 40 + c:41 + c],
                                                r[:, t, 50 + c:51 + c], ALU.is_equal, ALU.mult)
                        ins = nc.vector.tensor_scalar(r[:, t, 16 + 8 * c:24 + 8 * c], expert_no[:, :], r[:, t, 40 + c:41 + c], None,
                                                      ALU.is_equal)
                settled(ins)
                nc.vector.tensor_tensor(r[:, :, TAKES:TAKES + 8], r[:, :, 16:24], r[:, :, 24:32], ALU.add)
                settled(nc.vector.tensor_tensor(r[:, :, 0:8], r[:, :, 0:8], r[:, :, 8:16], ALU.add))
                nc.vector.tensor_scalar(st.buf["upto"], anti[:, 0, 0:P].bitcast(F32), 0.0, None, ALU.is_equal)
                settled(nc.vector.memset(st.buf["sel"], 1.0))
                nc.vector.tensor_tensor_scan(st.buf["slot_no"], st.buf["sel"].rearrange("p t n -> p (t n)"),
                                             st.buf["sel"].rearrange("p t n -> p (t n)"), 0.0, ALU.mult, ALU.add)\
                    .then_inc(stage_dve, 1)
                dve.wait_ge(stage_pe, st.at["pe"] + 2)
                nc.vector.tensor_copy(r[:, :, PLACE:PLACE + 8], ps[:, 1, 0:TT * N_EXP].rearrange("p (t e) -> p t e", e=N_EXP))
                settled(nc.vector.tensor_reduce(r[0:1, 0, 48:49], ps[0:1, 2, 0:N_EXP], AX.X, ALU.max))
                nc.vector.tensor_copy(st.buf["flag"], r[0:1, 0, 48:49]).then_inc(stage_dve, 1)

            def mod_cols(st):
                dve.wait_ge(stage_pe, st.at["pe"] + 1)
                n = MOD_W // P
                bc = col_second(st.l, "b_mod")
                parts = ps[:, 0, 0:4 * n].rearrange("p (b s) -> p b s", s=4)
                settled(nc.vector.tensor_tensor(mod[:, :, :], parts[:, :, 0:2], cols[:, bc:bc + n].unsqueeze(2).to_broadcast([P, n, 2]),
                                                ALU.add))
                settled(nc.vector.tensor_tensor(mod[:, :, :], parts[:, :, 2:4], mod[:, :, :], ALU.add))
                for i, (pre, post) in enumerate((("g_pre_mix", "g_post_mix"), ("g_pre_ffn", "g_post_ffn"))):
                    at = 3 * i * DC
                    g = cols[:, col_second(st.l, pre):][:, 0:DC].unsqueeze(2).to_broadcast([P, DC, 2])
                    nc.vector.scalar_tensor_tensor(mod_gain[:, i, :, :], mod[:, at + DC:at + 2 * DC, :], 1.0, g, ALU.add, ALU.mult)
                    g = cols[:, col_second(st.l, post):][:, 0:DC].unsqueeze(2).to_broadcast([P, DC, 2])
                    nc.vector.tensor_tensor(mod_post[:, i, :, :], mod[:, at + 2 * DC:at + 3 * DC, :], g, ALU.mult)

            def post(st):
                for s in range(2):
                    for c in range(DC):
                        ins = nc.vector.tensor_scalar(st.diag[:, s, c, :], ident[:, :], mod_post[:, st.which, c, s:s + 1], None,
                                                      ALU.mult)
                ins.then_inc(stage_dve, 1)
                dve.wait_ge(stage_pe, st.at["pe"] + 1)
                inverse_root(st, st.nq)
                for t in range(st.nq):
                    s = t // TT
                    gain = ps[:, 2 * s:2 * s + 2, :].rearrange("p b n -> p (b n)")
                    settled(nc.vector.scalar_tensor_tensor(st.o[:, t, :], st.o[:, t, :], small[:, 64 + t:65 + t], gain,
                                                           ALU.mult, ALU.mult))
                    nc.vector.tensor_tensor(x_tm[:, t, :], x_tm[:, t, :], st.o[:, t, :], ALU.add)

            def ml_norm(st):
                n = ML_H * st.nq
                settled(nc.vector.tensor_tensor(st.sq, st.mh, st.mh, ALU.mult))
                nc.vector.tensor_reduce(small[:, 0:n], st.sq.rearrange("p h t e -> p (h t) e"), AX.X, ALU.add).then_inc(sums_done, 1)
                inverse_root(st, n)
                rs = small[:, 64:64 + n].rearrange("p (h t) -> p h t", t=st.nq).unsqueeze(3).to_broadcast([P, ML_H, st.nq, ML_D])
                nc.vector.tensor_tensor(st.mh, st.mh, rs, ALU.mult)

            for st in plan:
                if st.kind == "segment":
                    stream(st.seg)
                elif st.kind == "overflow":
                    most = dve.value_load(st.seg.flag, min_val=0, max_val=T)
                    with dve.If(most > P):
                        stream(st.seg)
                elif st.kind == "barrier":
                    dve.drain().then_inc(at_barrier, 1)
                    dve.wait_ge(at_barrier, 4 * (st.at["barrier"] + 1))
                elif st.kind == "norm":
                    inverse_root(st, st.tiles)
                    for t in range(st.tiles):
                        nc.vector.tensor_scalar(XN[:, t, :], x_tm[:, t, :], small[:, 64 + t:65 + t], None, ALU.mult)
                elif st.kind == "turn":
                    def value(i):
                        src, gain, shift, hi, lo = st.items[i]
                        i0 = st.at["turn"] + i
                        v = turn_value[:, i0 % 2, :].rearrange("p (c t) -> p c t", t=P)
                        t_ = ps[:, i0 % 4, :].rearrange("p (c t) -> p c t", t=P)
                        dve.wait_ge(turned, i0 + 1)
                        dve.wait_ge(split_done, i0 - 1)
                        if gain is None:
                            ins = nc.vector.tensor_copy(v, t_)
                        else:
                            ins = nc.vector.tensor_tensor(v, t_, gain.unsqueeze(2).to_broadcast([P, 4, P]), ALU.mult)
                            if shift is not None:
                                settled(ins)
                                ins = nc.vector.tensor_tensor(v, v, shift.unsqueeze(2).to_broadcast([P, 4, P]), ALU.add)
                        ins.then_inc(value_ready, 1)

                    def lower(i):
                        src, gain, shift, hi, lo = st.items[i]
                        i0 = st.at["turn"] + i
                        dve.wait_ge(split_hi_done, i0 + 2)
                        nc.vector.tensor_tensor(lo, turn_value[:, i0 % 2, :].rearrange("p (c t) -> p c t", t=P),
                                                hi.bitcast(F32), ALU.subtract).then_inc(split_done, 1)

                    for i in range(len(st.items) + 1):
                        if i < len(st.items):
                            value(i)
                        if i:
                            lower(i - 1)
                elif st.kind == "attend":
                    attend(st)
                elif st.kind in ("route", "mod_cols", "post", "ml_norm"):
                    {"route": route, "mod_cols": mod_cols, "post": post,
                     "ml_norm": ml_norm}[st.kind](st)

        @block.tensor
        def _(pe):
            pe.wait_ge(params_loaded, PARAMS)
            pe.wait_ge(constants_set, 1)
            mm = nc.tensor.matmul

            def use(seg, it, j, first):
                q, k, m, opens, closes, width, source = seg.units[j]
                b = 4 * (q % 2) if q >= 0 else 2 + q % 2
                if opens and q < 0:
                    pe.wait_ge(mod_saved, seg.at["mod"] + it * MOD_RESULTS - q - 2)
                elif opens:
                    if q == seg.down + 1 and seg.mod_rows is not None:
                        pe.wait_ge(mod_saved, seg.at["mod"] + (it + 1) * seg.mods)
                    alternates = q > 0 or seg.results % 2 == 0 and not first
                    pe.wait_ge(seg.sig.results_saved, seg.result(it, q) - (1 if alternates else 0))
                if seg.mode == "moe" and q == 0 and opens:
                    pe.wait_ge(seg.ex.xg_done, 2 * it + (M + 2))
                if seg.mode == "moe" and q == DOWN:
                    pe.wait_ge(seg.ex.act_done, 3 * it + (M + (k + m + 3) // 4))
                if seg.mode == "ffn" and q == FB:
                    pe.wait_ge(act_done, it * FB + (seg.at["act"] + k + m))
                pe.wait_ge(seg.sig.hi_ready, seg.unit(it, j) + 1)
                half = seg.slot(it, j, HL)
                wh, wl = w_hi[:, half, :], w_lo[:, half, :]
                for w in (wh, wl):
                    upper = w is wh
                    if not upper:
                        ins.then_inc(seg.sig.hi_used, 1)
                        pe.wait_ge(seg.sig.lo_ready, seg.unit(it, j) + 1)
                    if q < 0:
                        for c in range(m):
                            ins = mm(ps[0:4, b, :], c_split[:, k + c, :], w[:, c * width:(c + 1) * width],
                                     start=upper and opens and c == 0, stop=not upper and closes and c == m - 1)
                    elif seg.mode == "fm" or seg.mode == "ffn" and q < FB:
                        ah, al = seg.A
                        wide = min(width, P)
                        for f in range(width // wide):
                            bank = b + f if seg.mode == "fm" else b + (0 if opens else 1)
                            dst = ps[0:wide, bank, 0:seg.N]
                            for c in range(m):
                                f0 = c * width + f * P
                                for x in ((ah, al) if upper else (ah,)):
                                    ins = mm(dst, w[:, f0:f0 + wide], x[:, k + c, 0:seg.N], start=upper and k + c == 0 and x is ah,
                                             stop=not upper and k + c == DC - 1)
                    else:
                        branch = seg.evac == "merge" and q % 2
                        biased = seg.evac == "merge" and not branch and seg.bias_layer is not None
                        for t in range(seg.tiles):
                            dst = ps[:, b + t, 0:width]
                            for c in range(m):
                                if q >= seg.down:
                                    at = (k + c) * seg.N + t * P
                                    xh, xl = act_hi[:, at:at + P], act_lo[:, at:at + P]
                                else:
                                    ah, al = seg.B if branch else seg.A
                                    xh, xl = ah[:, k + c, t * P:(t + 1) * P], al[:, k + c, t * P:(t + 1) * P]
                                last = not upper and closes and c == m - 1
                                for x in ((xh, xl) if upper else (xh,)):
                                    ins = mm(dst, x, w[:, c * width:(c + 1) * width], start=upper and opens and c == 0 and x is xh,
                                             stop=last and not biased)
                                if last and biased:
                                    row = 4 * seg.bias_layer + 2 * seg.n_branch + q // 2
                                    ins = mm(dst, row_of[:, row, :], bias_rows[:, :], start=False, stop=True)
                ins.then_inc(seg.sig.units_used, 1)

            def gather(seg, e, half):
                pe.wait_ge(seg.ex.sel_ready, e + (M + 1))
                pe.wait_ge(seg.ex.xg_value, 2 * e + (M + half - 1))
                for c in range(4):
                    d0 = (4 * half + c) * P
                    for t in range(TT):
                        ins = mm(ps[:, 1 + half, c * P:(c + 1) * P], seg.buf["tokens"][:, t, d0:d0 + P], seg.buf["sel"][:, t, :],
                                 start=t == 0, stop=t == TT - 1)
                ins.then_inc(seg.ex.gathered, 1)

            def scatter(seg, e, half):
                pe.wait_ge(seg.sig.results_saved, seg.result(e, DOWN + half) + 1)
                pe.wait_ge(seg.ex.selt_saved, e + (M + 1))
                pe.wait_ge(seg.ex.accumulated, 2 * e + (M + half))
                for t in range(TT):
                    ins = mm(ps[:, 6 + t, :], seg.buf["sel_t"][:, t * P:(t + 1) * P], seg.buf["y"][:, half, :], start=True, stop=True)
                ins.then_inc(seg.ex.scattered, 1)

            def between(seg, it, j, first):
                if j == SCATTER[1] and not first:
                    scatter(seg, it - 1, 1)
                if j == SEL_T:
                    pe.wait_ge(seg.ex.selt_saved, it + M)
                    for t in range(TT):
                        ins = nc.tensor.transpose(ps[:, 5, t * P:(t + 1) * P], seg.buf["sel"][:, t, :], ident[:, :])
                    ins.then_inc(seg.ex.selt_turned, 1)
                for i, (f, n) in enumerate(GROUPS):
                    if j == TURN[i]:
                        pe.wait_ge(seg.sig.results_saved, seg.result(it, 2 * i + 1) + 1)
                        pe.wait_ge(seg.ex.act_done, 3 * it + (M + i))
                        for c in range(n // P):
                            ins = nc.tensor.transpose(ps[:, 3, c * P:(c + 1) * P], seg.buf["value"][:, c * P:(c + 1) * P], ident[:, :])
                        ins.then_inc(seg.ex.act_turned, 1)
                for half in range(2):
                    if j == GATHER + half:
                        gather(seg, it + 1, half)
                if j == SCATTER[0]:
                    scatter(seg, it, 0)

            def aside(seg, st, j):
                if st.kind == "ml_rows" and j == 2:
                    n = 4 * ML_H
                    pe.wait_ge(stage_dve, st.at["d"] + 1)
                    for kind in range(4):
                        ins = mm(ps[0:ML_H, KINDS[kind], :], ident[0:n, kind * ML_H:(kind + 1) * ML_H], st.rows[0:n, kind % 2, :],
                                 start=True, stop=True)
                    ins.then_inc(stage_pe, 1)
                if st.kind == "ml_rows" and j == 6:
                    pe.wait_ge(stage_dve, st.at["d"] + 2)
                    for t in range(2 * TT):
                        for kind in range(4):
                            at = (t * 4 + kind) * ML_H
                            ins = nc.tensor.transpose(ps[:, 6, at:at + ML_H], st.d[0:ML_H, kind, t * P:(t + 1) * P],
                                                      ident[0:ML_H, 0:ML_H])
                    ins.then_inc(stage_pe, 1)

            def stream(seg):
                def body(it, first):
                    for j in range(seg.n):
                        use(seg, it, j, first)
                        if seg.mode == "moe":
                            between(seg, it, j, first)
                        if seg.aside is not None:
                            aside(seg, seg.aside, j)

                if seg.mode == "moe":
                    for half in range(2):
                        gather(seg, 0, half)
                body(0, True)
                if seg.iters > 2:
                    with pe.Fori(1, seg.iters) as it:
                        body(it, False)
                elif seg.iters == 2:
                    body(1, False)
                if seg.mode == "moe":
                    scatter(seg, seg.iters - 1, 1)

            def attend(st):
                k0 = st.at["item"]
                n = len(st.items)

                def scores(i):
                    e, i0 = st.items[i], k0 + i
                    nk = e["nk"]
                    if st.mode == "mlstm":
                        pe.wait_ge(probs_done, i0 - 1)
                        pe.wait_ge(exp_done, i0 - 1)
                        for d in range(2):
                            dst = ps[:, 4 + 2 * (i0 % 2) + d, :]
                            row = row_of_r[:, e["h"], :]
                            for c in range(nk // T):
                                keys = slice(e["k0"] + c * T, e["k0"] + (c + 1) * T)
                                mm(dst[:, c * T:(c + 1) * T], row, ml_hi[:, d, keys], start=True, stop=False)
                                mm(dst[:, c * T:(c + 1) * T], row, ml_lo[:, d, keys], start=False, stop=c > 0)
                                if c == 0:
                                    mm(dst[:, 0:T], ident_r[:, :], e["masks"][d], start=False, stop=True)
                        mm(ps[:, i0 % 2, 0:nk], e["q"], e["k"], start=True, stop=True).then_inc(scores_done, 1)
                        return
                    pe.wait_ge(exp_done, i0 - 1)
                    n_add = T if e["add"] and nk > T else nk
                    ins = mm(ps[:, i0 % 2, 0:n_add], e["q"], e["k"][:, 0:n_add], start=True, stop=not e["add"])
                    for j, (lhs, rhs, ready) in enumerate(e["add"]):
                        if ready is not None:
                            pe.wait_ge(bias_ready, ready)
                        ins = mm(ps[:, i0 % 2, 0:n_add], lhs, rhs, start=False, stop=j == len(e["add"]) - 1)
                    if n_add < nk:
                        ins = mm(ps[:, i0 % 2, n_add:nk], e["q"], e["k"][:, n_add:nk], start=True, stop=True)
                    ins.then_inc(scores_done, 1)

                def turn(i):
                    e, i0 = st.items[i], k0 + i
                    pe.wait_ge(probs_done, i0 + 1)
                    pe.wait_ge(pt_saved, i0 - 1)
                    if st.mode == "mlstm":
                        pe.wait_ge(ml_saved, st.at["ml"] + i - 1)
                    for c in range(e["nk"] // P):
                        ins = nc.tensor.transpose(ps[:, 2 + i0 % 2, c * P:(c + 1) * P], prob[:, i0 % 2, c * P:(c + 1) * P],
                                                  ident[:, :])
                    ins.then_inc(pt_done, 1)

                def gather(i):
                    e, i0 = st.items[i], k0 + i
                    chunks = e["nk"] // P
                    pe.wait_ge(pt_saved, i0 + 1)
                    if st.mode == "mlstm":
                        for c in range(chunks):
                            ins = mm(ps[:, 2 + i0 % 2, 0:P], prob_t[:, i0 % 2, c * P:(c + 1) * P], e["v"][c],
                                     start=c == 0, stop=c == chunks - 1)
                    else:
                        pair = st.at["pair"] + i // 2
                        if not e["hh"]:
                            pe.wait_ge(y_saved, pair - 1)
                        for c in range(chunks):
                            ins = mm(ps[e["hh"] * HD:(e["hh"] + 1) * HD, 4 + pair % 2, 0:P], e["v"][c],
                                     prob_t[:, i0 % 2, c * P:(c + 1) * P], start=c == 0, stop=c == chunks - 1)
                    ins.then_inc(pv_done, 1)

                for i in range(n + 3):
                    if i < n:
                        scores(i)
                    if 2 <= i <= n + 1:
                        turn(i - 2)
                    if i >= 3:
                        gather(i - 3)

            for st in plan:
                if st.kind == "segment":
                    stream(st.seg)
                elif st.kind == "overflow":
                    most = pe.value_load(st.seg.flag, min_val=0, max_val=T)
                    with pe.If(most > P):
                        stream(st.seg)
                elif st.kind == "barrier":
                    pe.drain().then_inc(at_barrier, 1)
                    pe.wait_ge(at_barrier, 4 * (st.at["barrier"] + 1))
                elif st.kind == "turn":
                    for i, (src, gain, shift, hi, lo) in enumerate(st.items):
                        i0 = st.at["turn"] + i
                        pe.wait_ge(value_ready, i0 - 3)
                        for c in range(4):
                            ins = nc.tensor.transpose(ps[:, i0 % 4, c * P:(c + 1) * P], src[c], ident[:, :])
                        ins.then_inc(turned, 1)
                elif st.kind == "turn_heads":
                    for i, (src, dst) in enumerate(st.jobs):
                        if i >= 4:
                            pe.wait_ge(stage_act, st.at["a"] + i - 3)
                        for c, s in enumerate(src):
                            ins = nc.tensor.transpose(ps[:, i % 4, c * P:(c + 1) * P], s, ident[:, :])
                        ins.then_inc(stage_pe, 1)
                elif st.kind == "attend":
                    attend(st)
                elif st.kind == "route":
                    for t in range(TT):
                        ins = nc.tensor.transpose(ps[:, 0, t * N_EXP:(t + 1) * N_EXP], st.logits[:, t * P:(t + 1) * P],
                                                  ident[0:N_EXP, 0:N_EXP])
                    ins.then_inc(stage_pe, 1)
                    pe.wait_ge(stage_dve, st.at["d"] + 2)
                    takes = [st.route[:, t, TAKES:TAKES + N_EXP] for t in range(TT)]
                    for t in range(TT):
                        for before in range(t):
                            mm(ps[:, 1, t * N_EXP:(t + 1) * N_EXP], ones[:, :], takes[before], start=before == 0, stop=False)
                        mm(ps[:, 1, t * N_EXP:(t + 1) * N_EXP], st.buf["upto"], takes[t], start=t == 0, stop=True)
                    for t in range(TT):
                        ins = mm(ps[:, 2, 0:N_EXP], ones[:, :], takes[t], start=t == 0, stop=t == TT - 1)
                    ins.then_inc(stage_pe, 1)
                elif st.kind == "mod_cols":
                    for c in range(MOD_W // P):
                        ins = nc.tensor.transpose(ps[:, 0, 4 * c:4 * c + 4], st.rows[2 * c // (MOD_W // P)][0:4, c % (MOD_W // P // 2) * P:][:, 0:P], ident[0:4, 0:4])
                    ins.then_inc(stage_pe, 1)
                elif st.kind == "post":
                    pe.wait_ge(stage_dve, st.at["d"] + 1)
                    for s in range(2):
                        for c in range(DC):
                            ins = mm(ps[:, 2 * s + c // 4, (c % 4) * P:(c % 4 + 1) * P], ones[:, :], st.diag[:, s, c, :],
                                     start=True, stop=True)
                    ins.then_inc(stage_pe, 1)


_WEIGHTS = ["w_in", "w_o_sb", "w_o_fox", "w_out", "w_gu_dense", "w_dn_dense", "w_router", "w_gu_exp", "w_dn_exp", "w_mod_2",
            "w_in_2", "w_branch_2", "w_out_2", "w_up_2", "w_down_2", "x", "ctx_2"]


def _constants():
    t, s = np.arange(T)[:, None], np.arange(T)[None, :]

    def tiles(m):
        return np.ascontiguousarray(m.astype(np.float32).reshape(TT, P, -1).transpose(1, 0, 2))

    c0 = np.clip(t % GRID_W - NA_C // 2, 0, GRID_W - NA_C)
    inside = (s % GRID_W >= c0) & (s % GRID_W < c0 + NA_C)
    half = HD // 2
    inv = np.float32(ROPE_THETA) ** (-np.arange(0, half, 2, dtype=np.float32) / np.float32(half))
    n = np.arange(T)
    ang_r, ang_c = ((n // GRID_W).astype(np.float32)[:, None] * inv, (n % GRID_W).astype(np.float32)[:, None] * inv)
    ang = np.concatenate([ang_r, ang_r, ang_c, ang_c], axis=-1)
    sign = np.repeat(np.array([-1, 1, -1, 1], np.float32), HD // 4)
    row_of = np.zeros((NH, NH, P), np.float32)
    row_of[np.arange(NH), np.arange(NH)] = 1
    return {
        "ident": np.eye(P, dtype=np.float32), "row_of": row_of,
        "causal": tiles(np.where(s <= t, 0, NEG)), "anti": tiles(np.where(s >= t, 0, NEG)),
        "strict": tiles(np.where(s < t, -NEG, -BOUND)), "window": tiles(np.where(inside, 0, NEG)),
        "rope_cos": tiles(np.cos(ang)), "rope_sin": tiles(np.sin(ang) * sign),
        "expert_no": np.arange(N_EXP, dtype=np.float32),
    }


def _laid_out(v):
    def columns(x):
        return np.asarray(x).reshape(-1, P).T

    parts = []
    for l in range(DEPTH):
        parts += [columns(v["g_mix"][l]), columns(v["g_ffn"][l])]
    for l in range(DEPTH):
        parts += [columns(v[n + "_2"][l]) for n in ("g_pre_mix", "g_pre_ffn", "g_post_mix", "g_post_ffn", "g_ml_out", "b_mod",
                                                    "conv_b", "conv_w")]
    parts.append(np.stack([columns(v["c_2"][0]), columns(v["c_ctx_2"])], axis=-1).reshape(P, -1))
    gate_bias = np.zeros((4 * ML_H, 2 * DEPTH), np.float32)
    gate_bias[0:NH, 0:DEPTH] = np.asarray(v["b_f"]).T
    gate_bias[:, DEPTH:] = np.asarray(v["b_ml_gates_2"]).T
    rpb = np.asarray(v["na_rpb_2"])
    padded = np.zeros(rpb.shape[:3] + (2 * GRID_W,), np.float32)
    padded[..., GRID_W - NA_C:GRID_W - NA_C + 2 * NA_C - 1] = rpb
    bias = np.zeros(rpb.shape[:2] + (ROWS, GRID_W, ROWS, GRID_W), np.float32)
    for r in range(ROWS):
        for c in range(GRID_W):
            bias[:, :, r, c] = padded[:, :, NA_R - 1 - r:NA_R - 1 - r + ROWS, GRID_W - 1 - c:2 * GRID_W - 1 - c]
    rows = [np.asarray(v[n])[l] for sfx in ("", "_2") for l in range(DEPTH) for n in ("g_q" + sfx, "g_k" + sfx)]
    return {"cols": np.ascontiguousarray(np.concatenate(parts, axis=1)), "gate_bias": gate_bias, "position_bias": bias.reshape(DEPTH, NH, T, T),
            "g_rows": np.stack(rows), "bias_rows": np.asarray(v["b_gate"]).reshape(4 * DEPTH, NT)}


def kernel(**inputs):
    import concourse.bacc as bacc
    from concourse.bass_utils import run_bass_kernel_spmd

    given = {n: np.ascontiguousarray(inputs[n]) for n in _WEIGHTS}
    given.update(_laid_out(inputs))
    given.update(_constants())
    nc = bacc.Bacc("TRN2", target_bir_lowering=False, num_devices=1)
    arrays = {f"in_{n}": x for n, x in given.items()}
    aps = {n: nc.dram_tensor(f"in_{n}", x.shape, F32, kind="ExternalInput").ap() for n, x in given.items()}
    out = nc.dram_tensor("out", (1, T, D), F32, kind="ExternalOutput").ap()
    build(nc, aps, out)
    r = run_bass_kernel_spmd(nc, [arrays], core_ids=[0])
    return r.results[0]["out"]
```
